# Optimizing a Trainium2 kernel written in Bass

```python
import jax, jax.numpy as jnp
from jax import lax
import numpy as np

D_MODEL = 1024
BATCH = 1
SEQ = 512
DEPTH = 2

EPS = 1e-6
GRID_W = 64

POOL_WINDOWS = (2, 4, 8, 16)
N_POOL_GROUPS = 4
POOL_GROUP_DIM = D_MODEL // 8
POOL_DIM = N_POOL_GROUPS * POOL_GROUP_DIM

ATT_HEADS = 8
ATT_KV_HEADS = 2
ATT_HEAD_DIM = D_MODEL // 16
ATT_Q_DIM = ATT_HEADS * ATT_HEAD_DIM
ATT_KV_DIM = ATT_KV_HEADS * ATT_HEAD_DIM
Q_BLOCK = 128
ROPE_THETA = 10000.0

EVEN_IN_DIM = POOL_DIM + ATT_Q_DIM + 2 * ATT_KV_DIM
EVEN_MIX_DIM = POOL_DIM + ATT_Q_DIM

MLSTM_HEADS = 8
MLSTM_QK_DIM = D_MODEL // 16
MLSTM_V_DIM = D_MODEL // 8
MLSTM_QK_WIDTH = MLSTM_HEADS * MLSTM_QK_DIM
MLSTM_V_WIDTH = MLSTM_HEADS * MLSTM_V_DIM
N_GATES = 4 * MLSTM_HEADS
ODD_IN_DIM = 2 * MLSTM_QK_WIDTH + 2 * MLSTM_V_WIDTH + N_GATES
CONV_K = 5
CHUNK = 128

FFN_HIDDEN = -(-8 * D_MODEL // (3 * 256)) * 256


def rms_norm(x):
    x32 = x.astype(jnp.float32)
    y = x32 * lax.rsqrt(jnp.mean(x32 * x32, axis=-1, keepdims=True) + EPS)
    return y.astype(x.dtype)

def modulate(h, shift, scale):
    return h * (1.0 + scale[:, None, :]) + shift[:, None, :]

def grid_rope(seq_len):
    rows = seq_len // GRID_W
    row = jnp.repeat(jnp.arange(rows), GRID_W).astype(jnp.float32)
    col = jnp.tile(jnp.arange(GRID_W), rows).astype(jnp.float32)
    n_freq = ATT_HEAD_DIM // 4
    inv_freq = ROPE_THETA ** (-jnp.arange(n_freq, dtype=jnp.float32) / n_freq)
    ang = jnp.concatenate([row[:, None] * inv_freq, col[:, None] * inv_freq], axis=-1)
    return jnp.cos(ang), jnp.sin(ang)

def apply_rope(x, cos, sin):
    x32 = x.astype(jnp.float32)
    x1, x2 = x32[..., 0::2], x32[..., 1::2]
    c, s = cos[None, :, None, :], sin[None, :, None, :]
    out = jnp.stack([x1 * c - x2 * s, x1 * s + x2 * c], axis=-1).reshape(x.shape)
    return out.astype(x.dtype)

def multiscale_pool(u):
    B, S, _ = u.shape
    u32 = u.astype(jnp.float32)
    csum = jnp.concatenate([jnp.zeros((B, 1, POOL_DIM), jnp.float32), jnp.cumsum(u32, axis=1)], axis=1)
    t = jnp.arange(S)
    means = []
    for g, w in enumerate(POOL_WINDOWS):
        lo = jnp.clip(t - w // 2, 0, S)
        hi = jnp.clip(t + w - w // 2, 0, S)
        cg = csum[..., g * POOL_GROUP_DIM:(g + 1) * POOL_GROUP_DIM]
        total = jnp.take(cg, hi, axis=1) - jnp.take(cg, lo, axis=1)
        count = (hi - lo).astype(jnp.float32)
        means.append(total / count[None, :, None])
    return (jnp.concatenate(means, axis=-1) - u32).astype(u.dtype)

def grid_attention(q, k, v, cos, sin, q_gain, k_gain):
    q = apply_rope(rms_norm(q) * q_gain, cos, sin)
    k = apply_rope(rms_norm(k) * k_gain, cos, sin)
    B, S, H, Dh = q.shape
    G = H // ATT_KV_HEADS
    nb = S // Q_BLOCK
    qb = q.reshape(B, nb, Q_BLOCK, ATT_KV_HEADS, G, Dh).transpose(1, 0, 3, 4, 2, 5)
    kt = k.transpose(0, 2, 1, 3)
    vt = v.transpose(0, 2, 1, 3)
    scale = Dh ** -0.5

    def block(q_blk):
        s = jnp.einsum('bkgqd,bksd->bkgqs', q_blk, kt).astype(jnp.float32) * scale
        p = jax.nn.softmax(s, axis=-1).astype(vt.dtype)
        return jnp.einsum('bkgqs,bksd->bkgqd', p, vt)

    o = lax.map(block, qb)
    return o.transpose(1, 0, 4, 2, 3, 5).reshape(B, S, H * Dh)

def pool_attention_mixer(h, w_in, w_pool, b_pool, pool_scale, q_gain, k_gain, w_out, cos, sin):
    B, S, _ = h.shape
    z = h @ w_in
    u = z[..., :POOL_DIM]
    q = z[..., POOL_DIM:POOL_DIM + ATT_Q_DIM]
    k = z[..., POOL_DIM + ATT_Q_DIM:POOL_DIM + ATT_Q_DIM + ATT_KV_DIM]
    v = z[..., POOL_DIM + ATT_Q_DIM + ATT_KV_DIM:]
    pooled = multiscale_pool(u).reshape(B, S, N_POOL_GROUPS, POOL_GROUP_DIM)
    a = (jnp.einsum('bsgc,gcd->bsgd', pooled, w_pool) + b_pool).reshape(B, S, POOL_DIM) * pool_scale
    att = grid_attention(q.reshape(B, S, ATT_HEADS, ATT_HEAD_DIM),
                         k.reshape(B, S, ATT_KV_HEADS, ATT_HEAD_DIM),
                         v.reshape(B, S, ATT_KV_HEADS, ATT_HEAD_DIM),
                         cos, sin, q_gain, k_gain)
    return jnp.concatenate([a, att], axis=-1) @ w_out

def centred_depthwise_conv(u, w, b):
    y = lax.conv_general_dilated(u, w[:, None, :].astype(u.dtype), window_strides=(1,),
                                 padding=[(CONV_K // 2, CONV_K // 2)],
                                 dimension_numbers=('NWC', 'WIO', 'NWC'),
                                 feature_group_count=u.shape[-1])
    return y + b

def mlstm_chunkwise(q, k, v, log_i, log_f):
    q, k, v = (a.astype(jnp.float32) for a in (q, k, v))
    B, H, S, Dk = q.shape
    Dv = v.shape[-1]
    nc = S // CHUNK

    def to_chunks(a):
        return jnp.moveaxis(a.reshape(B, H, nc, CHUNK, *a.shape[3:]), 2, 0)

    qc, kc, vc, ic, fc = (to_chunks(a) for a in (q, k, v, log_i, log_f))
    lower = jnp.tril(jnp.ones((CHUNK, CHUNK), bool))

    def step(carry, inp):
        C, n, m = carry
        qj, kj, vj, ij, fj = inp
        b = jnp.cumsum(fj, axis=-1)
        a = b + m[..., None]
        D = jnp.where(lower, b[..., :, None] - b[..., None, :] + ij[..., None, :], -jnp.inf)
        m_t = jnp.maximum(a, jnp.max(D, axis=-1))
        w_inter = jnp.exp(a - m_t)
        s = jnp.einsum('bhtd,bhsd->bhts', qj, kj) * jnp.exp(D - m_t[..., None])
        num = jnp.einsum('bhts,bhsv->bhtv', s, vj) + w_inter[..., None] * jnp.einsum('bhvd,bhtd->bhtv', C, qj)
        den = jnp.sum(s, axis=-1) + w_inter * jnp.einsum('bhd,bhtd->bht', n, qj)
        h = num / jnp.maximum(jnp.abs(den), jnp.exp(-m_t))[..., None]
        bL = b[..., -1]
        g = bL[..., None] - b + ij
        m_new = jnp.maximum(bL + m, jnp.max(g, axis=-1))
        decay = jnp.exp(bL + m - m_new)
        wk = jnp.exp(g - m_new[..., None])
        C = decay[..., None, None] * C + jnp.einsum('bhsv,bhsd->bhvd', vj * wk[..., None], kj)
        n = decay[..., None] * n + jnp.einsum('bhs,bhsd->bhd', wk, kj)
        return (C, n, m_new), h

    init = (jnp.zeros((B, H, Dv, Dk), jnp.float32), jnp.zeros((B, H, Dk), jnp.float32),
            jnp.zeros((B, H), jnp.float32))
    _, hc = lax.scan(step, init, (qc, kc, vc, ic, fc))
    return jnp.moveaxis(hc, 0, 2).reshape(B, H, S, Dv)

def mlstm_mixer(h, w_in, conv_w, conv_b, gate_b, head_gain, w_out):
    B, S, _ = h.shape
    z = h @ w_in
    qk_raw = z[..., :2 * MLSTM_QK_WIDTH]
    v = z[..., 2 * MLSTM_QK_WIDTH:2 * MLSTM_QK_WIDTH + MLSTM_V_WIDTH]
    o = z[..., 2 * MLSTM_QK_WIDTH + MLSTM_V_WIDTH:2 * MLSTM_QK_WIDTH + 2 * MLSTM_V_WIDTH]
    gates = z[..., 2 * MLSTM_QK_WIDTH + 2 * MLSTM_V_WIDTH:]
    qk = jax.nn.silu(centred_depthwise_conv(qk_raw, conv_w, conv_b))
    q = qk[..., :MLSTM_QK_WIDTH].reshape(B, S, MLSTM_HEADS, MLSTM_QK_DIM).transpose(0, 2, 1, 3)
    k = (qk[..., MLSTM_QK_WIDTH:] * MLSTM_QK_DIM ** -0.5).reshape(B, S, MLSTM_HEADS, MLSTM_QK_DIM).transpose(0, 2, 1, 3)
    v = v.reshape(B, S, MLSTM_HEADS, MLSTM_V_DIM).transpose(0, 2, 1, 3)
    g = (gates.astype(jnp.float32) + gate_b.astype(jnp.float32)).reshape(B, S, 2, 2, MLSTM_HEADS)
    g = jnp.transpose(g, (2, 3, 0, 4, 1))
    h_fwd = mlstm_chunkwise(q, k, v, g[0, 0], jax.nn.log_sigmoid(g[0, 1]))
    flip = lambda a: jnp.flip(a, axis=2)
    h_bwd = flip(mlstm_chunkwise(flip(q), flip(k), flip(v), flip(g[1, 0]), flip(jax.nn.log_sigmoid(g[1, 1]))))
    hs = (h_fwd + h_bwd).transpose(0, 2, 1, 3).astype(h.dtype)
    hs = rms_norm(hs) * head_gain
    out = jax.nn.sigmoid(o).reshape(B, S, MLSTM_HEADS, MLSTM_V_DIM) * hs
    return out.reshape(B, S, MLSTM_V_WIDTH) @ w_out

def swiglu(h, w1, w3, w2):
    return (jax.nn.silu(h @ w1) * (h @ w3)) @ w2

def first_inputs(seed: int = 0) -> dict:
    key = jax.random.key(seed)
    ks = jax.random.split(key, 24)
    n_ev = (DEPTH + 1) // 2
    n_od = DEPTH // 2
    f32 = jnp.float32

    def nrm(k, shape, scale):
        return jax.random.normal(k, shape, f32) * scale

    i_bias = nrm(ks[14], (n_od, 2, MLSTM_HEADS), 0.1)
    f_bias = jnp.linspace(3.0, 6.0, MLSTM_HEADS, dtype=f32)[None, None, :] + nrm(ks[15], (n_od, 2, MLSTM_HEADS), 0.1)
    return {
        'x': nrm(ks[0], (BATCH, SEQ, D_MODEL), 1.0),
        'c': nrm(ks[1], (BATCH, D_MODEL), 1.0),
        'ada_w': nrm(ks[2], (DEPTH, D_MODEL, 6 * D_MODEL), D_MODEL ** -0.5),
        'ada_b': nrm(ks[3], (DEPTH, 6 * D_MODEL), 0.02),
        'ev_w_in': nrm(ks[4], (n_ev, D_MODEL, EVEN_IN_DIM), D_MODEL ** -0.5),
        'ev_w_pool': nrm(ks[5], (n_ev, N_POOL_GROUPS, POOL_GROUP_DIM, POOL_GROUP_DIM), POOL_GROUP_DIM ** -0.5),
        'ev_b_pool': nrm(ks[6], (n_ev, N_POOL_GROUPS, POOL_GROUP_DIM), 0.02),
        'ev_pool_scale': 1.0 + nrm(ks[7], (n_ev, POOL_DIM), 0.1),
        'ev_q_gain': 1.0 + nrm(ks[8], (n_ev, ATT_HEAD_DIM), 0.1),
        'ev_k_gain': 1.0 + nrm(ks[9], (n_ev, ATT_HEAD_DIM), 0.1),
        'ev_w_out': nrm(ks[10], (n_ev, EVEN_MIX_DIM, D_MODEL), EVEN_MIX_DIM ** -0.5),
        'od_w_in': nrm(ks[11], (n_od, D_MODEL, ODD_IN_DIM), D_MODEL ** -0.5),
        'od_conv_w': nrm(ks[12], (n_od, CONV_K, 2 * MLSTM_QK_WIDTH), CONV_K ** -0.5),
        'od_conv_b': nrm(ks[13], (n_od, 2 * MLSTM_QK_WIDTH), 0.02),
        'od_gate_b': jnp.stack([i_bias, f_bias], axis=2).reshape(n_od, N_GATES),
        'od_head_gain': 1.0 + nrm(ks[16], (n_od, MLSTM_HEADS, MLSTM_V_DIM), 0.1),
        'od_w_out': nrm(ks[17], (n_od, MLSTM_V_WIDTH, D_MODEL), MLSTM_V_WIDTH ** -0.5),
        'ffn_w1': nrm(ks[18], (DEPTH, D_MODEL, FFN_HIDDEN), D_MODEL ** -0.5),
        'ffn_w3': nrm(ks[19], (DEPTH, D_MODEL, FFN_HIDDEN), D_MODEL ** -0.5),
        'ffn_w2': nrm(ks[20], (DEPTH, FFN_HIDDEN, D_MODEL), FFN_HIDDEN ** -0.5),
    }

def first_block(x, c, ada_w, ada_b, ev_w_in, ev_w_pool, ev_b_pool, ev_pool_scale, ev_q_gain, ev_k_gain,
              ev_w_out, od_w_in, od_conv_w, od_conv_b, od_gate_b, od_head_gain, od_w_out,
              ffn_w1, ffn_w3, ffn_w2):
    cos, sin = grid_rope(x.shape[1])
    cond = jax.nn.silu(c)
    for layer in range(DEPTH):
        mod = cond @ ada_w[layer] + ada_b[layer]
        sh1, sc1, g1, sh2, sc2, g2 = jnp.split(mod, 6, axis=-1)
        h = modulate(rms_norm(x), sh1, sc1)
        j = layer // 2
        if layer % 2 == 0:
            y = pool_attention_mixer(h, ev_w_in[j], ev_w_pool[j], ev_b_pool[j], ev_pool_scale[j],
                                     ev_q_gain[j], ev_k_gain[j], ev_w_out[j], cos, sin)
        else:
            y = mlstm_mixer(h, od_w_in[j], od_conv_w[j], od_conv_b[j], od_gate_b[j],
                            od_head_gain[j], od_w_out[j])
        x = x + g1[:, None, :] * y
        h = modulate(rms_norm(x), sh2, sc2)
        x = x + g2[:, None, :] * swiglu(h, ffn_w1[layer], ffn_w3[layer], ffn_w2[layer])
    return x


DEPTH_2 = 1

CHUNK_2 = 64
N_MEM = 256
MEM_HEADS = 4
MEM_HEAD_DIM = D_MODEL // MEM_HEADS
MIX_WIDTH = D_MODEL
HG_WIDTH = MIX_WIDTH // 2
HG_HEADS = 4
HG_HEAD_DIM = HG_WIDTH // HG_HEADS
SB_WIDTH = MIX_WIDTH - HG_WIDTH
SB_HEADS = 8
SB_HEAD_DIM = SB_WIDTH // SB_HEADS
SB_BLOCK = 128
D_FF = 2816
IN_COLS = 4 * HG_WIDTH + 3 * SB_WIDTH


def rmsnorm(x, g):
    xf = x.astype(jnp.float32)
    y = xf * lax.rsqrt(jnp.mean(xf * xf, axis=-1, keepdims=True) + EPS)
    return (y * g.astype(jnp.float32)).astype(x.dtype)

def head_rmsnorm(o, g):
    B, S, H, d = o.shape
    of = o.astype(jnp.float32)
    y = of * lax.rsqrt(jnp.mean(of * of, axis=-1, keepdims=True) + EPS)
    return y * g.astype(jnp.float32).reshape(H, d)

def swiglu_2(h, w_gu, w_down):
    gu = h @ w_gu
    gate, up = jnp.split(gu, 2, axis=-1)
    return (jax.nn.silu(gate) * up) @ w_down

def hgrn2_mixer(q, f_logit, i, g, lb, gnorm):
    B, S, _ = q.shape
    n_chunks = S // CHUNK_2
    lbf = lb.astype(jnp.float32)
    f = lbf + (1.0 - lbf) * jax.nn.sigmoid(f_logit.astype(jnp.float32))
    k = 1.0 - f
    logf = jnp.log(f)

    def to_chunks(t):
        return t.astype(jnp.float32).reshape(B, n_chunks, CHUNK_2, HG_HEADS, HG_HEAD_DIM).transpose(1, 0, 3, 2, 4)

    qc, kc, vc = to_chunks(q), to_chunks(k), to_chunks(i)
    bc = jnp.cumsum(to_chunks(logf), axis=3)
    causal = jnp.tril(jnp.ones((CHUNK_2, CHUNK_2), dtype=bool))[None, None, :, :, None]

    def step(state, inp):
        qt, kt, vt, bt = inp
        diff = bt[:, :, :, None, :] - bt[:, :, None, :, :]
        decay = jnp.exp(jnp.where(causal, diff, -jnp.inf))
        a = jnp.einsum('bhtd,bhsd,bhtsd->bhts', qt, kt, decay)
        o_intra = jnp.einsum('bhts,bhsv->bhtv', a, vt)
        o_inter = jnp.einsum('bhtd,bhdv->bhtv', qt * jnp.exp(bt), state)
        b_last = bt[:, :, -1:, :]
        k_dec = kt * jnp.exp(b_last - bt)
        new_state = jnp.exp(b_last[:, :, 0, :])[..., None] * state + jnp.einsum('bhsd,bhsv->bhdv', k_dec, vt)
        return new_state, o_intra + o_inter

    s0 = jnp.zeros((B, HG_HEADS, HG_HEAD_DIM, HG_HEAD_DIM), jnp.float32)
    _, o = lax.scan(step, s0, (qc, kc, vc, bc))
    o = o.transpose(1, 0, 3, 2, 4).reshape(B, S, HG_HEADS, HG_HEAD_DIM)
    o = head_rmsnorm(o, gnorm).reshape(B, S, HG_WIDTH)
    return o * jax.nn.silu(g.astype(jnp.float32))

def stick_breaking_mixer(q, k, v, gnorm):
    B, S, _ = q.shape
    n_blk = S // SB_BLOCK
    scale = SB_HEAD_DIM ** -0.5

    def heads(t):
        return t.astype(jnp.float32).reshape(B, S, SB_HEADS, SB_HEAD_DIM).transpose(0, 2, 1, 3)

    qh, kh, vh = heads(q), heads(k), heads(v)
    qb = qh.reshape(B, SB_HEADS, n_blk, SB_BLOCK, SB_HEAD_DIM).transpose(2, 0, 1, 3, 4)
    key_pos = jnp.arange(S)

    def block(args):
        q_blk, blk = args
        z = jnp.einsum('bhtd,bhsd->bhts', q_blk, kh) * scale
        q_pos = blk * SB_BLOCK + jnp.arange(SB_BLOCK)
        before = (key_pos[None, :] < q_pos[:, None])[None, None]
        log_beta = jax.nn.log_sigmoid(z)
        log_one_minus = jnp.where(before, jax.nn.log_sigmoid(-z), 0.0)
        between = lax.cumsum(log_one_minus, axis=3, reverse=True) - log_one_minus
        weights = jnp.exp(jnp.where(before, log_beta + between, -jnp.inf))
        return jnp.einsum('bhts,bhsd->bhtd', weights, vh)

    o = lax.map(block, (qb, jnp.arange(n_blk)))
    o = o.transpose(1, 0, 3, 2, 4).reshape(B, S, SB_HEADS, SB_HEAD_DIM)
    return head_rmsnorm(o, gnorm).reshape(B, S, SB_WIDTH)

def memory_cross_attention(h, m, w_q, w_kv, w_o):
    B, S, _ = h.shape
    q = (h @ w_q).reshape(B, S, MEM_HEADS, MEM_HEAD_DIM)
    k, v = jnp.split(m @ w_kv, 2, axis=-1)
    k = k.reshape(B, N_MEM, MEM_HEADS, MEM_HEAD_DIM)
    v = v.reshape(B, N_MEM, MEM_HEADS, MEM_HEAD_DIM)
    s = jnp.einsum('bthd,bnhd->bhtn', q, k).astype(jnp.float32) * (MEM_HEAD_DIM ** -0.5)
    p = jax.nn.softmax(s, axis=-1).astype(h.dtype)
    o = jnp.einsum('bhtn,bnhd->bthd', p, v).reshape(B, S, D_MODEL)
    return o @ w_o

def second_inputs(seed: int = 0) -> dict:
    key = jax.random.key(seed)
    ks = jax.random.split(key, 24)
    f32 = jnp.float32

    def w(k, shape, fan_in, gain=1.0):
        return (jax.random.normal(k, shape, f32) * (gain * fan_in ** -0.5)).astype(f32)

    def norm_gain(k, shape):
        return (1.0 + 0.02 * jax.random.normal(k, shape, f32)).astype(f32)

    return {
        "x": jax.random.normal(ks[0], (BATCH, SEQ, D_MODEL), f32),
        "mem": jax.random.normal(ks[1], (BATCH, N_MEM, D_MODEL), f32),
        "ffn1_norm": norm_gain(ks[2], (DEPTH_2, D_MODEL)),
        "ffn1_w_gu": w(ks[3], (DEPTH_2, D_MODEL, 2 * D_FF), D_MODEL),
        "ffn1_w_down": w(ks[4], (DEPTH_2, D_FF, D_MODEL), D_FF),
        "mix_norm": norm_gain(ks[5], (DEPTH_2, D_MODEL)),
        "w_in": w(ks[6], (DEPTH_2, D_MODEL, IN_COLS), D_MODEL),
        "hg_lb_raw": (0.5 * jax.random.normal(ks[7], (DEPTH_2 + 1, HG_WIDTH), f32)).astype(f32),
        "hg_gnorm": norm_gain(ks[8], (DEPTH_2, HG_WIDTH)),
        "sb_gnorm": norm_gain(ks[9], (DEPTH_2, SB_WIDTH)),
        "w_out": w(ks[10], (DEPTH_2, MIX_WIDTH, D_MODEL), MIX_WIDTH),
        "mem_q_norm": norm_gain(ks[11], (DEPTH_2, D_MODEL)),
        "mem_kv_norm": norm_gain(ks[12], (DEPTH_2, D_MODEL)),
        "mem_w_q": w(ks[13], (DEPTH_2, D_MODEL, D_MODEL), D_MODEL),
        "mem_w_kv": w(ks[14], (DEPTH_2, D_MODEL, 2 * D_MODEL), D_MODEL),
        "mem_w_o": w(ks[15], (DEPTH_2, D_MODEL, D_MODEL), D_MODEL),
        "ffn2_norm": norm_gain(ks[16], (DEPTH_2, D_MODEL)),
        "ffn2_w_gu": w(ks[17], (DEPTH_2, D_MODEL, 2 * D_FF), D_MODEL),
        "ffn2_w_down": w(ks[18], (DEPTH_2, D_FF, D_MODEL), D_FF),
        "final_norm": norm_gain(ks[19], (D_MODEL,)),
    }

def second_block(x, mem, ffn1_norm, ffn1_w_gu, ffn1_w_down, mix_norm, w_in, hg_lb_raw,
              hg_gnorm, sb_gnorm, w_out, mem_q_norm, mem_kv_norm, mem_w_q, mem_w_kv,
              mem_w_o, ffn2_norm, ffn2_w_gu, ffn2_w_down, final_norm):
    lb_all = jnp.cumsum(jax.nn.softmax(hg_lb_raw.astype(jnp.float32), axis=0), axis=0)
    for l in range(DEPTH_2):
        x = x + 0.5 * swiglu_2(rmsnorm(x, ffn1_norm[l]), ffn1_w_gu[l], ffn1_w_down[l])

        h = rmsnorm(x, mix_norm[l])
        proj = h @ w_in[l]
        hg_q, hg_f, hg_i, hg_g, sb_q, sb_k, sb_v = jnp.split(
            proj, np.cumsum([HG_WIDTH] * 4 + [SB_WIDTH] * 2).tolist(), axis=-1)
        o_hg = hgrn2_mixer(hg_q, hg_f, hg_i, hg_g, lb_all[l], hg_gnorm[l])
        o_sb = stick_breaking_mixer(sb_q, sb_k, sb_v, sb_gnorm[l])
        mixed = jnp.concatenate([o_hg, o_sb], axis=-1).astype(x.dtype)
        x = x + mixed @ w_out[l]

        x = x + memory_cross_attention(rmsnorm(x, mem_q_norm[l]), rmsnorm(mem, mem_kv_norm[l]),
                                       mem_w_q[l], mem_w_kv[l], mem_w_o[l])

        x = x + 0.5 * swiglu_2(rmsnorm(x, ffn2_norm[l]), ffn2_w_gu[l], ffn2_w_down[l])
    return rmsnorm(x, final_norm)


def setup_inputs(seed=0):
    out = dict(first_inputs(seed))
    for name, value in second_inputs(seed + 1).items():
        if name != "x":
            out[name + "_2"] = value
    return out


def reference(
    x, c, ada_w, ada_b, ev_w_in, ev_w_pool, ev_b_pool, ev_pool_scale, ev_q_gain, ev_k_gain,
    ev_w_out, od_w_in, od_conv_w, od_conv_b, od_gate_b, od_head_gain, od_w_out, ffn_w1, ffn_w3,
    ffn_w2, mem_2, ffn1_norm_2, ffn1_w_gu_2, ffn1_w_down_2, mix_norm_2, w_in_2, hg_lb_raw_2,
    hg_gnorm_2, sb_gnorm_2, w_out_2, mem_q_norm_2, mem_kv_norm_2, mem_w_q_2, mem_w_kv_2,
    mem_w_o_2, ffn2_norm_2, ffn2_w_gu_2, ffn2_w_down_2, final_norm_2,
):
    x = first_block(
        x, c, ada_w, ada_b, ev_w_in, ev_w_pool, ev_b_pool, ev_pool_scale, ev_q_gain, ev_k_gain,
        ev_w_out, od_w_in, od_conv_w, od_conv_b, od_gate_b, od_head_gain, od_w_out, ffn_w1,
        ffn_w3, ffn_w2,
    )
    return second_block(
        x, mem_2, ffn1_norm_2, ffn1_w_gu_2, ffn1_w_down_2, mix_norm_2, w_in_2, hg_lb_raw_2,
        hg_gnorm_2, sb_gnorm_2, w_out_2, mem_q_norm_2, mem_kv_norm_2, mem_w_q_2, mem_w_kv_2,
        mem_w_o_2, ffn2_norm_2, ffn2_w_gu_2, ffn2_w_down_2, final_norm_2,
    )


_drawn_inputs = setup_inputs


def setup_inputs(seed=0):
    import zlib

    import numpy as np

    out = dict(_drawn_inputs(seed))
    spreads = {}
    factors = {'ev_b_pool': 4.911,
     'ev_q_gain': 8.0,
     'ev_k_gain': 8.0,
     'od_conv_b': 8.0,
     'ffn1_norm_2': 8.0,
     'mix_norm_2': 4.08,
     'hg_gnorm_2': 8.0,
     'sb_gnorm_2': 45.242,
     'mem_q_norm_2': 8.0,
     'mem_kv_norm_2': 8.0,
     'ffn2_norm_2': 25.141}
    for name, (base, spread) in spreads.items():
        noise = np.random.default_rng([zlib.crc32(name.encode()), seed]).standard_normal(out[name].shape)
        drawn = base * np.exp(spread * noise) if base else spread * noise
        out[name] = __import__('jax').numpy.asarray(drawn.astype(out[name].dtype))
    for name, factor in factors.items():
        out[name] = (out[name] * factor).astype(out[name].dtype)
    return out
```

```python
from contextlib import ExitStack, contextmanager

import numpy as np

import concourse.bass as bass
from concourse import mybir

ALU = mybir.AluOpType
ACT = mybir.ActivationFunctionType
AX = mybir.AxisListType
F32 = mybir.dt.float32
F32R = mybir.dt.float32r
I32 = mybir.dt.int32

P = 128
D = 1024
S = 512
KC = D // P
TB = S // P
FF = 2816
FB = FF // P
N_MEM = 256
MB = N_MEM // P
UNIT = 2048
EPS = 1e-6
BIG = 1.0e30

ADA_UNITS = 2 * 3 * KC
FFN_UNITS = FB + FB // 2

PLAN = [("even_in", 5), ("even_out", 4), ("ffn0", FFN_UNITS), ("odd_in", 13), ("odd_out", 4),
        ("ffn1", FFN_UNITS), ("ffn2", FFN_UNITS), ("mix_in", 14), ("mix_out", 4), ("mem_kv", 8), ("mem_q", 4),
        ("mem_out", 4), ("ffn3", FFN_UNITS)]
FIRST_UNIT = {}
_m = 0
for _name, _n in PLAN:
    FIRST_UNIT[_name] = _m
    _m += _n
N_UNITS = _m

PARAMS = [("c", 8), ("ada_b", 96), ("b_pool", 4), ("pool_scale", 4), ("q_gain", 1), ("k_gain", 1), ("conv_w", 40),
          ("conv_b", 8), ("head_gain", 8), ("ffn1_norm", 8), ("mix_norm", 8), ("mem_q_norm", 8),
          ("mem_kv_norm", 8), ("ffn2_norm", 8), ("final_norm", 8), ("lb_raw0", 4), ("lb_raw1", 4),
          ("hg_gnorm", 4), ("sb_gnorm", 4), ("gate_b_i", 1), ("gate_b_f", 1), ("eps", 1), ("zero", 1),
          ("one", 1), ("half", 1)]
PCOL = {}
_m = 0
for _name, _n in PARAMS:
    PCOL[_name] = _m
    _m += _n
N_PARAMS = _m

TABLES = [("ident", 128), ("swap", 128), ("tri", 128), ("strict", 128), ("neg_strict", 128), ("hide_fwd", 128),
          ("hide_bwd", 128), ("ones", 128), ("pair_rows", 32), ("gate_i", 40), ("gate_f", 40),
          ("pair_spread", 5 * 128)]
TCOL = {}
_m = 0
for _name, _n in TABLES:
    TCOL[_name] = _m
    _m += _n
N_TABLES = _m
EVEN_TABLES = 4 * S + 2 * S
LEVELS = 7
MIX_TABLES = (LEVELS + 1) * P + S


class Steps:

    def __init__(self, eng, sem):
        self.eng, self.sem, self.n, self.loop = eng, sem, 0, 0

    def add(self, ins):
        ins.then_inc(self.sem, 1)
        self.n += 1

    def settle(self):
        self.eng.wait_ge(self.sem, self.loop + self.n)

    def link(self, ins):
        self.add(ins)
        self.settle()


def program(nc, xT, memT, stream, params, tables, even_tables, mix_tables, w_pool, outT):
    ctx = ExitStack()
    with ctx:
        at = [16512]

        def place(name, shape, dt=F32, offset=None):
            if offset is None:
                offset = at[0]
                at[0] += -(-int(np.prod(shape[1:])) * 4 // 32) * 32
            return nc.alloc_sbuf_tensor_at(name, shape, dt, offset=offset)

        x = place("x", [P, KC, S])
        h_hi = place("h_hi", [P, KC, S], F32R)
        h_lo = place("h_lo", [P, KC, S], F32R)
        raw = place("raw", [P, 2, UNIT])
        w_hi = place("w_hi", [P, 2, UNIT], F32R)
        w_lo = place("w_lo", [P, 2, UNIT], F32R)
        par = place("par", [P, N_PARAMS])
        tab = place("tab", [P, N_TABLES])
        mod = place("mod", [P, 96])
        mod1 = place("mod1", [P, 96])
        cond = place("cond", [P, KC])
        small = place("small", [P, 512])
        WORK = 25600
        work_at = at[0]
        work = place("work", [P, WORK])
        assert at[0] <= nc.sbuf_usable_end, at[0]

        def area(start, *shape):
            n = int(np.prod(shape))
            assert start + n <= WORK, (start, shape)
            v = work[:, start:start + n]
            if len(shape) == 2:
                v = v.rearrange("p (a b) -> p a b", a=shape[0])
            if len(shape) == 3:
                v = v.rearrange("p (a b c) -> p a b c", a=shape[0], b=shape[1])
            return v

        g_hi = place("g_hi", [P, FB, S], F32R, offset=work_at)
        g_lo = place("g_lo", [P, FB, S], F32R, offset=work_at + FB * S * 4)
        mem_hi = place("mem_hi", [P, KC, N_MEM], F32R, offset=work_at + 19456 * 4)
        mem_lo = place("mem_lo", [P, KC, N_MEM], F32R, offset=work_at + 21504 * 4)
        bank = ctx.enter_context(nc.psum_tensor("bank", [P, 8, 512], F32))

        def col(name, i=0):
            return par[:, PCOL[name] + i:PCOL[name] + i + 1]

        def table(name):
            n = dict(TABLES)[name]
            return tab[:, TCOL[name]:TCOL[name] + n]

        ident, ones = table("ident"), table("ones")
        eps = col("eps")

        sems = {}

        def sem(name):
            assert name not in sems, name
            sems[name] = ctx.enter_context(nc.semaphore(name))
            return sems[name]

        setup_loaded = sem("setup_loaded")
        even_loaded = sem("even_loaded")
        mix_loaded = sem("mix_loaded")
        mem_loaded = sem("mem_loaded")
        landed = [sem("landed0"), sem("landed1")]
        ada_used = sem("ada_used")
        hi_split = sem("hi_split")
        lo_split = sem("lo_split")
        unit_used = sem("unit_used")
        x_ready = sem("x_ready")
        stored = sem("stored")

        def slot(m):
            return m % 2

        def split_hi(act, m, i=0):
            act.wait_ge(landed[slot(m)], 16 * ((ADA_UNITS + m) // 2 + 1) + 16 * i)
            if m >= 2:
                act.wait_ge(unit_used, m - 1 + 2 * i)
            nc.scalar.activation(w_hi[:, slot(m), :], raw[:, slot(m), :], ACT.Copy).then_inc(hi_split, 1)

        def split_lo(dve, m, i=0):
            dve.wait_ge(hi_split, m + 1 + 2 * i)
            nc.vector.tensor_tensor(w_lo[:, slot(m), :], raw[:, slot(m), :], w_hi[:, slot(m), :],
                                    ALU.subtract).then_inc(lo_split, 1)

        def split_next_hi(act, m, i=0):
            if m + 2 < n_units:
                split_hi(act, m + 2, i)

        def split_next_lo(dve, m, i=0):
            if m + 2 < n_units:
                split_lo(dve, m + 2, i)

        def three_passes(out, stationary, moving, first, last):
            nc.tensor.matmul(out, stationary[0], moving[0], start=first, stop=False)
            nc.tensor.matmul(out, stationary[0], moving[1], start=False, stop=False)
            return nc.tensor.matmul(out, stationary[1], moving[0], start=False, stop=last)

        def unit_cols(m):
            return [w[:, slot(m), :].rearrange("p (k n) -> p k n", k=KC) for w in (w_hi, w_lo)]

        def features(pe, m, block, out, wait_chunk=None, src=None, i=0):
            hh, hl = src or (h_hi, h_lo)
            wh, wl = unit_cols(m)
            c0 = block * P
            for k in range(KC):
                if wait_chunk:
                    wait_chunk(pe, k)
                last = three_passes(out, (wh[:, k, c0:c0 + P], wl[:, k, c0:c0 + P]), (hh[:, k, :], hl[:, k, :]),
                                    k == 0, k == KC - 1)
            return last

        def tokens(pe, m, out, blocks=TB, c0=0, n=256, src=None):
            hh, hl = src or (h_hi, h_lo)
            wh, wl = unit_cols(m)
            for t in range(blocks):
                r = slice(t * P, t * P + P)
                for k in range(KC):
                    last = three_passes(out[:, t, :], (hh[:, k, r], hl[:, k, r]),
                                        (wh[:, k, c0:c0 + n], wl[:, k, c0:c0 + n]), k == 0, k == KC - 1)
            return last

        def two_banks(m, blocks=TB, n=256):
            b = 2 * slot(m)
            return bank[:, b:b + 2, :].rearrange("p a n -> p (a n)")[:, 0:blocks * n].rearrange(
                "p (t n) -> p t n", t=blocks)

        class Conditioning:
            acc = area(8192, 2, UNIT)
            silu_done = sem("cond_silu")
            summed = sem("ada_summed")
            mod_done = sem("mod_done")

            def scalar(self, act, st):
                act.wait_ge(setup_loaded, 48)
                nc.scalar.activation(cond[:, :], par[:, PCOL["c"]:PCOL["c"] + KC], ACT.Silu).then_inc(self.silu_done, 1)
                split_hi(act, 0)
                split_hi(act, 1)

            def vector(self, dve, st):
                dve.wait_ge(setup_loaded, 48)
                dve.wait_ge(self.silu_done, 1)

                def pair_of_thirds(i, first):
                    for r in range(2):
                        for k in range(KC):
                            n = KC * r + k
                            dve.wait_ge(landed[n % 2], 16 * (n // 2 + 1) + 16 * KC * i)
                            if k == 0:
                                if not first:
                                    dve.wait_ge(self.summed, 2 * i + r - 1)
                                ins = nc.vector.tensor_scalar(self.acc[:, r, :], raw[:, n % 2, :], cond[:, k:k + 1],
                                                              None, ALU.mult)
                            else:
                                dve.wait_ge(ada_used, n + 2 * KC * i)
                                ins = nc.vector.scalar_tensor_tensor(self.acc[:, r, :], raw[:, n % 2, :],
                                                                     cond[:, k:k + 1], self.acc[:, r, :],
                                                                     ALU.mult, ALU.add)
                            ins.then_inc(ada_used, 1)

                pair_of_thirds(0, True)
                with dve.Fori(1, 3) as i:
                    pair_of_thirds(i, False)
                split_lo(dve, 0)
                split_lo(dve, 1)
                dve.wait_ge(self.summed, 6)
                st.link(nc.vector.tensor_tensor(mod[:, :], bank[:, 0, 0:96], par[:, PCOL["ada_b"]:PCOL["ada_b"] + 96],
                                                ALU.add))
                nc.vector.tensor_scalar(mod1[:, :], mod[:, :], 1.0, None, ALU.add).then_inc(self.mod_done, 1)
                dve.wait_ge(self.mod_done, 1)

            def tensor(self, pe):
                pe.wait_ge(setup_loaded, 48)
                for q in range(6):
                    pe.wait_ge(ada_used, KC * (q + 1))
                    for b in range(16):
                        last = nc.tensor.matmul(bank[:, 0, 16 * q + b:16 * q + b + 1],
                                                self.acc[:, q % 2, b * P:b * P + P], ones[:, 0:1],
                                                start=True, stop=True)
                    last.then_inc(self.summed, 1)

        norms = [0]
        updates = [0]
        sq_done = sem("sq_done")
        ms_done = sem("ms_done")
        root_done = sem("root_done")
        scaled = sem("scaled")
        h_hi_done = sem("h_hi_done")
        h_ready = sem("h_ready")

        class Norm:

            def __init__(self, scale, shift, free_bank, final=False, root_at=24576):
                self.n, self.scale, self.shift, self.bank, self.final = norms[0], scale, shift, free_bank, final
                self.version = updates[0]
                norms[0] += 1
                self.sq, self.t = area(0, KC, S), area(4096, KC, S)
                self.root, self.rstd = area(root_at, S), area(root_at + S, S)

            def wait_x(self, eng, k):
                if self.version:
                    eng.wait_ge(x_ready, KC * (self.version - 1) + k + 1)

            def wait_chunk(self, eng, k):
                eng.wait_ge(h_ready, KC * self.n + k + 1)

            def scalar(self, act, st):
                for k in range(KC):
                    self.wait_x(act, k)
                    nc.scalar.activation(self.sq[:, k, :], x[:, k, :], ACT.Square).then_inc(sq_done, 1)
                act.wait_ge(ms_done, self.n + 1)
                nc.scalar.activation(self.root[:, :], bank[:, self.bank, :], ACT.Sqrt, bias=eps,
                                     scale=1.0 / D).then_inc(root_done, 1)
                if self.final:
                    return
                for k in range(KC):
                    act.wait_ge(scaled, KC * self.n + k + 1)
                    nc.scalar.activation(h_hi[:, k, :], self.t[:, k, :], ACT.Identity,
                                         bias=self.shift(k)).then_inc(h_hi_done, 1)

            def vector(self, dve, st):
                self.wait_x(dve, KC - 1)
                dve.wait_ge(root_done, self.n + 1)
                st.link(nc.vector.reciprocal(self.rstd[:, :], self.root[:, :]))

                def low(k):
                    dve.wait_ge(h_hi_done, KC * self.n + k + 1)
                    nc.vector.scalar_tensor_tensor(h_lo[:, k, :], self.t[:, k, :], self.shift(k), h_hi[:, k, :],
                                                   ALU.add, ALU.subtract).then_inc(h_ready, 1)

                for k in range(KC):
                    nc.vector.scalar_tensor_tensor(self.t[:, k, :], x[:, k, :], self.scale(k), self.rstd[:, :],
                                                   ALU.mult, ALU.mult).then_inc(scaled, 1)
                    if k and not self.final:
                        low(k - 1)
                if not self.final:
                    low(KC - 1)

            def tensor(self, pe):
                for k in range(KC):
                    pe.wait_ge(sq_done, KC * self.n + k + 1)
                    last = nc.tensor.matmul(bank[:, self.bank, :], ones[:, :], self.sq[:, k, :],
                                            start=(k == 0), stop=(k == KC - 1))
                last.then_inc(ms_done, 1)

        class Project:

            def __init__(self, name, gate, wait_chunk):
                self.m0, self.gate, self.wait_chunk = FIRST_UNIT[name], gate, wait_chunk
                self.base = KC * updates[0]
                updates[0] += 1

            def scalar(self, act, st):
                for u in range(4):
                    split_next_hi(act, self.m0 + u)

            def vector(self, dve, st):
                for u in range(4):
                    m = self.m0 + u
                    dve.wait_ge(unit_used, m + 1)
                    for b in range(2):
                        o = 2 * u + b
                        nc.vector.scalar_tensor_tensor(x[:, o, :], bank[:, 2 * slot(m) + b, :], self.gate(o),
                                                       x[:, o, :], ALU.mult, ALU.add).then_inc(x_ready, 1)
                    split_next_lo(dve, m)

            def tensor(self, pe):
                for u in range(4):
                    m = self.m0 + u
                    pe.wait_ge(lo_split, m + 1)
                    if u >= 2:
                        pe.wait_ge(x_ready, self.base + 2 * (u - 1))
                    for b in range(2):
                        last = features(pe, m, b, bank[:, 2 * slot(m) + b, :],
                                        self.wait_chunk if u == 0 and b == 0 else None)
                    last.then_inc(unit_used, 1)

        ffns = [0]
        silu_done = sem("silu_done")
        gated = sem("gated")
        g_hi_done = sem("g_hi_done")
        g_ready = sem("g_ready")
        down_block = sem("down_block")

        class FeedForward:
            silu, gu = area(2 * FB * S, 2, S), area(2 * FB * S + 2 * S, 2, S)

            def __init__(self, name, gate, norm):
                self.m0, self.gate, self.norm = FIRST_UNIT[name], gate, norm
                self.md = self.m0 + FB
                self.j0 = FB * ffns[0]
                self.f = ffns[0]
                ffns[0] += 1
                self.base = KC * updates[0]
                updates[0] += 1

            def scalar(self, act, st):
                def block(r, i):
                    m, b = self.m0 + r, 2 * slot(self.m0 + r)
                    act.wait_ge(unit_used, m + 1 + 2 * i)
                    nc.scalar.activation(self.silu[:, r, :], bank[:, b, :], ACT.Silu).then_inc(silu_done, 1)
                    act.wait_ge(gated, self.j0 + r + 1 + 2 * i)
                    nc.scalar.activation(g_hi[:, bass.ds(2 * i + r, 1), :], self.gu[:, r:r + 1, :],
                                         ACT.Copy).then_inc(g_hi_done, 1)
                    split_next_hi(act, m, i)

                with act.Fori(0, FB // 2) as i:
                    block(0, i)
                    block(1, i)

                def rows(d, i):
                    act.wait_ge(unit_used, self.md + d + 1 + 2 * i)
                    split_next_hi(act, self.md + d, i)

                rows(0, 0)
                with act.Fori(0, 4) as i:
                    rows(1, i)
                    rows(2, i)
                rows(9, 0)
                rows(10, 0)

            def vector(self, dve, st):
                def block(r, i):
                    m, b = self.m0 + r, 2 * slot(self.m0 + r)
                    dve.wait_ge(silu_done, self.j0 + r + 1 + 2 * i)
                    nc.vector.tensor_tensor(self.gu[:, r, :], self.silu[:, r, :], bank[:, b + 1, :],
                                            ALU.mult).then_inc(gated, 1)
                    dve.wait_ge(g_hi_done, self.j0 + r + 1 + 2 * i)
                    nc.vector.tensor_tensor(g_lo[:, bass.ds(2 * i + r, 1), :], self.gu[:, r:r + 1, :],
                                            g_hi[:, bass.ds(2 * i + r, 1), :], ALU.subtract).then_inc(g_ready, 1)
                    split_next_lo(dve, m, i)

                with dve.Fori(0, FB // 2) as i:
                    block(0, i)
                    block(1, i)
                split_next_lo(dve, self.md)
                with dve.Fori(0, 4) as i:
                    split_next_lo(dve, self.md + 1, i)
                    split_next_lo(dve, self.md + 2, i)
                for o in range(KC):
                    if o < KC - 1:
                        dve.wait_ge(down_block, (KC - 1) * self.f + o + 1)
                    else:
                        dve.wait_ge(unit_used, self.md + 11)
                    nc.vector.scalar_tensor_tensor(x[:, o, :], bank[:, o, :], self.gate(o), x[:, o, :],
                                                   ALU.mult, ALU.add).then_inc(x_ready, 1)
                split_next_lo(dve, self.md + 9)
                split_next_lo(dve, self.md + 10)

            def tensor(self, pe):
                def block(r, i, first=False):
                    m = self.m0 + r
                    pe.wait_ge(lo_split, m + 1 + 2 * i)
                    if not first:
                        pe.wait_ge(gated, self.j0 + r - 1 + 2 * i)
                    for b in range(2):
                        last = features(pe, m, b, bank[:, 2 * slot(m) + b, :],
                                        self.norm.wait_chunk if first and r == 0 and b == 0 else None)
                    last.then_inc(unit_used, 1)

                block(0, 0, True)
                block(1, 0, True)
                with pe.Fori(1, FB // 2) as i:
                    block(0, i)
                    block(1, i)

                def rows(d, i, first=False, end=False):
                    m = self.md + d
                    wh, wl = (w[:, slot(m), :].rearrange("p (k n) -> p k n", k=2) for w in (w_hi, w_lo))
                    pe.wait_ge(lo_split, m + 1 + 2 * i)
                    order = [(k, o) for k in range(2) for o in range(KC)]
                    if end:
                        order = [(k, o) for o in range(KC) for k in range(2)]
                    for k, o in order:
                        c = bass.ds(2 * d + k + 4 * i, 1)
                        r = slice(o * P, o * P + P)
                        last = three_passes(bank[:, o, :], (wh[:, k, r], wl[:, k, r]),
                                            (g_hi[:, c, :], g_lo[:, c, :]), first and k == 0, end and k == 1)
                        if end and k == 1 and o < KC - 1:
                            last.then_inc(down_block, 1)
                    last.then_inc(unit_used, 1)

                pe.wait_ge(g_ready, self.j0 + FB)
                rows(0, 0, first=True)
                with pe.Fori(0, 4) as i:
                    rows(1, i)
                    rows(2, i)
                rows(9, 0)
                rows(10, 0, end=True)

        tails = [0]
        tail_cols = 0

        class ToFeatures:

            def __init__(self, name, rows, first, n, group=None, squares=None, gate=None, gain=None, banks=(4, 5),
                         ready=None):
                self.rows, self.first, self.n, self.group, self.squares = rows, first, n, group, squares
                self.gate, self.gain, self.banks, self.ready = gate, gain, banks, ready
                self.count = TB * n * P // group if group else 0
                self.sq = sem(name + "_sq")
                self.ss = sem(name + "_ss")
                self.root = sem(name + "_root")
                self.rows_ready = sem(name + "_rows_ready")
                self.turned = sem(name + "_turned")
                self.hi = sem(name + "_hi")
                self.lo = sem(name + "_lo")
                self.sums, self.roots, self.inv = (small[:, a:a + self.count] for a in (0, 64, 128))

            def flat(self, v):
                return v.rearrange("p t n -> p (t n)")

            def grouped(self, v):
                return self.flat(v).rearrange("p (a g) -> p a g", g=self.group)

            def scalar_norm(self, act):
                if self.group:
                    self.ready(act)
                    nc.scalar.activation(self.squares, self.flat(self.rows), ACT.Square).then_inc(self.sq, 1)
                    act.wait_ge(self.ss, 1)
                    nc.scalar.activation(self.roots, self.sums, ACT.Sqrt, bias=eps,
                                         scale=1.0 / self.group).then_inc(self.root, 1)

            def vector_norm(self, dve, st):
                if self.group:
                    dve.wait_ge(self.sq, 1)
                    nc.vector.tensor_reduce(self.sums, self.squares.rearrange("p (a g) -> p a g", g=self.group),
                                            AX.X, ALU.add).then_inc(self.ss, 1)
                    dve.wait_ge(self.root, 1)
                    st.link(nc.vector.reciprocal(self.inv, self.roots))
                    last = nc.vector.tensor_tensor(
                        self.grouped(self.rows), self.grouped(self.rows),
                        self.inv.unsqueeze(2).to_broadcast([P, self.count, self.group]), ALU.mult)
                    if self.gate is not None:
                        st.link(last)
                        last = nc.vector.tensor_tensor(self.flat(self.rows), self.flat(self.rows),
                                                       self.flat(self.gate), ALU.mult)
                    last.then_inc(self.rows_ready, 1)

            def scalar(self, act, st):
                self.scalar_norm(act)
                for b in range(self.n):
                    act.wait_ge(self.turned, b + 1)
                    out, src = h_hi[:, self.first + b, :], bank[:, self.banks[b % 2], :]
                    if self.gain:
                        ins = nc.scalar.activation(out, src, ACT.Identity, bias=0.0, scale=self.gain(b))
                    else:
                        ins = nc.scalar.activation(out, src, ACT.Copy)
                    ins.then_inc(self.hi, 1)

            def vector(self, dve, st):
                self.vector_norm(dve, st)
                for b in range(self.n):
                    dve.wait_ge(self.hi, b + 1)
                    out, src, hi = (h_lo[:, self.first + b, :], bank[:, self.banks[b % 2], :],
                                    h_hi[:, self.first + b, :])
                    if self.gain:
                        ins = nc.vector.scalar_tensor_tensor(out, src, self.gain(b), hi, ALU.mult, ALU.subtract)
                    else:
                        ins = nc.vector.tensor_tensor(out, src, hi, ALU.subtract)
                    ins.then_inc(self.lo, 1)

            def tensor(self, pe):
                if self.group:
                    pe.wait_ge(self.rows_ready, 1)
                else:
                    self.ready(pe)
                for b in range(self.n):
                    if b >= 2:
                        pe.wait_ge(self.lo, b - 1)
                    for t in range(TB):
                        last = nc.tensor.transpose(bank[:, self.banks[b % 2], t * P:t * P + P],
                                                   self.rows[:, t, b * P:b * P + P], ident)
                    last.then_inc(self.turned, 1)

            def wait_chunk(self, eng, k):
                if self.first <= k < self.first + self.n:
                    eng.wait_ge(self.lo, k - self.first + 1)

        class Softmax:

            def __init__(self, name, n, keys, scale, scores, values, out, n_out, p, pt, ready):
                self.n, self.keys, self.scale, self.scores, self.values, self.out = n, keys, scale, scores, values, out
                self.n_out, self.p, self.pt, self.ready = n_out, p, pt, ready
                (self.scored, self.max_done, self.p_done, self.turned, self.pt_done, self.summed,
                 self.out_done) = (sem(name + s) for s in ("_scored", "_max_done", "_p_done", "_turned", "_pt_done",
                                                           "_summed", "_out_done"))
                self.mx, self.nm, self.rs, self.rc = (small[:, 192 + 32 * a:224 + 32 * a] for a in range(4))

            def tensor(self, pe):
                self.ready(pe)
                for s in range(self.n + 2):
                    if s < self.n:
                        if s >= 2:
                            pe.wait_ge(self.p_done, s - 1)
                        pairs = self.scores(s)
                        for a, (q, k) in enumerate(pairs):
                            last = nc.tensor.matmul(bank[:, 4 + s % 2, 0:self.keys], q, k, start=(a == 0),
                                                    stop=(a == len(pairs) - 1))
                        last.then_inc(self.scored, 1)
                    t = s - 1
                    if 0 <= t < self.n:
                        pe.wait_ge(self.p_done, t + 1)
                        if t >= 2:
                            pe.wait_ge(self.pt_done, t - 1)
                        for k in range(self.keys // P):
                            last = nc.tensor.transpose(bank[:, 6 + t % 2, k * P:k * P + P],
                                                       self.p[:, t % 2, k * P:k * P + P], ident)
                        last.then_inc(self.turned, 1)
                    t = s - 2
                    if 0 <= t < self.n:
                        pe.wait_ge(self.pt_done, t + 1)
                        if t >= 2:
                            pe.wait_ge(self.out_done, t - 1)
                        for k in range(self.keys // P):
                            last = nc.tensor.matmul(bank[:, t % 2, 0:self.n_out], self.pt[:, t % 2, k * P:k * P + P],
                                                    self.values(t, k), start=(k == 0),
                                                    stop=(k == self.keys // P - 1))
                        last.then_inc(self.summed, 1)

            def vector(self, dve, st):
                for s in range(self.n + 2):
                    if s < self.n:
                        dve.wait_ge(self.scored, s + 1)
                        st.link(nc.vector.tensor_reduce(self.mx[:, s:s + 1], bank[:, 4 + s % 2, 0:self.keys], AX.X,
                                                        ALU.max))
                        nc.vector.tensor_scalar(self.nm[:, s:s + 1], self.mx[:, s:s + 1], -self.scale, None,
                                                ALU.mult).then_inc(self.max_done, 1)
                    t = s - 2
                    if t >= 0:
                        dve.wait_ge(self.summed, t + 1)
                        st.link(nc.vector.reciprocal(self.rc[:, t:t + 1], self.rs[:, t:t + 1]))
                        nc.vector.tensor_scalar(self.out(t), bank[:, t % 2, 0:self.n_out], self.rc[:, t:t + 1], None,
                                                ALU.mult).then_inc(self.out_done, 1)

            def scalar(self, act, st):
                for s in range(self.n + 1):
                    if s < self.n:
                        act.wait_ge(self.max_done, s + 1)
                        if s >= 2:
                            act.wait_ge(self.turned, s - 1)
                        nc.scalar.activation(self.p[:, s % 2, :], bank[:, 4 + s % 2, 0:self.keys], ACT.Exp,
                                             bias=self.nm[:, s:s + 1], scale=self.scale,
                                             accum_out=self.rs[:, s:s + 1]).then_inc(self.p_done, 1)
                    t = s - 1
                    if t >= 0:
                        act.wait_ge(self.turned, t + 1)
                        if t >= 2:
                            act.wait_ge(self.summed, t - 1)
                        nc.scalar.activation(self.pt[:, t % 2, :], bank[:, 6 + t % 2, 0:self.keys],
                                             ACT.Copy).then_inc(self.pt_done, 1)

        class Even:
            PAD = 8
            W = S + 2 * PAD
            u = area(0, 4, W)
            sums = area(4 * W, 2, W)
            pooled = area(6 * W, 4, S)
            mixed = area(6 * W + 4 * S, 4, S)
            qk = area(8192, 5, S)
            v = area(10752, TB, P)
            sq = area(11264, 5, S)
            qn = area(13824, 5, S)
            counts, cos, sin, wp = (area(16384, 4, S), area(18432, S), area(18944, S), area(19456, 4, P))
            inv, t = area(19968, S), area(20480, 2, S)
            p, pt = area(21504, 2, S), area(22528, 2, S)
            out = area(23552, TB, 4 * P)

            def __init__(self, norm):
                self.norm, self.m0 = norm, FIRST_UNIT["even_in"]
                self.evac = sem("even_evac")
                self.padded = sem("even_padded")
                self.pool_ready, self.pool_mm, self.pool_out = sem("pool_ready"), sem("pool_mm"), sem("pool_out")
                self.mix_hi, self.mix_lo = sem("pool_hi"), sem("pool_lo")
                self.sq_done, self.ms_mm, self.rooted = sem("qk_sq"), sem("qk_ms"), sem("qk_root")
                self.inv_done, self.spread = sem("qk_inv"), sem("qk_spread")
                self.normed, self.swapped, self.turned = sem("qk_normed"), sem("qk_swapped"), sem("qk_rope")

                def scores(s):
                    head, t = s // TB, s % TB
                    b, half = head // 2, slice(64 * (head % 2), 64 * (head % 2) + 64)
                    return [(self.qk[half, b, t * P:t * P + P], self.qk[half, 4, :])]

                def values(s, k):
                    half = 64 * ((s // TB) % 2)
                    return self.v[:, k, half:half + 64]

                def out(s):
                    head, t = s // TB, s % TB
                    return self.out[:, t, head * 64:head * 64 + 64]

                self.softmax = Softmax("even", 8 * TB, S, 64 ** -0.5, scores, values, out, 64, self.p, self.pt,
                                       lambda pe: pe.wait_ge(self.turned, 5))
                self.tail = ToFeatures("even_rows", self.out, 4, 4,
                                       ready=lambda pe: pe.wait_ge(self.softmax.out_done, 8 * TB))

            def wait_chunk(self, eng, k):
                if k < 4:
                    eng.wait_ge(self.mix_lo, k + 1)
                else:
                    self.tail.wait_chunk(eng, k)

            def scalar(self, act, st):
                for u in range(5):
                    m, b = self.m0 + u, 2 * slot(self.m0 + u)
                    act.wait_ge(unit_used, m + 1)
                    if u < 2:
                        for r in range(2):
                            ins = nc.scalar.activation(self.u[:, 2 * u + r, self.PAD:self.PAD + S], bank[:, b + r, :],
                                                       ACT.Copy)
                            ins.then_inc(self.evac, 1)
                    elif u < 4:
                        for r in range(2):
                            nc.scalar.activation(self.qk[:, 2 * (u - 2) + r, :], bank[:, b + r, :],
                                                 ACT.Copy).then_inc(self.evac, 1)
                    else:
                        nc.scalar.activation(self.qk[:, 4, :], bank[:, b, :], ACT.Copy).then_inc(self.evac, 1)
                        nc.scalar.activation(self.v.rearrange("p t n -> p (t n)"), bank[:, b + 1, :],
                                             ACT.Copy).then_inc(self.evac, 1)
                    split_next_hi(act, m)
                act.wait_ge(self.evac, 10)
                nc.scalar.activation(self.sq.rearrange("p a n -> p (a n)"), self.qk.rearrange("p a n -> p (a n)"),
                                     ACT.Square).then_inc(self.sq_done, 1)
                act.wait_ge(self.ms_mm, 1)
                nc.scalar.activation(self.t[0:16, 0, :], bank[0:16, 4, :], ACT.Sqrt, bias=par[0:16, PCOL["eps"]:PCOL["eps"] + 1],
                                     scale=1.0 / 64).then_inc(self.rooted, 1)
                for g in range(4):
                    act.wait_ge(self.pool_out, g + 1)
                    nc.scalar.activation(h_hi[:, g, :], self.mixed[:, g, :], ACT.Copy).then_inc(self.mix_hi, 1)
                self.softmax.scalar(act, st)
                self.tail.scalar(act, st)

            def vector(self, dve, st):
                for u in range(5):
                    if u == 1:
                        dve.wait_ge(unit_used, self.m0 + 1)
                        st.add(nc.vector.memset(self.u[:, :, 0:self.PAD], 0.0))
                        st.link(nc.vector.memset(self.u[:, :, self.PAD + S:], 0.0))
                    split_next_lo(dve, self.m0 + u)
                dve.wait_ge(self.evac, 4)
                for g in range(4):
                    src, n = self.u[:, g, :], self.W
                    for a in range(g + 1):
                        step = 1 << a
                        n -= step
                        dst = self.sums[:, a % 2, :]
                        st.link(nc.vector.tensor_tensor(dst[:, 0:n], src[:, 0:n], src[:, step:step + n], ALU.add))
                        src = dst
                    if g == 0:
                        dve.wait_ge(even_loaded, 48)
                    lead = self.PAD - (1 << g)
                    other = self.sums[:, (g + 1) % 2, 0:S]
                    st.link(nc.vector.tensor_tensor(other, src[:, lead:lead + S], self.counts[:, g, :], ALU.mult))
                    nc.vector.tensor_tensor(self.pooled[:, g, :], other, self.u[:, g, self.PAD:self.PAD + S],
                                            ALU.subtract).then_inc(self.pool_ready, 1)
                    dve.wait_ge(self.pool_ready, g + 1)
                dve.wait_ge(self.rooted, 1)
                nc.vector.reciprocal(self.inv[0:16, :], self.t[0:16, 0, :]).then_inc(self.inv_done, 1)
                for g in range(4):
                    dve.wait_ge(self.pool_mm, g + 1)
                    nc.vector.tensor_scalar(self.mixed[:, g, :], bank[:, g, :], col("b_pool", g), col("pool_scale", g),
                                            ALU.add, ALU.mult).then_inc(self.pool_out, 1)
                for g in range(4):
                    dve.wait_ge(self.mix_hi, g + 1)
                    nc.vector.tensor_tensor(h_lo[:, g, :], self.mixed[:, g, :], h_hi[:, g, :],
                                            ALU.subtract).then_inc(self.mix_lo, 1)
                for i in range(6):
                    b = i
                    if b < 5:
                        dve.wait_ge(self.spread, b + 1)
                        nc.vector.scalar_tensor_tensor(self.qn[:, b, :], self.qk[:, b, :],
                                                       col("q_gain") if b < 4 else col("k_gain"),
                                                       bank[:, 4 + b % 2, :], ALU.mult,
                                                       ALU.mult).then_inc(self.normed, 1)
                    b = i - 1
                    if b >= 0:
                        dve.wait_ge(self.normed, b + 1)
                        st.add(nc.vector.tensor_tensor(self.t[:, 0, :], self.qn[:, b, :], self.cos, ALU.mult))
                        dve.wait_ge(self.swapped, b + 1)
                        st.link(nc.vector.tensor_tensor(self.t[:, 1, :], bank[:, 6 + b % 2, :], self.sin, ALU.mult))
                        nc.vector.tensor_tensor(self.qk[:, b, :], self.t[:, 0, :], self.t[:, 1, :],
                                                ALU.add).then_inc(self.turned, 1)
                        dve.wait_ge(self.turned, b + 1)
                self.softmax.vector(dve, st)
                self.tail.vector(dve, st)

            def tensor(self, pe):
                for u in range(5):
                    m, b = self.m0 + u, 2 * slot(self.m0 + u)
                    pe.wait_ge(lo_split, m + 1)
                    if u >= 2:
                        pe.wait_ge(self.evac, 2 * (u - 1))
                    elif u == 0:
                        pe.wait_ge(Conditioning.mod_done, 1)
                    features(pe, m, 0, bank[:, b, :], self.norm.wait_chunk if u == 0 else None)
                    if u < 4:
                        last = features(pe, m, 1, bank[:, b + 1, :])
                    else:
                        last = tokens(pe, m, bank[:, b + 1, :].rearrange("p (t n) -> p t n", t=TB), c0=P, n=P)
                    last.then_inc(unit_used, 1)
                pe.wait_ge(self.sq_done, 1)
                pair = table("pair_rows")
                for b in range(5):
                    last = nc.tensor.matmul(bank[0:16, 4, :], pair[:, 15 - 2 * b:31 - 2 * b], self.sq[:, b, :],
                                            start=(b == 0), stop=(b == 4))
                last.then_inc(self.ms_mm, 1)
                pe.wait_ge(even_loaded, 48)
                for g in range(4):
                    pe.wait_ge(self.pool_ready, g + 1)
                    nc.tensor.matmul(bank[:, g, :], self.wp[:, g, :], self.pooled[:, g, :], start=True,
                                     stop=True).then_inc(self.pool_mm, 1)
                pe.wait_ge(self.inv_done, 1)

                def spread(b):
                    if b >= 2:
                        pe.wait_ge(self.normed, b - 1)
                    rows = table("pair_spread")[0:16, b * P:b * P + P]
                    nc.tensor.matmul(bank[:, 4 + b % 2, :], rows, self.inv[0:16, :], start=True,
                                     stop=True).then_inc(self.spread, 1)

                spread(0)
                for b in range(5):
                    if b < 4:
                        spread(b + 1)
                    pe.wait_ge(self.normed, b + 1)
                    if b >= 2:
                        pe.wait_ge(self.turned, b - 1)
                    nc.tensor.matmul(bank[:, 6 + b % 2, :], table("swap"), self.qn[:, b, :], start=True,
                                     stop=True).then_inc(self.swapped, 1)
                pe.wait_ge(self.pool_out, 4)
                self.softmax.tensor(pe)
                self.tail.tensor(pe)

        class Mlstm:
            R, H, PAD = 40, 8, 4
            SEG = [[0, 512, 896, 1152], [0, 128, 384, 768]]
            raw_qk = area(0, 8, S + PAD)
            out = area(0, TB, D)
            qk = area(4128, 8, S)
            squares = area(4128, TB * D)
            v = area(8224, TB, H, P + 1)
            o = area(12352, TB, D)
            e, se = area(16448, 2, 1280), area(19008, 2, 1280)
            gates, fb, ab, lf, f, g, em, ex, ln = (area(16448 + a * S, S) for a in range(9))
            md = area(21568, 2, S)
            m = area(22592, S)
            acc = area(23104, 2, S)

            def __init__(self, norm):
                self.norm, self.m0 = norm, FIRST_UNIT["odd_in"]
                (self.s_evac, self.s_sel, self.s_abs, self.s_ln, self.s_em, self.s_em_in, self.s_cols_mm, self.s_cols,
                 self.s_conv, self.s_silu, self.s_scored, self.s_spread, self.s_masked, self.s_weights, self.s_se,
                 self.s_summed, self.s_out) = (
                    sem("mlstm_" + n) for n in ("evac", "sel", "abs", "ln", "em", "em_in", "cols_mm", "cols", "conv",
                                                "silu", "scored", "spread", "masked", "weights", "se", "summed",
                                                "out"))
                self.tail = ToFeatures("mlstm_rows", self.out, 0, 8, group=P, squares=self.squares, gate=self.o,
                                       gain=lambda b: col("head_gain", b), banks=(0, 1),
                                       ready=lambda act: act.wait_ge(self.s_out, 2 * self.H))
                self.gcol, self.emcol = small[:, 320:480], small[:, 160:320]

            def span(self, d, a):
                return (a * P, S) if d == 0 else (0, (a + 1) * P)

            def wait_chunk(self, eng, k):
                self.tail.wait_chunk(eng, k)

            def scalar(self, act, st):
                R = self.R
                for u in range(13):
                    m, b = self.m0 + u, 2 * slot(self.m0 + u)
                    act.wait_ge(unit_used, m + 1)
                    if u == 0:
                        nc.scalar.activation(self.gates, bank[:, b, :], ACT.Copy).then_inc(self.s_evac, 1)
                    elif u < 5:
                        nc.scalar.activation(self.raw_qk[:, 2 * u - 2:2 * u, 2:2 + S], bank[:, b:b + 2, :],
                                             ACT.Copy).then_inc(self.s_evac, 1)
                    elif u < 9:
                        h = 2 * (u - 5)
                        for t in range(TB):
                            ins = nc.scalar.activation(
                                self.v[:, t, h:h + 2, 0:P],
                                two_banks(m)[:, t, :].rearrange("p (h n) -> p h n", h=2), ACT.Copy)
                            if t < TB - 1:
                                st.add(ins)
                        ins.then_inc(self.s_evac, 1)
                    else:
                        c = 256 * (u - 9)
                        nc.scalar.activation(self.o[:, :, c:c + 256], two_banks(m), ACT.Sigmoid).then_inc(self.s_evac, 1)
                    split_next_hi(act, m)
                    if u == 2:
                        act.wait_ge(self.s_abs, 1)
                        st.link(nc.scalar.activation(self.ex[0:R, :], self.ab[0:R, :], ACT.Exp, scale=-1.0))
                        nc.scalar.activation(self.ln[0:R, :], self.ex[0:R, :], ACT.Ln, bias=1.0).then_inc(self.s_ln, 1)
                    if u == 3:
                        act.wait_ge(self.s_em_in, 1)
                        nc.scalar.activation(self.em[0:R, :], self.fb[0:R, :], ACT.Exp, scale=-1.0).then_inc(self.s_em, 1)
                    if u == 7:
                        for c in range(8):
                            act.wait_ge(self.s_conv, c + 1)
                            nc.scalar.activation(self.qk[:, c, :], self.acc_of(c), ACT.Silu,
                                                 bias=col("conv_b", c)).then_inc(self.s_silu, 1)
                act.wait_ge(self.s_cols, 1)
                for q in range(2 * self.H):
                    h, d = q // 2, q % 2
                    r = h + 32 * d
                    act.wait_ge(self.s_masked, q + 1)
                    if q >= 2:
                        act.wait_ge(self.s_se, q - 1)
                    for a in range(TB):
                        lo, hi = self.span(d, a)
                        seg = self.e[:, q % 2, self.SEG[d][a]:self.SEG[d][a] + hi - lo]
                        bias = self.gcol[:, a * R + r:a * R + r + 1]
                        at_ = a * P - lo
                        ins = nc.scalar.activation(seg[:, at_:at_ + P], self.md[:, q % 2, a * P:a * P + P], ACT.Exp,
                                                   bias=bias, scale=-1.0)
                        if hi - lo > P:
                            st.add(ins)
                            rest = (P, hi - lo) if d == 0 else (0, hi - lo - P)
                            ins = nc.scalar.activation(seg[:, rest[0]:rest[1]],
                                                       bank[:, 4 + q % 2, lo + rest[0]:lo + rest[1]], ACT.Exp,
                                                       bias=bias, scale=-1.0)
                        if a < TB - 1:
                            st.add(ins)
                        else:
                            ins.then_inc(self.s_weights, 1)
                self.tail.scalar(act, st)

            def acc_of(self, c):
                return self.qk[:, c, :]

            def vector(self, dve, st):
                R = self.R
                rows = (slice(0, 8), slice(32, 40))
                for u in range(13):
                    m = self.m0 + u
                    if u == 0:
                        dve.wait_ge(unit_used, m + 1)
                        st.add(nc.vector.memset(self.raw_qk[:, :, 0:2], 0.0))
                        st.link(nc.vector.memset(self.raw_qk[:, :, 2 + S:], 0.0))
                        st.add(nc.vector.memset(self.v[:, :, :, P:P + 1], 1.0))
                        for v in (self.f, self.m):
                            st.add(nc.vector.memset(v[0:R, :], 0.0))
                    split_next_lo(dve, m)
                    if u == 1:
                        dve.wait_ge(self.s_sel, 1)
                        st.link(nc.vector.tensor_scalar(self.fb[0:R, :], bank[0:R, 5, :],
                                                        par[0:R, PCOL["gate_b_f"]:PCOL["gate_b_f"] + 1], None, ALU.add))
                        nc.vector.scalar_tensor_tensor(self.ab[0:R, :], self.fb[0:R, :], -1.0, self.fb[0:R, :], ALU.mult,
                                                       ALU.max).then_inc(self.s_abs, 1)
                    if u == 2:
                        dve.wait_ge(self.s_ln, 1)
                        st.link(nc.vector.scalar_tensor_tensor(self.lf[0:R, :], self.fb[0:R, :], 0.0, self.ln[0:R, :],
                                                               ALU.min, ALU.subtract))
                        for d, r in enumerate(rows):
                            way = slice(None, None, -1) if d else slice(None)
                            st.add(nc.vector.tensor_tensor_scan(
                                self.f[r, way], ones[r, 0:1].to_broadcast([8, S]), self.lf[r, way], 0.0, ALU.mult,
                                ALU.add))
                        st.settle()
                        st.link(nc.vector.scalar_tensor_tensor(self.g[0:R, :], bank[0:R, 4, :],
                                                               par[0:R, PCOL["gate_b_i"]:PCOL["gate_b_i"] + 1],
                                                               self.f[0:R, :], ALU.add, ALU.subtract))
                        for d, r in enumerate(rows):
                            way = slice(None, None, -1) if d else slice(None)
                            st.add(nc.vector.tensor_tensor_scan(self.m[r, way], self.g[r, way], self.g[r, way], 0.0,
                                                                ALU.max, ALU.max))
                        st.settle()
                        nc.vector.tensor_tensor(self.fb[0:R, :], self.f[0:R, :], self.m[0:R, :],
                                                ALU.add).then_inc(self.s_em_in, 1)
                    if 1 <= u < 5:
                        dve.wait_ge(self.s_evac, u + 1)
                        for c in (2 * u - 2, 2 * u - 1):
                            acc = self.acc_of(c)
                            for j in range(5):
                                w = col("conv_w", 8 * j + c)
                                src = self.raw_qk[:, c, j:j + S]
                                if j == 0:
                                    ins = nc.vector.tensor_scalar(acc, src, w, None, ALU.mult)
                                else:
                                    ins = nc.vector.scalar_tensor_tensor(acc, src, w, acc, ALU.mult, ALU.add)
                                if j < 4:
                                    st.link(ins)
                                else:
                                    ins.then_inc(self.s_conv, 1)
                    if u == 5:
                        dve.wait_ge(self.s_cols_mm, 1)
                        nc.vector.tensor_copy(small[:, 160:480], bank[:, 6, 0:320]).then_inc(self.s_cols, 1)
                dve.wait_ge(self.s_cols, 1)
                for q in range(2 * self.H + 1):
                    if q < 2 * self.H:
                        self.weigh(dve, st, q)
                    if q >= 1:
                        self.divide(dve, st, q - 1)
                self.tail.vector(dve, st)

            def weigh(self, dve, st, q):
                d = q % 2
                dve.wait_ge(self.s_spread, q + 1)
                if q >= 2:
                    dve.wait_ge(self.s_weights, q - 1)
                hide = table("hide_bwd" if d else "hide_fwd").unsqueeze(1).to_broadcast([P, TB, P])
                nc.vector.tensor_tensor(self.md[:, q % 2, :].rearrange("p (a t) -> p a t", a=TB),
                                        bank[:, 4 + q % 2, :].rearrange("p (a t) -> p a t", a=TB), hide,
                                        ALU.add).then_inc(self.s_masked, 1)
                dve.wait_ge(self.s_weights, q + 1)
                dve.wait_ge(self.s_scored, q // 2 + 1)
                if q >= 2:
                    dve.wait_ge(self.s_summed, q - 1)
                for a in range(TB):
                    lo, hi = self.span(d, a)
                    seg = slice(self.SEG[d][a], self.SEG[d][a] + hi - lo)
                    ins = nc.vector.scalar_tensor_tensor(self.se[:, q % 2, seg], bank[:, a, lo:hi], 64 ** -0.5,
                                                         self.e[:, q % 2, seg], ALU.mult, ALU.mult)
                    if a < TB - 1:
                        st.add(ins)
                    else:
                        ins.then_inc(self.s_se, 1)

            def divide(self, dve, st, q):
                h, d = q // 2, q % 2
                r = h + 32 * d
                num = bank[:, 6:8, 0:2 * (P + 1)].rearrange("p a (b n) -> p a b n", b=2)
                dn, ab, fl, rc = (small[:, 12 * 4 + 4 * a:12 * 4 + 4 * a + 4] for a in range(4))
                dve.wait_ge(self.s_summed, q + 1)
                st.link(nc.vector.tensor_copy(dn.rearrange("p (a b) -> p a b", a=2).unsqueeze(3), num[:, :, :, P:P + 1]))
                st.link(nc.vector.scalar_tensor_tensor(ab, dn, -1.0, dn, ALU.mult, ALU.max))
                em = self.emcol.rearrange("p (a r) -> p a r", a=TB)[:, :, r]
                st.link(nc.vector.tensor_tensor(fl, ab, em, ALU.max))
                st.link(nc.vector.reciprocal(rc, fl))
                for t in range(TB):
                    out = self.out[:, t, h * P:h * P + P]
                    src = num[:, t // 2, t % 2, 0:P]
                    if d == 0:
                        ins = nc.vector.tensor_scalar(out, src, rc[:, t:t + 1], None, ALU.mult)
                    else:
                        if t == 0:
                            dve.wait_ge(self.s_out, q)
                        ins = nc.vector.scalar_tensor_tensor(out, src, rc[:, t:t + 1], out, ALU.mult, ALU.add)
                    if t < TB - 1:
                        st.add(ins)
                    else:
                        ins.then_inc(self.s_out, 1)

            def tensor(self, pe):
                R = self.R
                for u in range(13):
                    m, b = self.m0 + u, 2 * slot(self.m0 + u)
                    pe.wait_ge(lo_split, m + 1)
                    if u >= 2:
                        pe.wait_ge(self.s_evac, u - 1)
                    if u == 0:
                        last = features(pe, m, 0, bank[:, b, :], self.norm.wait_chunk)
                    elif u < 5:
                        features(pe, m, 0, bank[:, b, :])
                        last = features(pe, m, 1, bank[:, b + 1, :])
                    else:
                        last = tokens(pe, m, two_banks(m))
                    last.then_inc(unit_used, 1)
                    if u == 1:
                        pe.wait_ge(self.s_evac, 1)
                        nc.tensor.matmul(bank[0:R, 4, :], table("gate_i"), self.gates, start=True, stop=True)
                        nc.tensor.matmul(bank[0:R, 5, :], table("gate_f"), self.gates, start=True,
                                         stop=True).then_inc(self.s_sel, 1)
                    if u == 4:
                        pe.wait_ge(self.s_em, 1)
                        for a, src in ((0, self.em), (1, self.g)):
                            for t in range(TB):
                                c = a * TB * R + t * R
                                last = nc.tensor.transpose(bank[:, 6, c:c + R], src[0:R, t * P:t * P + P],
                                                           ident[0:R, 0:R])
                        last.then_inc(self.s_cols_mm, 1)
                pe.wait_ge(self.s_cols, 1)
                pe.wait_ge(self.s_evac, 13)
                pe.wait_ge(self.s_silu, 8)
                for q in range(2 * self.H + 1):
                    if q < 2 * self.H:
                        h, d = q // 2, q % 2
                        r = h + 32 * d
                        if q >= 2:
                            pe.wait_ge(self.s_weights, q - 1)
                        nc.tensor.matmul(bank[:, 4 + q % 2, :], ident[0:R, r:r + 1].to_broadcast([R, P]),
                                         self.m[0:R, :], start=True, stop=True).then_inc(self.s_spread, 1)
                        if d == 0:
                            half = slice(64 * (h % 2), 64 * (h % 2) + 64)
                            if h:
                                pe.wait_ge(self.s_se, 2 * h)
                            for a in range(TB):
                                last = nc.tensor.matmul(bank[:, a, :], self.qk[half, 4 + h // 2, a * P:a * P + P],
                                                        self.qk[half, h // 2, :], start=True, stop=True)
                            last.then_inc(self.s_scored, 1)
                    if q >= 1:
                        self.sum_values(pe, q - 1)
                self.tail.tensor(pe)

            def sum_values(self, pe, q):
                h, d = q // 2, q % 2
                pe.wait_ge(self.s_se, q + 1)
                if q:
                    pe.wait_ge(self.s_out, q)
                for t in range(TB):
                    blocks = range(0, t + 1) if d == 0 else range(t, TB)
                    out = bank[:, 6 + t // 2, (t % 2) * (P + 1):(t % 2 + 1) * (P + 1)]
                    for a in blocks:
                        c = self.SEG[d][a] + t * P - self.span(d, a)[0]
                        last = nc.tensor.matmul(out, self.se[:, q % 2, c:c + P], self.v[:, a, h, :],
                                                start=(a == blocks[0]), stop=(a == blocks[-1]))
                last.then_inc(self.s_summed, 1)

        class Hgrn:
            H = 4
            STEPS = LEVELS + 2
            q, k, b = area(0, H, S), area(2048, H, S), area(4096, H, S)
            f = area(6144, H, S)
            out = area(6144, TB, H * P)
            v, gate = area(8192, TB, H * P), area(10240, TB, H * P)
            sq, sk, sv = area(12288, 4, S), area(14336, 4, S), area(16384, TB, 512)
            diff, e, kq = area(18432, 2, S), area(19456, 2, S), area(20480, 2, S)
            near, far = area(21504, 2, S), area(22528, 2, 768)
            masks, run = area(24064, LEVELS + 1, P), area(25088, S)
            squares = area(4096, 2048)

            def __init__(self, norm):
                self.norm, self.m0 = norm, FIRST_UNIT["mix_in"]
                (self.s_evac, self.s_f, self.s_lf, self.s_b, self.s_diff, self.s_e, self.s_kq, self.s_mm, self.s_cp,
                 self.s_summed, self.s_out, self.s_lb) = (
                    sem("hgrn_" + n) for n in ("evac", "f", "lf", "b", "diff", "e", "kq", "mm", "cp", "summed", "out",
                                               "lb"))
                self.tail = ToFeatures("hgrn_rows", self.out, 0, 4, group=P, squares=self.squares, gate=self.gate,
                                       gain=lambda b: col("hg_gnorm", b), banks=(0, 1),
                                       ready=lambda act: act.wait_ge(self.s_out, self.H))
                self.lb, self.one_lb = small[:, 192:196], small[:, 196:200]
                self.lbt = small[:, 200:224]
                self.tot01 = small[:, 224:228]

            def scalar(self, act, st):
                act.wait_ge(self.s_lb, 1)
                nc.scalar.activation(self.lbt[:, 8:16], self.lbt[:, 0:8], ACT.Exp).then_inc(self.s_lb, 1)
                for u in range(14):
                    m, b = self.m0 + u, 2 * slot(self.m0 + u)
                    act.wait_ge(unit_used, m + 1)
                    both = bank[:, b:b + 2, :]
                    c = 256 * (u % 2)
                    r = slice(2 * (u % 2), 2 * (u % 2) + 2)
                    dst, src, fn, scale = [
                        (self.f[:, r, :], both, ACT.Sigmoid, 1.0), (self.q[:, r, :], both, ACT.Copy, 1.0),
                        (self.v[:, :, c:c + 256], two_banks(m), ACT.Copy, 1.0),
                        (self.gate[:, :, c:c + 256], two_banks(m), ACT.Silu, 1.0),
                        (self.sq[:, r, :], both, ACT.Copy, 0.125), (self.sk[:, r, :], both, ACT.Copy, 1.0),
                        (self.sv[:, :, c:c + 256], two_banks(m), ACT.Copy, 1.0)][u // 2]
                    nc.scalar.activation(dst, src, fn, scale=scale).then_inc(self.s_evac, 1)
                    split_next_hi(act, m)
                    if u == 3:
                        act.wait_ge(self.s_f, 1)
                        nc.scalar.activation(self.f.rearrange("p a n -> p (a n)"), self.f.rearrange("p a n -> p (a n)"),
                                             ACT.Ln).then_inc(self.s_lf, 1)
                act.wait_ge(self.s_b, 1)
                for h in range(self.H):
                    bh = self.b[:, h, :]
                    for l in range(self.STEPS):
                        g = h * self.STEPS + l
                        e = self.e[:, g % 2, :]
                        if g >= 2:
                            act.wait_ge(self.s_kq, g - 1)
                        if l < LEVELS:
                            n = 1 << l
                            act.wait_ge(self.s_diff, h * LEVELS + l + 1)
                            d4 = self.diff[:, (h * LEVELS + l) % 2, :].rearrange("p (b z m) -> p b z m", z=2, m=n)
                            e4 = e.rearrange("p (b z m) -> p b z m", z=2, m=n)
                            st.add(nc.scalar.activation(e4[:, :, 0, :], d4[:, :, 0, :], ACT.Exp, scale=-1.0))
                            nc.scalar.activation(e4[:, :, 1, :], d4[:, :, 1, :], ACT.Exp).then_inc(self.s_e, 1)
                            continue

                        def total(t):
                            return bh[:, t * P + P - 1:t * P + P]

                        if l == LEVELS:
                            parts = [(-1.0, total(0)), (1.0, 0.0), (-1.0, total(2)), (1.0, 0.0)]
                        else:
                            parts = [(-1.0, self.tot01[:, h:h + 1]), (-1.0, total(1)), (1.0, 0.0), (1.0, total(2))]
                        for t, (sign, bias) in enumerate(parts):
                            ins = nc.scalar.activation(e[:, t * P:t * P + P], bh[:, t * P:t * P + P], ACT.Exp,
                                                       bias=bias, scale=sign)
                            if t < TB - 1:
                                st.add(ins)
                            else:
                                ins.then_inc(self.s_e, 1)
                    if h:
                        self.copy_out(act, h - 1)
                self.copy_out(act, self.H - 1)

            def copy_out(self, act, h):
                act.wait_ge(self.s_summed, h + 1)
                nc.scalar.activation(self.out[:, :, h * P:h * P + P],
                                     bank[:, 4 + h % 2, :].rearrange("p (t n) -> p t n", t=TB),
                                     ACT.Copy).then_inc(self.s_out, 1)

            def vector(self, dve, st):
                raws = par[:, PCOL["lb_raw0"]:PCOL["lb_raw0"] + 8].rearrange("p (a b) -> p a b", a=2)
                t = self.lbt
                st.link(nc.vector.tensor_tensor(t[:, 16:20], raws[:, 0, :], raws[:, 1, :], ALU.max))
                st.add(nc.vector.tensor_tensor(t[:, 0:4], raws[:, 0, :], t[:, 16:20], ALU.subtract))
                nc.vector.tensor_tensor(t[:, 4:8], raws[:, 1, :], t[:, 16:20], ALU.subtract).then_inc(self.s_lb, 1)
                st.settle()
                dve.wait_ge(self.s_lb, 2)
                st.link(nc.vector.tensor_tensor(t[:, 16:20], t[:, 8:12], t[:, 12:16], ALU.add))
                st.link(nc.vector.reciprocal(t[:, 20:24], t[:, 16:20]))
                st.link(nc.vector.tensor_tensor(self.lb, t[:, 8:12], t[:, 20:24], ALU.mult))
                st.link(nc.vector.tensor_scalar(self.one_lb, self.lb, -1.0, 1.0, ALU.mult, ALU.add))
                dve.wait_ge(mix_loaded, 16)
                for u in range(14):
                    split_next_lo(dve, self.m0 + u)
                    if u == 2:
                        dve.wait_ge(self.s_evac, 2)
                        for h in range(self.H):
                            st.link(nc.vector.tensor_scalar(self.f[:, h, :], self.f[:, h, :], self.one_lb[:, h:h + 1],
                                                            self.lb[:, h:h + 1], ALU.mult, ALU.add))
                        nc.vector.tensor_scalar(self.k.rearrange("p a n -> p (a n)"),
                                                self.f.rearrange("p a n -> p (a n)"), -1.0, 1.0, ALU.mult,
                                                ALU.add).then_inc(self.s_f, 1)
                    if u == 4:
                        dve.wait_ge(self.s_lf, 1)
                        for h in range(self.H):
                            st.add(nc.vector.tensor_tensor_scan(self.b[:, h, :], self.run, self.f[:, h, :], 0.0,
                                                                ALU.mult, ALU.add))
                        st.settle()
                        nc.vector.tensor_tensor(self.tot01, self.b[:, :, P - 1], self.b[:, :, 2 * P - 1],
                                                ALU.add).then_inc(self.s_b, 1)
                dve.wait_ge(self.s_evac, 14)
                dve.wait_ge(self.s_b, 1)
                n = self.H * self.STEPS
                for g in range(n + 1):
                    if g == 0:
                        self.differ(dve, 0)
                    if g < n:
                        if g + 1 < n:
                            self.differ(dve, g + 1)
                        self.weigh(dve, st, g)
                    if g:
                        self.keep(dve, g - 1)
                self.tail.vector(dve, st)

            def differ(self, dve, g):
                h, l = g // self.STEPS, g % self.STEPS
                if l >= LEVELS:
                    return
                n, i = 1 << l, h * LEVELS + l
                if i >= 2:
                    back = i - 2
                    dve.wait_ge(self.s_e, (back // LEVELS) * self.STEPS + back % LEVELS + 1)
                b3 = self.b[:, h, :].rearrange("p (b m) -> p b m", m=2 * n)
                nc.vector.tensor_tensor(self.diff[:, i % 2, :].rearrange("p (b m) -> p b m", m=2 * n), b3,
                                        b3[:, :, n - 1:n].to_broadcast([P, S // (2 * n), 2 * n]),
                                        ALU.subtract).then_inc(self.s_diff, 1)

            def weigh(self, dve, st, g):
                h, l = g // self.STEPS, g % self.STEPS
                n = 1 << l
                dve.wait_ge(self.s_e, g + 1)
                if g >= 2:
                    dve.wait_ge(self.s_mm, g - 1)
                e, kq, k, q = (v.rearrange("p (b z m) -> p b z m", z=2, m=n) for v in
                               (self.e[:, g % 2, :], self.kq[:, g % 2, :], self.k[:, h, :], self.q[:, h, :]))
                st.add(nc.vector.tensor_tensor(kq[:, :, 0, :], k[:, :, 0, :], e[:, :, 0, :], ALU.mult))
                nc.vector.tensor_tensor(kq[:, :, 1, :], q[:, :, 1, :], e[:, :, 1, :], ALU.mult).then_inc(self.s_kq, 1)

            def keep(self, dve, g):
                h, l = g // self.STEPS, g % self.STEPS
                near = self.near[:, h % 2, :].rearrange("p (a t) -> p a t", a=TB)
                far = self.far[:, h % 2, :]
                src = bank[:, g % 2, :]
                dve.wait_ge(self.s_mm, g + 1)
                if l == 0:
                    if h >= 2:
                        dve.wait_ge(self.s_summed, h - 1)
                    diag = self.masks[:, LEVELS:LEVELS + 1, :].to_broadcast([P, TB, P])
                    nc.vector.tensor_tensor(near, bank[:, 2 + h % 2, :].rearrange("p (a t) -> p a t", a=TB), diag,
                                            ALU.mult).then_inc(self.s_cp, 1)
                if l < LEVELS:
                    dve.wait_ge(self.s_cp, h * (self.STEPS + 1) + l + 1)
                    nc.vector.copy_predicated(near, self.masks[:, l:l + 1, :].bitcast(I32).to_broadcast([P, TB, P]),
                                              src.rearrange("p (a t) -> p a t", a=TB)).then_inc(self.s_cp, 1)
                elif l == LEVELS:
                    nc.vector.tensor_copy(far[:, 0:256], src[:, 0:256]).then_inc(self.s_cp, 1)
                else:
                    nc.vector.tensor_copy(far[:, 256:768], src).then_inc(self.s_cp, 1)

            def tensor(self, pe):
                for u in range(14):
                    m, b = self.m0 + u, 2 * slot(self.m0 + u)
                    pe.wait_ge(lo_split, m + 1)
                    if u >= 2:
                        pe.wait_ge(self.s_evac, u - 1)
                    if u // 2 in (0, 1, 4, 5):
                        features(pe, m, 0, bank[:, b, :], self.norm.wait_chunk if u == 0 else None)
                        last = features(pe, m, 1, bank[:, b + 1, :])
                    else:
                        last = tokens(pe, m, two_banks(m))
                    last.then_inc(unit_used, 1)
                pe.wait_ge(self.s_evac, 14)
                for g in range(self.H * self.STEPS):
                    h, l = g // self.STEPS, g % self.STEPS
                    if l == 0:
                        if h >= 2:
                            pe.wait_ge(self.s_cp, (h - 2) * (self.STEPS + 1) + 1)
                        for t in range(TB):
                            r = slice(t * P, t * P + P)
                            nc.tensor.matmul(bank[:, 2 + h % 2, r], self.k[:, h, r], self.q[:, h, r], start=True,
                                             stop=True)
                    pe.wait_ge(self.s_kq, g + 1)
                    if g >= 2:
                        hh, ll = (g - 2) // self.STEPS, (g - 2) % self.STEPS
                        pe.wait_ge(self.s_cp, hh * (self.STEPS + 1) + ll + 2)
                    kq, out = self.kq[:, g % 2, :], bank[:, g % 2, :]
                    if l < LEVELS:
                        for t in range(TB):
                            r = slice(t * P, t * P + P)
                            last = nc.tensor.matmul(out[:, r], kq[:, r], kq[:, r], start=True, stop=True)
                    elif l == LEVELS:
                        nc.tensor.matmul(out[:, 0:P], kq[:, 0:P], kq[:, P:2 * P], start=True, stop=True)
                        last = nc.tensor.matmul(out[:, P:2 * P], kq[:, 2 * P:3 * P], kq[:, 3 * P:4 * P], start=True,
                                                stop=True)
                    else:
                        nc.tensor.matmul(out[:, 0:2 * P], kq[:, 0:P], kq[:, 2 * P:4 * P], start=True, stop=True)
                        last = nc.tensor.matmul(out[:, 2 * P:4 * P], kq[:, P:2 * P], kq[:, 2 * P:4 * P], start=True,
                                                stop=True)
                    last.then_inc(self.s_mm, 1)
                    if l == 1 and h:
                        self.sum_values(pe, h - 1)
                self.sum_values(pe, self.H - 1)
                self.tail.tensor(pe)

            def sum_values(self, pe, h):
                pe.wait_ge(self.s_cp, (h + 1) * (self.STEPS + 1))
                if h >= 2:
                    pe.wait_ge(self.s_out, h - 1)
                near, far = self.near[:, h % 2, :], self.far[:, h % 2, :]
                where = {(a, a): near[:, a * P:a * P + P] for a in range(TB)}
                for n, pair in enumerate([(0, 1), (2, 3), (0, 2), (0, 3), (1, 2), (1, 3)]):
                    where[pair] = far[:, n * P:n * P + P]
                for t in range(TB):
                    for a in range(t + 1):
                        last = nc.tensor.matmul(bank[:, 4 + h % 2, t * P:t * P + P], where[(a, t)],
                                                self.v[:, a, h * P:h * P + P], start=(a == 0), stop=(a == t))
                last.then_inc(self.s_summed, 1)

        class Stick:
            H = 8
            OFF = [0, 512, 896, 1152]
            N = 1280
            z = [area(2048, 1280), area(18432, 1280)]
            e = [area(3328, 1280), area(19712, 1280)]
            l = [area(4608, 1280), area(20992, 1280)]
            out = area(0, TB, 512)
            squares = area(4608, 2048)

            def __init__(self, hgrn):
                self.hg = hgrn
                (self.s_z, self.s_abs, self.s_ln, self.s_l, self.s_suf, self.s_x, self.s_nx, self.s_a, self.s_o,
                 self.s_out) = (sem("stick_" + n) for n in ("z", "abs", "ln", "l", "suf", "x", "nx", "a", "o", "out"))
                self.squares = area(6144 + 2048, 2048)
                self.tail = ToFeatures("stick_rows", self.out, 4, 4, group=64, squares=self.squares,
                                       gain=lambda b: col("sb_gnorm", b), banks=(0, 1),
                                       ready=lambda act: act.wait_ge(self.s_out, self.H))

            def seg(self, a):
                return slice(self.OFF[a], self.OFF[a] + S - a * P)

            def diag(self, a):
                return slice(self.OFF[a], self.OFF[a] + P)

            def wait_chunk(self, eng, k):
                self.hg.tail.wait_chunk(eng, k)
                self.tail.wait_chunk(eng, k)

            def tensor(self, pe):
                pe.wait_ge(self.hg.tail.lo, 4)
                for i in range(self.H + 2):
                    h = i
                    if h < self.H:
                        half = slice(64 * (h % 2), 64 * (h % 2) + 64)
                        if h:
                            pe.wait_ge(self.s_abs, h)
                        for a in range(TB):
                            last = nc.tensor.matmul(bank[:, a, a * P:S], self.hg.sk[half, h // 2, a * P:a * P + P],
                                                    self.hg.sq[half, h // 2, a * P:S], start=True, stop=True)
                        last.then_inc(self.s_z, 1)
                    h = i - 2
                    if h >= 0:
                        pe.wait_ge(self.s_a, h + 1)
                        if h >= 2:
                            pe.wait_ge(self.s_out, h - 1)
                        w = self.z[h % 2]
                        for t in range(TB):
                            for a in range(t + 1):
                                c = self.OFF[a] + (t - a) * P
                                last = nc.tensor.matmul(bank[:, 6 + h % 2, t * 64:t * 64 + 64], w[:, c:c + P],
                                                        self.hg.sv[:, a, h * 64:h * 64 + 64], start=(a == 0),
                                                        stop=(a == t))
                        last.then_inc(self.s_o, 1)
                    h = i - 1
                    if 0 <= h < self.H:
                        pe.wait_ge(self.s_l, h + 1)
                        for a in range(TB):
                            n = TB * h + a
                            if n >= 2:
                                pe.wait_ge(self.s_x, n - 1)
                            for j in range(a, TB):
                                last = nc.tensor.matmul(bank[:, 4 + n % 2, j * P:S],
                                                        table("tri") if j == a else ones,
                                                        self.l[h % 2][:, self.seg(j)], start=(j == a),
                                                        stop=(j == TB - 1))
                            last.then_inc(self.s_suf, 1)

            def vector(self, dve, st):
                for i in range(self.H + 1):
                    h = i
                    if h < self.H:
                        z, e = self.z[h % 2], self.e[h % 2]
                        dve.wait_ge(self.s_z, h + 1)
                        if h >= 2:
                            dve.wait_ge(self.s_o, h - 1)
                        for a in range(TB):
                            st.add(nc.vector.tensor_copy(z[:, self.seg(a)], bank[:, a, a * P:S]))
                        st.settle()
                        nc.vector.scalar_tensor_tensor(e, z, -1.0, z, ALU.mult, ALU.max).then_inc(self.s_abs, 1)
                    h = i - 1
                    if h >= 0:
                        z = self.z[h % 2]
                        for a in range(TB):
                            n = TB * h + a
                            dve.wait_ge(self.s_suf, n + 1)
                            nc.vector.scalar_tensor_tensor(z[:, self.seg(a)], bank[:, 4 + n % 2, a * P:S], -1.0,
                                                           z[:, self.seg(a)], ALU.mult, ALU.add).then_inc(self.s_x, 1)
                        dve.wait_ge(self.s_x, TB * h + TB)
                        for a in range(TB):
                            ins = nc.vector.tensor_tensor(z[:, self.diag(a)], z[:, self.diag(a)], table("neg_strict"),
                                                          ALU.add)
                            if a < TB - 1:
                                st.add(ins)
                            else:
                                ins.then_inc(self.s_nx, 1)
                    h = i
                    if h < self.H:
                        z, e, l = self.z[h % 2], self.e[h % 2], self.l[h % 2]
                        dve.wait_ge(self.s_ln, h + 1)
                        st.link(nc.vector.scalar_tensor_tensor(l, z, 0.0, e, ALU.max, ALU.add))
                        for a in range(TB):
                            ins = nc.vector.tensor_tensor(l[:, self.diag(a)], l[:, self.diag(a)], table("strict"),
                                                          ALU.mult)
                            if a < TB - 1:
                                st.add(ins)
                            else:
                                ins.then_inc(self.s_l, 1)
                self.tail.vector(dve, st)

            def scalar(self, act, st):
                for i in range(self.H + 2):
                    h = i
                    if h < self.H:
                        e = self.e[h % 2]
                        act.wait_ge(self.s_abs, h + 1)
                        st.link(nc.scalar.activation(e, e, ACT.Exp, scale=-1.0))
                        nc.scalar.activation(e, e, ACT.Ln, bias=1.0).then_inc(self.s_ln, 1)
                    h = i - 1
                    if 0 <= h < self.H:
                        act.wait_ge(self.s_nx, h + 1)
                        nc.scalar.activation(self.z[h % 2], self.z[h % 2], ACT.Exp).then_inc(self.s_a, 1)
                    h = i - 2
                    if h >= 0:
                        act.wait_ge(self.s_o, h + 1)
                        nc.scalar.activation(self.out[:, :, h * 64:h * 64 + 64],
                                             bank[:, 6 + h % 2, 0:256].rearrange("p (t n) -> p t n", t=TB),
                                             ACT.Copy).then_inc(self.s_out, 1)
                self.tail.scalar(act, st)

        class Mix:
            def __init__(self, norm):
                self.hg = Hgrn(norm)
                self.sb = Stick(self.hg)
                self.wait_chunk = self.sb.wait_chunk

            def scalar(self, act, st):
                self.hg.scalar(act, st)
                self.hg.tail.scalar(act, st)
                self.sb.scalar(act, st)

            def vector(self, dve, st):
                self.hg.vector(dve, st)
                self.sb.vector(dve, st)

            def tensor(self, pe):
                self.hg.tensor(pe)
                self.sb.tensor(pe)
                self.sb.tail.tensor(pe)

        class Memory:
            HEADS = 4
            mt, sq, t = area(8192, KC, N_MEM), area(10240, KC, N_MEM), area(12288, KC, N_MEM)
            kt, v = area(8192, KC, N_MEM), area(10240, MB, D)
            q = area(0, KC, S)
            p, pt = area(14336, 2, N_MEM), area(14848, 2, N_MEM)
            out = area(15360, TB, D)
            root, rstd = area(23552, N_MEM), area(23808, N_MEM)

            def __init__(self, norm):
                self.norm, self.m0 = norm, FIRST_UNIT["mem_kv"]
                (self.s_sq, self.s_ms, self.s_root, self.s_scaled, self.s_hi, self.s_lo, self.s_evac) = (
                    sem("mem_" + n) for n in ("sq", "ms", "root", "scaled", "hi", "lo", "evac"))

                def scores(s):
                    h, t = s // TB, s % TB
                    return [(self.q[:, 2 * h + c, t * P:t * P + P], self.kt[:, 2 * h + c, :]) for c in range(2)]

                def values(s, k):
                    h = s // TB
                    return self.v[:, k, 256 * h:256 * h + 256]

                def out(s):
                    h, t = s // TB, s % TB
                    return self.out[:, t, 256 * h:256 * h + 256]

                self.softmax = Softmax("mem", self.HEADS * TB, N_MEM, 256 ** -0.5, scores, values, out, 256, self.p,
                                       self.pt, lambda pe: pe.wait_ge(self.s_evac, 12))
                self.tail = ToFeatures("mem_rows", self.out, 0, KC,
                                       ready=lambda pe: pe.wait_ge(self.softmax.out_done, self.HEADS * TB))
                self.wait_chunk = self.tail.wait_chunk

            def scalar(self, act, st):
                act.wait_ge(mem_loaded, 16)
                nc.scalar.activation(self.sq.rearrange("p a n -> p (a n)"), self.mt.rearrange("p a n -> p (a n)"),
                                     ACT.Square).then_inc(self.s_sq, 1)
                act.wait_ge(self.s_ms, 1)
                nc.scalar.activation(self.root, bank[:, 5, 0:N_MEM], ACT.Sqrt, bias=eps, scale=1.0 / D).then_inc(
                    self.s_root, 1)
                for k in range(KC):
                    act.wait_ge(self.s_scaled, k + 1)
                    nc.scalar.activation(mem_hi[:, k, :], self.t[:, k, :], ACT.Copy).then_inc(self.s_hi, 1)
                for u in range(12):
                    m, b = self.m0 + u, 2 * slot(self.m0 + u)
                    act.wait_ge(unit_used, m + 1)
                    if u < 4:
                        dst, src = self.kt[:, 2 * u:2 * u + 2, :], bank[:, b:b + 2, 0:N_MEM]
                    elif u < 8:
                        c = 256 * (u - 4)
                        dst, src = self.v[:, :, c:c + 256], two_banks(m, MB)
                    else:
                        dst, src = self.q[:, 2 * (u - 8):2 * (u - 8) + 2, :], bank[:, b:b + 2, :]
                    nc.scalar.activation(dst, src, ACT.Copy).then_inc(self.s_evac, 1)
                    split_next_hi(act, m)
                self.softmax.scalar(act, st)
                self.tail.scalar(act, st)

            def vector(self, dve, st):
                dve.wait_ge(mem_loaded, 16)
                dve.wait_ge(self.s_root, 1)
                st.link(nc.vector.reciprocal(self.rstd, self.root))
                for k in range(KC):
                    nc.vector.scalar_tensor_tensor(self.t[:, k, :], self.mt[:, k, :], col("mem_kv_norm", k), self.rstd,
                                                   ALU.mult, ALU.mult).then_inc(self.s_scaled, 1)
                for k in range(KC):
                    dve.wait_ge(self.s_hi, k + 1)
                    nc.vector.tensor_tensor(mem_lo[:, k, :], self.t[:, k, :], mem_hi[:, k, :],
                                            ALU.subtract).then_inc(self.s_lo, 1)
                for u in range(12):
                    split_next_lo(dve, self.m0 + u)
                self.softmax.vector(dve, st)
                self.tail.vector(dve, st)

            def tensor(self, pe):
                pe.wait_ge(self.s_sq, 1)
                for k in range(KC):
                    last = nc.tensor.matmul(bank[:, 5, 0:N_MEM], ones, self.sq[:, k, :], start=(k == 0),
                                            stop=(k == KC - 1))
                last.then_inc(self.s_ms, 1)
                pe.wait_ge(self.s_lo, KC)
                for u in range(12):
                    m, b = self.m0 + u, 2 * slot(self.m0 + u)
                    pe.wait_ge(lo_split, m + 1)
                    if u >= 2:
                        pe.wait_ge(self.s_evac, u - 1)
                    if u < 4:
                        features(pe, m, 0, bank[:, b, 0:N_MEM], src=(mem_hi, mem_lo))
                        last = features(pe, m, 1, bank[:, b + 1, 0:N_MEM], src=(mem_hi, mem_lo))
                    elif u < 8:
                        last = tokens(pe, m, two_banks(m, MB), blocks=MB, src=(mem_hi, mem_lo))
                    else:
                        features(pe, m, 0, bank[:, b, :], self.norm.wait_chunk if u == 8 else None)
                        last = features(pe, m, 1, bank[:, b + 1, :])
                    last.then_inc(unit_used, 1)
                self.softmax.tensor(pe)
                self.tail.tensor(pe)

        def shift_of(layer, part):
            return lambda k: mod[:, 48 * layer + 8 * part + k:48 * layer + 8 * part + k + 1]

        def scale_of(layer, part):
            return lambda k: mod1[:, 48 * layer + 8 * part + k:48 * layer + 8 * part + k + 1]

        def gain_of(name):
            return lambda k: col(name, k)

        def constant(name):
            return lambda k: col(name)

        DOWN, OUT = 0, 4
        stages = [Conditioning()]

        def add(stage):
            stages.append(stage)
            return stage

        norm = add(Norm(scale_of(0, 1), shift_of(0, 0), OUT))
        even = add(Even(norm))
        add(Project("even_out", shift_of(0, 2), even.wait_chunk))
        norm = add(Norm(scale_of(0, 4), shift_of(0, 3), OUT))
        add(FeedForward("ffn0", shift_of(0, 5), norm))
        norm = add(Norm(scale_of(1, 1), shift_of(1, 0), DOWN))
        odd = add(Mlstm(norm))
        add(Project("odd_out", shift_of(1, 2), odd.wait_chunk))
        norm = add(Norm(scale_of(1, 4), shift_of(1, 3), OUT))
        add(FeedForward("ffn1", shift_of(1, 5), norm))
        norm = add(Norm(gain_of("ffn1_norm"), constant("zero"), DOWN))
        add(FeedForward("ffn2", constant("half"), norm))
        mix_tables_free = KC * updates[0]
        norm = add(Norm(gain_of("mix_norm"), constant("zero"), DOWN, root_at=22528))
        mix = add(Mix(norm))
        add(Project("mix_out", constant("one"), mix.wait_chunk))
        mem_free = KC * updates[0]
        norm = add(Norm(gain_of("mem_q_norm"), constant("zero"), OUT))
        memory = add(Memory(norm))
        add(Project("mem_out", constant("one"), memory.wait_chunk))
        norm = add(Norm(gain_of("ffn2_norm"), constant("zero"), OUT))
        add(FeedForward("ffn3", constant("half"), norm))
        n_units = N_UNITS
        final = add(Norm(gain_of("final_norm"), constant("zero"), DOWN, final=True))

        block = ctx.enter_context(nc.Block())

        @block.sync
        def _(sp):
            for dst, src in ((par, params), (tab, tables)):
                sp.dma_start(dst[:, :], src[:, :]).then_inc(setup_loaded, 16)
            sp.dma_start(x[:, :, :], xT[:, :, :]).then_inc(setup_loaded, 16)

            def load(n, at_unit, r):
                sp.dma_start(raw[:, r, :], stream[at_unit, :, :].rearrange("o p n -> p (o n)")).then_inc(landed[r], 16)

            for n in range(2):
                load(n, slice(n, n + 1), n)
            with sp.Fori(1, ADA_UNITS // 2) as i:
                for r in range(2):
                    sp.wait_ge(ada_used, 2 * i + r - 1)
                    load(r, bass.ds(2 * i + r, 1), r)
            for m in range(2):
                sp.wait_ge(ada_used, ADA_UNITS - 1 + m)
                load(m, slice(ADA_UNITS + m, ADA_UNITS + m + 1), m)
            with sp.Fori(1, n_units // 2) as i:
                for r in range(2):
                    sp.wait_ge(lo_split, 2 * i + r - 1)
                    load(r, bass.ds(2 * i + (ADA_UNITS + r), 1), r)
            for k in range(KC):
                sp.wait_ge(scaled, KC * final.n + k + 1)
                sp.dma_start(outT[:, k, :], final.t[:, k, :]).then_inc(stored, 16)
            sp.wait_ge(stored, 16 * KC)

        @block.gpsimd
        def _(pool):
            pool.dma_start(area(16384, 4 * S), even_tables[:, 0:4 * S]).then_inc(even_loaded, 16)
            pool.dma_start(area(18432, 2 * S), even_tables[:, 4 * S:6 * S]).then_inc(even_loaded, 16)
            pool.dma_start(area(19456, 4 * P), w_pool[:, :]).then_inc(even_loaded, 16)
            pool.wait_ge(x_ready, mix_tables_free)
            pool.dma_start(area(24064, MIX_TABLES), mix_tables[:, :]).then_inc(mix_loaded, 16)
            pool.wait_ge(x_ready, mem_free)
            pool.dma_start(area(8192, KC * N_MEM), memT[:, :]).then_inc(mem_loaded, 16)

        @block.scalar
        def _(act):
            st = Steps(act, sem("act_steps"))
            for stage in stages:
                stage.scalar(act, st)

        @block.vector
        def _(dve):
            st = Steps(dve, sem("dve_steps"))
            for stage in stages:
                stage.vector(dve, st)

        @block.tensor
        def _(pe):
            for stage in stages:
                stage.tensor(pe)


def columns(v):
    return np.asarray(v).reshape(-1, P).T


def in_units(w, cols=256):
    k, n = w.shape
    return w.reshape(k // P, P, n // cols, cols).transpose(2, 1, 0, 3).reshape(n // cols, P, -1)


def by_rows(w):
    return w.reshape(-1, 2, P, D).transpose(0, 2, 1, 3).reshape(-1, P, UNIT)


def ffn_units(w1, w3, w2):
    a, b = in_units(w1, P).reshape(FB, P, KC, P), in_units(w3, P).reshape(FB, P, KC, P)
    return [np.concatenate([a, b], axis=3).reshape(FB, P, UNIT), by_rows(w2)]


def build_stream(i):
    ada = i["ada_w"].reshape(2, KC, P, 3, UNIT).transpose(0, 3, 1, 2, 4).reshape(ADA_UNITS, P, UNIT)
    w = i["ev_w_in"][0]
    heads = w[:, 512:1024].reshape(D, 2, 4, 64).transpose(0, 2, 1, 3).reshape(D, 512)
    even = np.concatenate([w[:, 0:512], heads, w[:, 1024:]], axis=1)
    wo = i["ev_w_out"][0]
    even_out = np.concatenate([wo[0:512], wo[512:].reshape(2, 4, 64, D).transpose(1, 0, 2, 3).reshape(512, D)], axis=0)
    w = i["od_w_in"][0]
    gates = np.concatenate([w[:, 3072:], np.zeros((D, 224), w.dtype)], axis=1)
    odd = np.concatenate([gates, w[:, 0:3072]], axis=1)
    w = i["w_in_2"][0]
    q, f, rest = w[:, 0:512], w[:, 512:1024], w[:, 1024:]
    mix = np.concatenate([f, q, rest], axis=1)
    parts = [ada, in_units(even), in_units(even_out)]
    parts += ffn_units(i["ffn_w1"][0], i["ffn_w3"][0], i["ffn_w2"][0])
    parts += [in_units(odd), in_units(i["od_w_out"][0])]
    parts += ffn_units(i["ffn_w1"][1], i["ffn_w3"][1], i["ffn_w2"][1])
    gu = i["ffn1_w_gu_2"][0]
    parts += ffn_units(gu[:, :FF], gu[:, FF:], i["ffn1_w_down_2"][0])
    parts += [in_units(mix), in_units(i["w_out_2"][0]), in_units(i["mem_w_kv_2"][0]), in_units(i["mem_w_q_2"][0]),
              in_units(i["mem_w_o_2"][0])]
    gu = i["ffn2_w_gu_2"][0]
    parts += ffn_units(gu[:, :FF], gu[:, FF:], i["ffn2_w_down_2"][0])
    return np.ascontiguousarray(np.concatenate(parts, axis=0))


def build_params(i):
    f = np.float32
    gb = np.zeros((P, 2), f)
    g = i["od_gate_b"][0].reshape(2, 2, 8)
    for d in range(2):
        for kind in range(2):
            gb[32 * d:32 * d + 8, kind] = g[d, kind]
    twice = lambda v: np.concatenate([v, v]).reshape(P, 1)
    cols = [columns(i["c"]), columns(i["ada_b"]), columns(i["ev_b_pool"]), columns(i["ev_pool_scale"]),
            twice(i["ev_q_gain"][0]), twice(i["ev_k_gain"][0]), columns(i["od_conv_w"]), columns(i["od_conv_b"]),
            columns(i["od_head_gain"]), columns(i["ffn1_norm_2"]), columns(i["mix_norm_2"]),
            columns(i["mem_q_norm_2"]), columns(i["mem_kv_norm_2"]), columns(i["ffn2_norm_2"]),
            columns(i["final_norm_2"]), columns(i["hg_lb_raw_2"]), columns(i["hg_gnorm_2"]), columns(i["sb_gnorm_2"]),
            gb, np.full((P, 1), EPS, f), np.zeros((P, 1), f), np.ones((P, 1), f), np.full((P, 1), 0.5, f)]
    out = np.ascontiguousarray(np.concatenate(cols, axis=1))
    assert out.shape == (P, N_PARAMS)
    return out


def build_tables():
    f = np.float32
    a = np.arange(P)
    part, free = a[:, None], a[None, :]
    pair = np.zeros((P, 32), f)
    pair[:64, 15], pair[64:, 16] = 1, 1
    gi, gf = np.zeros((P, 40), f), np.zeros((P, 40), f)
    for d in range(2):
        for h in range(8):
            gi[16 * d + h, 32 * d + h] = 1
            gf[16 * d + 8 + h, 32 * d + h] = 1
    spread = np.concatenate([part == 2 * b + free // 64 for b in range(5)], axis=1)
    t = [np.eye(P), free == (part ^ 1), part >= free, part < free, np.where(part < free, 0, -BIG),
         np.where(free < part, BIG, 0), np.where(free > part, BIG, 0), np.ones((P, P)), pair, gi, gf, spread]
    tables = np.ascontiguousarray(np.concatenate([np.asarray(v, f) for v in t], axis=1))
    t = np.arange(S)
    counts = [1.0 / (np.clip(t + w - w // 2, 0, S) - np.clip(t - w // 2, 0, S)) for w in (2, 4, 8, 16)]
    inv_freq = (np.float32(10000.0) ** (-np.arange(16, dtype=f) / f(16))).astype(f)
    ang = np.concatenate([(t // 64).astype(f)[:, None] * inv_freq, (t % 64).astype(f)[:, None] * inv_freq], axis=1)
    ang = ang[:, (a % 64) // 2].T.astype(np.float64)
    sign = np.where(a % 2 == 0, -1.0, 1.0)[:, None]
    even = np.concatenate([np.tile(np.concatenate(counts)[None, :], (P, 1)), np.cos(ang), sign * np.sin(ang)], axis=1)
    masks = []
    for l in range(LEVELS):
        n = 1 << l
        masks.append((part // (2 * n) == free // (2 * n)) & (part % (2 * n) < n) & (free % (2 * n) >= n))
    masks.append(part == free)
    run = np.tile((np.arange(S) % P != 0)[None, :], (P, 1))
    mix = np.concatenate([np.asarray(m, f) for m in masks] + [run.astype(f)], axis=1)
    return tables, np.ascontiguousarray(even.astype(f)), np.ascontiguousarray(mix)


def kernel(**inputs):
    import concourse.bacc as _bacc
    from concourse.bass_utils import run_bass_kernel_spmd as _run

    i = {n: np.asarray(v) for n, v in inputs.items()}
    tables, even_tables, mix_tables = build_tables()
    arrays = {
        "xT": np.ascontiguousarray(i["x"][0].T.reshape(KC, P, S).transpose(1, 0, 2)),
        "memT": np.ascontiguousarray(i["mem_2"][0].T.reshape(KC, P, N_MEM).transpose(1, 0, 2).reshape(P, -1)),
        "stream": build_stream(i),
        "params": build_params(i),
        "tables": tables,
        "even_tables": even_tables,
        "mix_tables": mix_tables,
        "w_pool": np.ascontiguousarray(i["ev_w_pool"][0].transpose(1, 0, 2).reshape(P, -1)),
    }
    nc = _bacc.Bacc("TRN2", target_bir_lowering=False, num_devices=1)
    args = [nc.dram_tensor(n, a.shape, F32, kind="ExternalInput").ap() for n, a in arrays.items()]
    args.append(nc.dram_tensor("outT", (P, KC, S), F32, kind="ExternalOutput").ap())
    program(nc, *args)
    r = _run(nc, [arrays], core_ids=[0])
    out = r.results[0]["outT"]
    return np.ascontiguousarray(out.transpose(1, 0, 2).reshape(D, S).T)[None]
```

```python
from contextlib import ExitStack, contextmanager

import numpy as np

import concourse.bass as bass
from concourse import mybir

ALU = mybir.AluOpType
ACT = mybir.ActivationFunctionType
AX = mybir.AxisListType
F32 = mybir.dt.float32
F32R = mybir.dt.float32r
I32 = mybir.dt.int32

P = 128
D = 1024
S = 512
KC = D // P
TB = S // P
FF = 2816
FB = FF // P
N_MEM = 256
MB = N_MEM // P
UNIT = 2048
EPS = 1e-6
BIG = 1.0e30

ADA_UNITS = 2 * 3 * KC
ADA_FIRST = KC
ADA_REST = ADA_UNITS - ADA_FIRST
FFN_UNITS = FB + FB // 2

PLAN = [("even_in", 5), ("even_out", 4), ("ffn0", FFN_UNITS), ("odd_in", 13), ("odd_out", 4),
        ("ffn1", FFN_UNITS), ("ffn2", FFN_UNITS), ("mix_in", 14), ("mix_out", 4), ("mem_kv", 8), ("mem_q", 4),
        ("mem_out", 4), ("ffn3", FFN_UNITS)]
FIRST_UNIT = {}
_m = 0
for _name, _n in PLAN:
    FIRST_UNIT[_name] = _m
    _m += _n
N_UNITS = _m

PARAMS = [("c", 8), ("ada_b", 96), ("b_pool", 4), ("pool_scale", 4), ("q_gain", 1), ("k_gain", 1), ("conv_w", 40),
          ("conv_b", 8), ("head_gain", 8), ("ffn1_norm", 8), ("mix_norm", 8), ("mem_q_norm", 8),
          ("mem_kv_norm", 8), ("ffn2_norm", 8), ("final_norm", 8), ("lb_raw0", 4), ("lb_raw1", 4),
          ("hg_gnorm", 4), ("sb_gnorm", 4), ("gate_b_i", 1), ("gate_b_f", 1), ("eps", 1), ("zero", 1),
          ("one", 1), ("half", 1)]
PCOL = {}
_m = 0
for _name, _n in PARAMS:
    PCOL[_name] = _m
    _m += _n
N_PARAMS = _m

TABLES = [("ident", 128), ("swap", 128), ("tri", 128), ("strict", 128), ("neg_strict", 128), ("hide_fwd", 128),
          ("hide_bwd", 128), ("ones", 128), ("pair_rows", 32), ("gate_i", 40), ("gate_f", 40),
          ("pair_spread", 5 * 128)]
TCOL = {}
_m = 0
for _name, _n in TABLES:
    TCOL[_name] = _m
    _m += _n
N_TABLES = _m
EVEN_TABLES = 4 * S + 2 * S
LEVELS = 7
MIX_TABLES = (LEVELS + 1) * P + S


class Steps:

    def __init__(self, eng, sem):
        self.eng, self.sem, self.n, self.loop = eng, sem, 0, 0

    def add(self, ins):
        ins.then_inc(self.sem, 1)
        self.n += 1

    def settle(self):
        self.eng.wait_ge(self.sem, self.loop + self.n)

    def link(self, ins):
        self.add(ins)
        self.settle()


def program(nc, xT, memT, stream, params, tables, even_tables, mix_tables, w_pool, outT):
    ctx = ExitStack()
    with ctx:
        at = [16512]

        def place(name, shape, dt=F32, offset=None):
            if offset is None:
                offset = at[0]
                at[0] += -(-int(np.prod(shape[1:])) * 4 // 32) * 32
            return nc.alloc_sbuf_tensor_at(name, shape, dt, offset=offset)

        x = place("x", [P, KC, S])
        h_hi = place("h_hi", [P, KC, S], F32R)
        h_lo = place("h_lo", [P, KC, S], F32R)
        raw = place("raw", [P, 2, UNIT])
        w_hi = place("w_hi", [P, 2, UNIT], F32R)
        w_lo = place("w_lo", [P, 2, UNIT], F32R)
        par = place("par", [P, N_PARAMS])
        tab = place("tab", [P, N_TABLES])
        mod = place("mod", [P, 96])
        mod1 = place("mod1", [P, 96])
        cond = place("cond", [P, KC])
        small = place("small", [P, 512])
        WORK = 25600
        work_at = at[0]
        work = place("work", [P, WORK])
        assert at[0] <= nc.sbuf_usable_end, at[0]

        def area(start, *shape):
            n = int(np.prod(shape))
            assert start + n <= WORK, (start, shape)
            v = work[:, start:start + n]
            if len(shape) == 2:
                v = v.rearrange("p (a b) -> p a b", a=shape[0])
            if len(shape) == 3:
                v = v.rearrange("p (a b c) -> p a b c", a=shape[0], b=shape[1])
            return v

        g_hi = place("g_hi", [P, FB, S], F32R, offset=work_at)
        g_lo = place("g_lo", [P, FB, S], F32R, offset=work_at + FB * S * 4)
        mem_hi = place("mem_hi", [P, KC, N_MEM], F32R, offset=work_at + 19456 * 4)
        mem_lo = place("mem_lo", [P, KC, N_MEM], F32R, offset=work_at + 21504 * 4)
        bank = ctx.enter_context(nc.psum_tensor("bank", [P, 8, 512], F32))

        def col(name, i=0):
            return par[:, PCOL[name] + i:PCOL[name] + i + 1]

        def table(name):
            n = dict(TABLES)[name]
            return tab[:, TCOL[name]:TCOL[name] + n]

        ident, ones = table("ident"), table("ones")
        eps = col("eps")

        sems = {}

        def sem(name):
            assert name not in sems, name
            sems[name] = ctx.enter_context(nc.semaphore(name))
            return sems[name]

        setup_loaded = sem("setup_loaded")
        x_loaded = sem("x_loaded")
        even_loaded = sem("even_loaded")
        mix_loaded = sem("mix_loaded")
        mem_loaded = sem("mem_loaded")
        landed = [sem("landed0"), sem("landed1")]
        ada_used = sem("ada_used")
        hi_split = sem("hi_split")
        lo_split = sem("lo_split")
        unit_used = sem("unit_used")
        x_ready = sem("x_ready")
        stored = sem("stored")

        def slot(m):
            return m % 2

        def place_of(m):
            return m + (ADA_FIRST if m < FIRST_UNIT["even_out"] else ADA_UNITS)

        def place_of_ada(n):
            return n + (0 if n < ADA_FIRST else FIRST_UNIT["even_out"])

        def split_hi(act, m, i=0):
            act.wait_ge(landed[slot(m)], 16 * (place_of(m) // 2 + 1) + 16 * i)
            if m >= 2:
                act.wait_ge(unit_used, m - 1 + 2 * i)
            nc.scalar.activation(w_hi[:, slot(m), :], raw[:, slot(m), :], ACT.Copy).then_inc(hi_split, 1)

        def split_lo(dve, m, i=0):
            dve.wait_ge(hi_split, m + 1 + 2 * i)
            nc.vector.tensor_tensor(w_lo[:, slot(m), :], raw[:, slot(m), :], w_hi[:, slot(m), :],
                                    ALU.subtract).then_inc(lo_split, 1)

        def split_next_hi(act, m, i=0):
            if m + 2 < n_units:
                split_hi(act, m + 2, i)

        def split_next_lo(dve, m, i=0):
            if m + 2 < n_units:
                split_lo(dve, m + 2, i)

        def three_passes(out, stationary, moving, first, last):
            nc.tensor.matmul(out, stationary[0], moving[0], start=first, stop=False)
            nc.tensor.matmul(out, stationary[0], moving[1], start=False, stop=False)
            return nc.tensor.matmul(out, stationary[1], moving[0], start=False, stop=last)

        def unit_cols(m):
            return [w[:, slot(m), :].rearrange("p (k n) -> p k n", k=KC) for w in (w_hi, w_lo)]

        def features(pe, m, block, out, wait_chunk=None, src=None, i=0):
            hh, hl = src or (h_hi, h_lo)
            wh, wl = unit_cols(m)
            c0 = block * P
            for k in range(KC):
                if wait_chunk:
                    wait_chunk(pe, k)
                last = three_passes(out, (wh[:, k, c0:c0 + P], wl[:, k, c0:c0 + P]), (hh[:, k, :], hl[:, k, :]),
                                    k == 0, k == KC - 1)
            return last

        def both_features(pe, m, out, wait_chunk):
            wh, wl = unit_cols(m)
            for k in range(KC):
                wait_chunk(pe, k)
                for b in range(2):
                    r = slice(b * P, b * P + P)
                    last = three_passes(out[:, b, :], (wh[:, k, r], wl[:, k, r]), (h_hi[:, k, :], h_lo[:, k, :]),
                                        k == 0, k == KC - 1)
            return last

        def tokens(pe, m, out, blocks=TB, c0=0, n=256, src=None):
            hh, hl = src or (h_hi, h_lo)
            wh, wl = unit_cols(m)
            for t in range(blocks):
                r = slice(t * P, t * P + P)
                for k in range(KC):
                    last = three_passes(out[:, t, :], (hh[:, k, r], hl[:, k, r]),
                                        (wh[:, k, c0:c0 + n], wl[:, k, c0:c0 + n]), k == 0, k == KC - 1)
            return last

        def two_banks(m, blocks=TB, n=256):
            b = 2 * slot(m)
            return bank[:, b:b + 2, :].rearrange("p a n -> p (a n)")[:, 0:blocks * n].rearrange(
                "p (t n) -> p t n", t=blocks)

        class Conditioning:
            silu_done = sem("cond_silu")
            summed = sem("ada_summed")
            mod_done = sem("mod_done")
            first_acc, acc = area(8192, UNIT), area(0, 2, UNIT)

            def acc_of(self, q):
                return self.acc[:, q % 2, :] if q else self.first_acc

            def bank_of(self, q):
                return 3 if q else 0

            def scalar(self, act, st):
                act.wait_ge(setup_loaded, 32)
                nc.scalar.activation(cond[:, :], par[:, PCOL["c"]:PCOL["c"] + KC], ACT.Silu).then_inc(self.silu_done, 1)
                for k in range(KC):
                    self.norm.square(act, k)
                split_hi(act, 0)
                split_hi(act, 1)

            def add_unit(self, dve, n):
                q, k, place = n // KC, n % KC, place_of_ada(n)
                acc, rows = self.acc_of(q), raw[:, place % 2, :]
                dve.wait_ge(landed[place % 2], 16 * (place // 2 + 1))
                if k == 0:
                    if q >= 3:
                        dve.wait_ge(self.summed, q - 1)
                    ins = nc.vector.tensor_scalar(acc, rows, cond[:, k:k + 1], None, ALU.mult)
                else:
                    dve.wait_ge(ada_used, n)
                    ins = nc.vector.scalar_tensor_tensor(acc, rows, cond[:, k:k + 1], acc, ALU.mult, ALU.add)
                ins.then_inc(ada_used, 1)

            def write_mod(self, dve, st, q0, q1):
                dve.wait_ge(self.summed, q1)
                c = slice(16 * q0, 16 * q1)
                st.link(nc.vector.tensor_tensor(mod[:, c], bank[:, self.bank_of(q0), c],
                                                par[:, PCOL["ada_b"] + 16 * q0:PCOL["ada_b"] + 16 * q1], ALU.add))
                st.link(nc.vector.tensor_scalar(mod1[:, c], mod[:, c], 1.0, None, ALU.add))

            def vector(self, dve, st):
                dve.wait_ge(setup_loaded, 32)
                dve.wait_ge(self.silu_done, 1)
                for n in range(ADA_FIRST):
                    self.add_unit(dve, n)
                    if n >= 2:
                        self.norm.add_square(dve, n - 1)
                split_lo(dve, 0)
                split_lo(dve, 1)
                self.write_mod(dve, st, 0, 1)
                dve.sem_inc(self.mod_done, 1)

            def sum_rows(self, pe, q):
                pe.wait_ge(ada_used, KC * (q + 1))
                for b in range(16):
                    last = nc.tensor.matmul(bank[:, self.bank_of(q), 16 * q + b:16 * q + b + 1],
                                            self.acc_of(q)[:, b * P:b * P + P], ones[:, 0:1], start=True, stop=True)
                last.then_inc(self.summed, 1)

            def tensor(self, pe):
                pe.wait_ge(setup_loaded, 32)
                self.sum_rows(pe, 0)

        def mod_steps(steps):
            units = [[] for _ in range(steps)]
            thirds = [[] for _ in range(steps + 2)]
            for j in range(ADA_REST):
                s = j * steps // ADA_REST
                units[s].append(ADA_FIRST + j)
                if (ADA_FIRST + j) % KC == KC - 1:
                    thirds[s + 2].append((ADA_FIRST + j) // KC)
            return units, thirds

        norms = [0]
        updates = [0]
        sq_done = sem("sq_done")
        sq_added = sem("sq_added")
        ms_done = sem("ms_done")
        root_done = sem("root_done")
        inv_done = sem("inv_done")
        row_done = sem("row_done")
        scaled = sem("scaled")
        h_hi_done = sem("h_hi_done")
        h_ready = sem("h_ready")

        class Norm:
            ROW = 6
            root, inv = small[:, 480:480 + TB], small[:, 484:484 + TB]

            def __init__(self, scale, shift, free_bank, before=None, final=False, late=True):
                self.n, self.scale, self.shift, self.bank, self.final = norms[0], scale, shift, free_bank, final
                self.version = updates[0]
                self.late = before.last_unit if before and late else None
                if before:
                    before.after = self
                norms[0] += 1
                self.sq, self.t = area(0, KC, S), area(4096, KC, S)

            def wait_x(self, eng, k):
                if self.version == 0:
                    eng.wait_ge(x_loaded, 16)
                else:
                    eng.wait_ge(x_ready, KC * (self.version - 1) + k + 1)

            def wait_chunk(self, eng, k):
                eng.wait_ge(h_ready, KC * self.n + k + 1)

            def square(self, act, k):
                if k == 4:
                    act.preload_act_table_set("sqrt_and_others")
                self.wait_x(act, k)
                nc.scalar.activation(self.sq[:, k, :], x[:, k, :], ACT.Square).then_inc(sq_done, 1)

            def add_square(self, dve, k):
                dve.wait_ge(sq_done, KC * self.n + k + 1)
                if k > 1:
                    dve.wait_ge(sq_added, (KC - 1) * self.n + k - 1)
                nc.vector.tensor_tensor(self.sq[:, 0, :], self.sq[:, 0, :], self.sq[:, k, :],
                                        ALU.add).then_inc(sq_added, 1)

            def take_root(self, act):
                act.wait_ge(ms_done, self.n + 1)
                nc.scalar.activation(self.root, bank[:, self.bank, 0:TB], ACT.Sqrt, bias=eps,
                                     scale=1.0 / D).then_inc(root_done, 1)

            def take_inverse(self, dve):
                dve.wait_ge(root_done, self.n + 1)
                nc.vector.reciprocal(self.inv, self.root).then_inc(inv_done, 1)

            def scale_chunk(self, dve, k):
                if k == 0:
                    self.wait_x(dve, KC - 1)
                    dve.wait_ge(row_done, self.n + 1)
                nc.vector.scalar_tensor_tensor(self.t[:, k, :], x[:, k, :], self.scale(k), bank[:, self.ROW, :],
                                               ALU.mult, ALU.mult).then_inc(scaled, 1)

            def high(self, act, k):
                act.wait_ge(scaled, KC * self.n + k + 1)
                nc.scalar.activation(h_hi[:, k, :], self.t[:, k, :], ACT.Identity,
                                     bias=self.shift(k)).then_inc(h_hi_done, 1)

            def low(self, dve, k):
                dve.wait_ge(h_hi_done, KC * self.n + k + 1)
                nc.vector.scalar_tensor_tensor(h_lo[:, k, :], self.t[:, k, :], self.shift(k), h_hi[:, k, :],
                                               ALU.add, ALU.subtract).then_inc(h_ready, 1)

            def sum_features(self, pe):
                pe.wait_ge(sq_added, (KC - 1) * (self.n + 1))
                for t in range(TB):
                    last = nc.tensor.matmul(bank[:, self.bank, t:t + 1], self.sq[:, 0, t * P:t * P + P],
                                            ones[:, 0:1], start=True, stop=True)
                last.then_inc(ms_done, 1)

            def spread_row(self, pe):
                pe.wait_ge(inv_done, self.n + 1)
                for t in range(TB):
                    last = nc.tensor.matmul(bank[:, self.ROW, t * P:t * P + P],
                                            self.inv[:, t:t + 1].to_broadcast([P, P]), ident, start=True, stop=True)
                last.then_inc(row_done, 1)

            def scalar(self, act, st):
                self.take_root(act)
                if self.final:
                    return
                for k in range(KC):
                    self.high(act, k)
                    if k == 2 and self.late is not None:
                        split_next_hi(act, self.late)

            def vector(self, dve, st):
                self.add_square(dve, KC - 1)
                self.take_inverse(dve)
                for k in range(KC):
                    self.scale_chunk(dve, k)
                    if k and not self.final:
                        self.low(dve, k - 1)
                if not self.final:
                    self.low(dve, KC - 1)
                    if self.late is not None:
                        split_next_lo(dve, self.late)

            def tensor(self, pe):
                self.sum_features(pe)
                self.spread_row(pe)

        class Project:

            def __init__(self, name, gate, wait_chunk, during=None):
                self.during = during
                self.m0, self.gate, self.wait_chunk = FIRST_UNIT[name], gate, wait_chunk
                self.base = KC * updates[0]
                updates[0] += 1
                self.last_unit, self.after = self.m0 + 3, None

            def scalar(self, act, st):
                for u in range(4):
                    if self.during:
                        self.during.prepare_scalar(act, u)
                    if u < 3:
                        split_next_hi(act, self.m0 + u)
                    for b in range(2):
                        self.after.square(act, 2 * u + b)
                if self.after.late is None:
                    split_next_hi(act, self.last_unit)

            def vector(self, dve, st):
                for u in range(4):
                    m = self.m0 + u
                    if self.during:
                        self.during.prepare_vector(dve, st, u)
                    if u:
                        for k in range(max(1, 2 * u - 2), 2 * u):
                            self.after.add_square(dve, k)
                    dve.wait_ge(unit_used, m + 1)
                    for b in range(2):
                        o = 2 * u + b
                        nc.vector.scalar_tensor_tensor(x[:, o, :], bank[:, 2 * slot(m) + b, :], self.gate(o),
                                                       x[:, o, :], ALU.mult, ALU.add).then_inc(x_ready, 1)
                    if u < 3:
                        split_next_lo(dve, m)
                self.after.add_square(dve, KC - 2)
                if self.after.late is None:
                    self.after.add_square(dve, KC - 1)
                    split_next_lo(dve, self.last_unit)

            def tensor(self, pe):
                for u in range(4):
                    m = self.m0 + u
                    pe.wait_ge(lo_split, m + 1)
                    if u >= 2:
                        pe.wait_ge(x_ready, self.base + 2 * (u - 1))
                    if u == 0:
                        last = both_features(pe, m, bank[:, 2 * slot(m):2 * slot(m) + 2, :], self.wait_chunk)
                    else:
                        for b in range(2):
                            last = features(pe, m, b, bank[:, 2 * slot(m) + b, :])
                    last.then_inc(unit_used, 1)
                    if self.during:
                        self.during.prepare_tensor(pe, u)

        ffns = [0]
        silu_done = sem("silu_done")
        gated = sem("gated")
        g_hi_done = sem("g_hi_done")
        g_ready = sem("g_ready")
        down_block = sem("down_block")

        class FeedForward:
            silu, gu = area(2 * FB * S, 2, S), area(2 * FB * S + 2 * S, 2, S)

            def __init__(self, name, gate, norm):
                self.m0, self.gate, self.norm = FIRST_UNIT[name], gate, norm
                self.md = self.m0 + FB
                self.j0 = FB * ffns[0]
                self.f = ffns[0]
                ffns[0] += 1
                self.base = KC * updates[0]
                updates[0] += 1
                self.last_unit, self.after = self.md + 10, None

            def scalar(self, act, st):
                def block(r, i):
                    m, b = self.m0 + r, 2 * slot(self.m0 + r)
                    act.wait_ge(unit_used, m + 1 + 2 * i)
                    nc.scalar.activation(self.silu[:, r, :], bank[:, b, :], ACT.Silu).then_inc(silu_done, 1)
                    act.wait_ge(gated, self.j0 + r + 1 + 2 * i)
                    nc.scalar.activation(g_hi[:, bass.ds(2 * i + r, 1), :], self.gu[:, r:r + 1, :],
                                         ACT.Copy).then_inc(g_hi_done, 1)
                    split_next_hi(act, m, i)

                with act.Fori(0, FB // 2) as i:
                    block(0, i)
                    block(1, i)

                def rows(d, i):
                    act.wait_ge(unit_used, self.md + d + 1 + 2 * i)
                    split_next_hi(act, self.md + d, i)

                rows(0, 0)
                with act.Fori(0, 4) as i:
                    rows(1, i)
                    rows(2, i)
                rows(9, 0)
                for k in range(KC):
                    self.after.square(act, k)

            def vector(self, dve, st):
                def block(r, i):
                    m, b = self.m0 + r, 2 * slot(self.m0 + r)
                    dve.wait_ge(silu_done, self.j0 + r + 1 + 2 * i)
                    nc.vector.tensor_tensor(self.gu[:, r, :], self.silu[:, r, :], bank[:, b + 1, :],
                                            ALU.mult).then_inc(gated, 1)
                    dve.wait_ge(g_hi_done, self.j0 + r + 1 + 2 * i)
                    nc.vector.tensor_tensor(g_lo[:, bass.ds(2 * i + r, 1), :], self.gu[:, r:r + 1, :],
                                            g_hi[:, bass.ds(2 * i + r, 1), :], ALU.subtract).then_inc(g_ready, 1)
                    split_next_lo(dve, m, i)

                with dve.Fori(0, FB // 2) as i:
                    block(0, i)
                    block(1, i)
                split_next_lo(dve, self.md)
                with dve.Fori(0, 4) as i:
                    split_next_lo(dve, self.md + 1, i)
                    split_next_lo(dve, self.md + 2, i)
                split_next_lo(dve, self.md + 9)
                for o in range(KC):
                    if o < KC - 1:
                        dve.wait_ge(down_block, (KC - 1) * self.f + o + 1)
                    else:
                        dve.wait_ge(unit_used, self.md + 11)
                    nc.vector.scalar_tensor_tensor(x[:, o, :], bank[:, o, :], self.gate(o), x[:, o, :],
                                                   ALU.mult, ALU.add).then_inc(x_ready, 1)
                    if o >= 2:
                        self.after.add_square(dve, o - 1)

            def tensor(self, pe):
                def block(r, i, first=False):
                    m = self.m0 + r
                    pe.wait_ge(lo_split, m + 1 + 2 * i)
                    if not first:
                        pe.wait_ge(gated, self.j0 + r - 1 + 2 * i)
                    if first and r == 0:
                        last = both_features(pe, m, bank[:, 2 * slot(m):2 * slot(m) + 2, :], self.norm.wait_chunk)
                    else:
                        for b in range(2):
                            last = features(pe, m, b, bank[:, 2 * slot(m) + b, :])
                    last.then_inc(unit_used, 1)

                block(0, 0, True)
                block(1, 0, True)
                with pe.Fori(1, FB // 2) as i:
                    block(0, i)
                    block(1, i)

                def rows(d, i, first=False, end=False):
                    m = self.md + d
                    wh, wl = (w[:, slot(m), :].rearrange("p (k n) -> p k n", k=2) for w in (w_hi, w_lo))
                    pe.wait_ge(lo_split, m + 1 + 2 * i)
                    order = [(k, o) for k in range(2) for o in range(KC)]
                    early, late = 2 * slot(self.md), 2 * slot(self.md + 1)
                    if first:
                        banks = (4, 5, 6, 7, early, early + 1, late, late + 1)
                        order = [(k, o) for k in range(2) for o in banks]
                    if end:
                        order = [(k, o) for o in range(KC) for k in range(2)]
                    for k, o in order:
                        if first and k == 0 and o == early:
                            pe.wait_ge(gated, self.j0 + FB - 1)
                        if first and k == 0 and o == late:
                            pe.wait_ge(gated, self.j0 + FB)
                        c = bass.ds(2 * d + k + 4 * i, 1)
                        r = slice(o * P, o * P + P)
                        last = three_passes(bank[:, o, :], (wh[:, k, r], wl[:, k, r]),
                                            (g_hi[:, c, :], g_lo[:, c, :]), first and k == 0, end and k == 1)
                        if end and k == 1 and o < KC - 1:
                            last.then_inc(down_block, 1)
                    last.then_inc(unit_used, 1)

                pe.wait_ge(g_ready, self.j0 + 2)
                rows(0, 0, first=True)
                pe.wait_ge(g_ready, self.j0 + FB)
                with pe.Fori(0, 4) as i:
                    rows(1, i)
                    rows(2, i)
                rows(9, 0)
                rows(10, 0, end=True)

        class ToFeatures:

            def __init__(self, name, rows, first, n, group=None, junk=None, gate=None, gain=None, banks=(4, 5),
                         ready=None, cols=0):
                self.rows, self.first, self.n, self.group, self.junk = rows, first, n, group, junk
                self.gate, self.gain, self.banks, self.ready = gate, gain, banks, ready
                self.groups = n * P // group if group else 0
                self.per_chunk = P // group if group else 0
                self.sq = sem(name + "_sq")
                self.gated = sem(name + "_gated")
                self.root = sem(name + "_root")
                self.rows_ready = sem(name + "_rows_ready")
                self.turned = sem(name + "_turned")
                self.hi = sem(name + "_hi")
                self.lo = sem(name + "_lo")
                count = TB * self.groups
                self.sums, self.roots, self.inv = (small[:, cols + a:cols + a + count] for a in (0, 64, 128))

            def group_squares(self, act, st, g):
                self.ready(act, g)
                if g:
                    act.wait_ge(self.sq, g)
                for t in range(TB):
                    c = t * self.groups + g
                    ins = nc.scalar.activation(self.junk[:, 0:self.group],
                                               self.rows[:, t, g * self.group:(g + 1) * self.group], ACT.Square,
                                               accum_out=self.sums[:, c:c + 1])
                    if t < TB - 1:
                        st.link(ins)
                    else:
                        ins.then_inc(self.sq, 1)

            def take_roots(self, act):
                act.wait_ge(self.sq, self.groups)
                nc.scalar.activation(self.roots, self.sums, ACT.Sqrt, bias=eps, scale=1.0 / self.group).then_inc(
                    self.root, 1)

            def gate_rows(self, dve, b):
                dve.wait_ge(self.sq, self.per_chunk * (b + 1))
                c = slice(b * P, b * P + P)
                nc.vector.tensor_tensor(self.rows[:, :, c], self.rows[:, :, c], self.gate[:, :, c],
                                        ALU.mult).then_inc(self.gated, 1)

            def take_inverses(self, dve, st):
                dve.wait_ge(self.root, 1)
                st.link(nc.vector.reciprocal(self.inv, self.roots))

            def scale_rows(self, dve, b):
                if self.gate is not None:
                    dve.wait_ge(self.gated, b + 1)
                for a in range(self.per_chunk):
                    g = self.per_chunk * b + a
                    c = slice(g * self.group, (g + 1) * self.group)
                    inv = self.inv.rearrange("p (t g) -> p t g", t=TB)[:, :, g:g + 1]
                    nc.vector.tensor_tensor(self.rows[:, :, c], self.rows[:, :, c],
                                            inv.to_broadcast([P, TB, self.group]), ALU.mult).then_inc(
                                                self.rows_ready, 1)

            def high(self, act, b):
                act.wait_ge(self.turned, b + 1)
                out, src = h_hi[:, self.first + b, :], bank[:, self.banks[b % 2], :]
                if self.gain:
                    ins = nc.scalar.activation(out, src, ACT.Identity, bias=0.0, scale=self.gain(b))
                else:
                    ins = nc.scalar.activation(out, src, ACT.Copy)
                ins.then_inc(self.hi, 1)

            def low(self, dve, b):
                dve.wait_ge(self.hi, b + 1)
                out, src, hi = (h_lo[:, self.first + b, :], bank[:, self.banks[b % 2], :],
                                h_hi[:, self.first + b, :])
                if self.gain:
                    ins = nc.vector.scalar_tensor_tensor(out, src, self.gain(b), hi, ALU.mult, ALU.subtract)
                else:
                    ins = nc.vector.tensor_tensor(out, src, hi, ALU.subtract)
                ins.then_inc(self.lo, 1)

            def turn(self, pe, b):
                if self.group:
                    pe.wait_ge(self.rows_ready, self.per_chunk * (b + 1))
                else:
                    self.ready(pe)
                if b >= 2:
                    pe.wait_ge(self.lo, b - 1)
                for t in range(TB):
                    last = nc.tensor.transpose(bank[:, self.banks[b % 2], t * P:t * P + P],
                                               self.rows[:, t, b * P:b * P + P], ident)
                last.then_inc(self.turned, 1)

            def scalar(self, act, st):
                if self.group:
                    self.take_roots(act)
                for b in range(self.n):
                    self.high(act, b)

            def vector(self, dve, st):
                if self.group:
                    self.take_inverses(dve, st)
                    for b in range(2):
                        self.scale_rows(dve, b)
                for b in range(self.n):
                    if self.group and b + 2 < self.n:
                        self.scale_rows(dve, b + 2)
                    self.low(dve, b)

            def tensor(self, pe):
                for b in range(2):
                    self.turn(pe, b)

            def wait_chunk(self, pe, k):
                b = k - self.first
                if 0 <= b < self.n:
                    pe.wait_ge(self.lo, b + 1)
                    if b + 2 < self.n:
                        self.turn(pe, b + 2)

        class Softmax:

            def __init__(self, name, n, keys, scale, scores, values, out, n_out, p, pt, ready,
                         also_vector=None, also_tensor=None):
                self.also_vector, self.also_tensor = also_vector, also_tensor
                self.n, self.keys, self.scale, self.scores, self.values, self.out = n, keys, scale, scores, values, out
                self.n_out, self.p, self.pt, self.ready = n_out, p, pt, ready
                (self.scored, self.max_done, self.p_done, self.turned, self.pt_done, self.summed,
                 self.out_done) = (sem(name + s) for s in ("_scored", "_max_done", "_p_done", "_turned", "_pt_done",
                                                           "_summed", "_out_done"))
                self.mx, self.nm, self.rs, self.rc = (small[:, 192 + 32 * a:224 + 32 * a] for a in range(4))

            def tensor(self, pe):
                self.ready(pe)
                for s in range(self.n + 2):
                    if s < self.n:
                        if s >= 2:
                            pe.wait_ge(self.p_done, s - 1)
                        pairs = self.scores(s)
                        for a, (q, k) in enumerate(pairs):
                            last = nc.tensor.matmul(bank[:, 4 + s % 2, 0:self.keys], q, k, start=(a == 0),
                                                    stop=(a == len(pairs) - 1))
                        last.then_inc(self.scored, 1)
                    t = s - 1
                    if 0 <= t < self.n:
                        pe.wait_ge(self.p_done, t + 1)
                        if t >= 2:
                            pe.wait_ge(self.pt_done, t - 1)
                        for k in range(self.keys // P):
                            last = nc.tensor.transpose(bank[:, 6 + t % 2, k * P:k * P + P],
                                                       self.p[:, t % 2, k * P:k * P + P], ident)
                        last.then_inc(self.turned, 1)
                    t = s - 2
                    if 0 <= t < self.n:
                        pe.wait_ge(self.pt_done, t + 1)
                        if t >= 2:
                            pe.wait_ge(self.out_done, t - 1)
                        for k in range(self.keys // P):
                            last = nc.tensor.matmul(bank[:, t % 2, 0:self.n_out], self.pt[:, t % 2, k * P:k * P + P],
                                                    self.values(t, k), start=(k == 0),
                                                    stop=(k == self.keys // P - 1))
                        last.then_inc(self.summed, 1)
                    if self.also_tensor:
                        self.also_tensor(pe, s)

            def vector(self, dve, st):
                for s in range(self.n + 2):
                    if s < self.n:
                        dve.wait_ge(self.scored, s + 1)
                        st.link(nc.vector.tensor_reduce(self.mx[:, s:s + 1], bank[:, 4 + s % 2, 0:self.keys], AX.X,
                                                        ALU.max))
                        nc.vector.tensor_scalar(self.nm[:, s:s + 1], self.mx[:, s:s + 1], -self.scale, None,
                                                ALU.mult).then_inc(self.max_done, 1)
                        if self.also_vector:
                            self.also_vector(dve, s)
                    t = s - 2
                    if t >= 0:
                        dve.wait_ge(self.summed, t + 1)
                        st.link(nc.vector.reciprocal(self.rc[:, t:t + 1], self.rs[:, t:t + 1]))
                        nc.vector.tensor_scalar(self.out(t), bank[:, t % 2, 0:self.n_out], self.rc[:, t:t + 1], None,
                                                ALU.mult).then_inc(self.out_done, 1)

            def scalar(self, act, st):
                for s in range(self.n + 1):
                    if s < self.n:
                        act.wait_ge(self.max_done, s + 1)
                        if s >= 2:
                            act.wait_ge(self.turned, s - 1)
                        nc.scalar.activation(self.p[:, s % 2, :], bank[:, 4 + s % 2, 0:self.keys], ACT.Exp,
                                             bias=self.nm[:, s:s + 1], scale=self.scale,
                                             accum_out=self.rs[:, s:s + 1]).then_inc(self.p_done, 1)
                    t = s - 1
                    if t >= 0:
                        act.wait_ge(self.turned, t + 1)
                        if t >= 2:
                            act.wait_ge(self.summed, t - 1)
                        nc.scalar.activation(self.pt[:, t % 2, :], bank[:, 6 + t % 2, 0:self.keys],
                                             ACT.Copy).then_inc(self.pt_done, 1)

        class Even:
            PAD = 8
            W = S + 2 * PAD
            u = area(0, 4, W)
            sums = area(4 * W, 2, W)
            pooled = area(6 * W, 4, S)
            mixed = area(6 * W + 4 * S, 4, S)
            qk = area(8192, 5, S)
            v = area(10752, TB, P)
            sq = area(11264, 5, S)
            qn = area(13824, 5, S)
            counts, cos, sin, wp = (area(16384, 4, S), area(18432, S), area(18944, S), area(19456, 4, P))
            inv, t = area(19968, S), area(20480, 2, S)
            p, pt = area(21504, 2, S), area(22528, 2, S)
            out = area(23552, TB, 4 * P)

            def __init__(self, norm):
                self.norm, self.m0 = norm, FIRST_UNIT["even_in"]
                self.evac = sem("even_evac")
                self.padded = sem("even_padded")
                self.pool_ready, self.pool_mm, self.pool_out = sem("pool_ready"), sem("pool_mm"), sem("pool_out")
                self.mix_hi, self.mix_lo = sem("pool_hi"), sem("pool_lo")
                self.sq_done, self.ms_mm, self.rooted = sem("qk_sq"), sem("qk_ms"), sem("qk_root")
                self.inv_done, self.spread = sem("qk_inv"), sem("qk_spread")
                self.normed, self.swapped, self.turned = sem("qk_normed"), sem("qk_swapped"), sem("qk_rope")

                def scores(s):
                    head, t = s // TB, s % TB
                    b, half = head // 2, slice(64 * (head % 2), 64 * (head % 2) + 64)
                    return [(self.qk[half, b, t * P:t * P + P], self.qk[half, 4, :])]

                def values(s, k):
                    half = 64 * ((s // TB) % 2)
                    return self.v[:, k, half:half + 64]

                def out(s):
                    head, t = s // TB, s % TB
                    return self.out[:, t, head * 64:head * 64 + 64]

                self.softmax = Softmax("even", 8 * TB, S, 64 ** -0.5, scores, values, out, 64, self.p, self.pt,
                                       lambda pe: pe.wait_ge(self.turned, 5), self.add_units, self.sum_thirds)
                self.units, self.thirds = mod_steps(8 * TB)
                self.tail = ToFeatures("even_rows", self.out, 4, 4,
                                       ready=lambda pe: pe.wait_ge(self.softmax.out_done, 8 * TB))

            def add_units(self, dve, s):
                for n in self.units[s]:
                    conditioning.add_unit(dve, n)

            def sum_thirds(self, pe, s):
                for q in self.thirds[s]:
                    conditioning.sum_rows(pe, q)

            def wait_chunk(self, eng, k):
                if k < 4:
                    eng.wait_ge(self.mix_lo, k + 1)
                else:
                    self.tail.wait_chunk(eng, k)

            def scalar(self, act, st):
                for u in range(5):
                    m, b = self.m0 + u, 2 * slot(self.m0 + u)
                    act.wait_ge(unit_used, m + 1)
                    if u < 2:
                        for r in range(2):
                            ins = nc.scalar.activation(self.u[:, 2 * u + r, self.PAD:self.PAD + S], bank[:, b + r, :],
                                                       ACT.Copy)
                            ins.then_inc(self.evac, 1)
                    elif u < 4:
                        for r in range(2):
                            nc.scalar.activation(self.qk[:, 2 * (u - 2) + r, :], bank[:, b + r, :],
                                                 ACT.Copy).then_inc(self.evac, 1)
                    else:
                        nc.scalar.activation(self.qk[:, 4, :], bank[:, b, :], ACT.Copy).then_inc(self.evac, 1)
                        nc.scalar.activation(self.v.rearrange("p t n -> p (t n)"), bank[:, b + 1, :],
                                             ACT.Copy).then_inc(self.evac, 1)
                    if u < 3:
                        split_next_hi(act, m)
                act.wait_ge(self.evac, 10)
                nc.scalar.activation(self.sq.rearrange("p a n -> p (a n)"), self.qk.rearrange("p a n -> p (a n)"),
                                     ACT.Square).then_inc(self.sq_done, 1)
                act.wait_ge(self.ms_mm, 1)
                nc.scalar.activation(self.t[0:16, 0, :], bank[0:16, 4, :], ACT.Sqrt, bias=par[0:16, PCOL["eps"]:PCOL["eps"] + 1],
                                     scale=1.0 / 64).then_inc(self.rooted, 1)
                for g in range(4):
                    act.wait_ge(self.pool_out, g + 1)
                    nc.scalar.activation(h_hi[:, g, :], self.mixed[:, g, :], ACT.Copy).then_inc(self.mix_hi, 1)
                self.softmax.scalar(act, st)
                for u in (3, 4):
                    split_next_hi(act, self.m0 + u)
                self.tail.scalar(act, st)

            def vector(self, dve, st):
                for u in range(5):
                    if u == 1:
                        dve.wait_ge(unit_used, self.m0 + 1)
                        st.add(nc.vector.memset(self.u[:, :, 0:self.PAD], 0.0))
                        st.link(nc.vector.memset(self.u[:, :, self.PAD + S:], 0.0))
                    if u < 3:
                        split_next_lo(dve, self.m0 + u)
                dve.wait_ge(self.evac, 4)
                for g in range(4):
                    src, n = self.u[:, g, :], self.W
                    for a in range(g + 1):
                        step = 1 << a
                        n -= step
                        dst = self.sums[:, a % 2, :]
                        st.link(nc.vector.tensor_tensor(dst[:, 0:n], src[:, 0:n], src[:, step:step + n], ALU.add))
                        src = dst
                    if g == 0:
                        dve.wait_ge(even_loaded, 48)
                    lead = self.PAD - (1 << g)
                    other = self.sums[:, (g + 1) % 2, 0:S]
                    st.link(nc.vector.tensor_tensor(other, src[:, lead:lead + S], self.counts[:, g, :], ALU.mult))
                    nc.vector.tensor_tensor(self.pooled[:, g, :], other, self.u[:, g, self.PAD:self.PAD + S],
                                            ALU.subtract).then_inc(self.pool_ready, 1)
                    dve.wait_ge(self.pool_ready, g + 1)
                dve.wait_ge(self.rooted, 1)
                nc.vector.reciprocal(self.inv[0:16, :], self.t[0:16, 0, :]).then_inc(self.inv_done, 1)
                for g in range(4):
                    dve.wait_ge(self.pool_mm, g + 1)
                    nc.vector.tensor_scalar(self.mixed[:, g, :], bank[:, g, :], col("b_pool", g), col("pool_scale", g),
                                            ALU.add, ALU.mult).then_inc(self.pool_out, 1)
                for g in range(4):
                    dve.wait_ge(self.mix_hi, g + 1)
                    nc.vector.tensor_tensor(h_lo[:, g, :], self.mixed[:, g, :], h_hi[:, g, :],
                                            ALU.subtract).then_inc(self.mix_lo, 1)
                for i in range(6):
                    b = i
                    if b < 5:
                        dve.wait_ge(self.spread, b + 1)
                        nc.vector.scalar_tensor_tensor(self.qn[:, b, :], self.qk[:, b, :],
                                                       col("q_gain") if b < 4 else col("k_gain"),
                                                       bank[:, 4 + b % 2, :], ALU.mult,
                                                       ALU.mult).then_inc(self.normed, 1)
                    b = i - 1
                    if b >= 0:
                        dve.wait_ge(self.normed, b + 1)
                        st.add(nc.vector.tensor_tensor(self.t[:, 0, :], self.qn[:, b, :], self.cos, ALU.mult))
                        dve.wait_ge(self.swapped, b + 1)
                        st.link(nc.vector.tensor_tensor(self.t[:, 1, :], bank[:, 6 + b % 2, :], self.sin, ALU.mult))
                        nc.vector.tensor_tensor(self.qk[:, b, :], self.t[:, 0, :], self.t[:, 1, :],
                                                ALU.add).then_inc(self.turned, 1)
                        dve.wait_ge(self.turned, b + 1)
                self.softmax.vector(dve, st)
                conditioning.write_mod(dve, st, 1, 6)
                for u in (3, 4):
                    split_next_lo(dve, self.m0 + u)
                self.tail.vector(dve, st)

            def tensor(self, pe):
                for u in range(5):
                    m, b = self.m0 + u, 2 * slot(self.m0 + u)
                    pe.wait_ge(lo_split, m + 1)
                    if u >= 2:
                        pe.wait_ge(self.evac, 2 * (u - 1))
                    elif u == 0:
                        pe.wait_ge(Conditioning.mod_done, 1)
                    if u == 0:
                        last = both_features(pe, m, bank[:, b:b + 2, :], self.norm.wait_chunk)
                    else:
                        features(pe, m, 0, bank[:, b, :])
                    if 0 < u < 4:
                        last = features(pe, m, 1, bank[:, b + 1, :])
                    elif u == 4:
                        last = tokens(pe, m, bank[:, b + 1, :].rearrange("p (t n) -> p t n", t=TB), c0=P, n=P)
                    last.then_inc(unit_used, 1)
                pe.wait_ge(self.sq_done, 1)
                pair = table("pair_rows")
                for b in range(5):
                    last = nc.tensor.matmul(bank[0:16, 4, :], pair[:, 15 - 2 * b:31 - 2 * b], self.sq[:, b, :],
                                            start=(b == 0), stop=(b == 4))
                last.then_inc(self.ms_mm, 1)
                pe.wait_ge(even_loaded, 48)
                for g in range(4):
                    pe.wait_ge(self.pool_ready, g + 1)
                    nc.tensor.matmul(bank[:, g, :], self.wp[:, g, :], self.pooled[:, g, :], start=True,
                                     stop=True).then_inc(self.pool_mm, 1)
                pe.wait_ge(self.inv_done, 1)

                def spread(b):
                    if b >= 2:
                        pe.wait_ge(self.normed, b - 1)
                    rows = table("pair_spread")[0:16, b * P:b * P + P]
                    nc.tensor.matmul(bank[:, 4 + b % 2, :], rows, self.inv[0:16, :], start=True,
                                     stop=True).then_inc(self.spread, 1)

                spread(0)
                for b in range(5):
                    if b < 4:
                        spread(b + 1)
                    pe.wait_ge(self.normed, b + 1)
                    if b >= 2:
                        pe.wait_ge(self.turned, b - 1)
                    nc.tensor.matmul(bank[:, 6 + b % 2, :], table("swap"), self.qn[:, b, :], start=True,
                                     stop=True).then_inc(self.swapped, 1)
                pe.wait_ge(self.pool_out, 4)
                self.softmax.tensor(pe)
                self.tail.tensor(pe)

        class Mlstm:
            R, H, PAD = 40, 8, 4
            SEG = [[0, 512, 896, 1152], [0, 128, 384, 768]]
            raw_qk = area(0, 8, S + PAD)
            out = area(0, TB, D)
            qk = area(4128, 8, S)
            v = area(8224, TB, H, P + 1)
            o = area(12352, TB, D)
            e, se = area(16448, 2, 1280), area(19008, 2, 1280)
            gates, fb, ab, lf, f, g, em, ex, ln = (area(16448 + a * S, S) for a in range(9))
            md = area(21568, 2, S)
            m = area(22592, S)
            junk = area(23104, P)

            def __init__(self, norm):
                self.norm, self.m0 = norm, FIRST_UNIT["odd_in"]
                (self.s_evac, self.s_sel, self.s_abs, self.s_ln, self.s_em, self.s_em_in, self.s_cols_mm, self.s_cols,
                 self.s_conv, self.s_silu, self.s_scored, self.s_spread, self.s_masked, self.s_weights, self.s_se,
                 self.s_summed, self.s_out) = (
                    sem("mlstm_" + n) for n in ("evac", "sel", "abs", "ln", "em", "em_in", "cols_mm", "cols", "conv",
                                                "silu", "scored", "spread", "masked", "weights", "se", "summed",
                                                "out"))
                self.tail = ToFeatures("mlstm_rows", self.out, 0, 8, group=P, junk=self.junk, gate=self.o,
                                       gain=lambda b: col("head_gain", b),
                                       ready=lambda act, g: act.wait_ge(self.s_out, 2 * (g + 1)))
                self.gcol, self.emcol = small[:, 320:480], small[:, 160:320]

            def span(self, d, a):
                return (a * P, S) if d == 0 else (0, (a + 1) * P)

            def wait_chunk(self, eng, k):
                self.tail.wait_chunk(eng, k)

            def scalar(self, act, st):
                R = self.R
                for u in range(13):
                    m, b = self.m0 + u, 2 * slot(self.m0 + u)
                    act.wait_ge(unit_used, m + 1)
                    if u == 0:
                        nc.scalar.activation(self.gates, bank[:, b, :], ACT.Copy).then_inc(self.s_evac, 1)
                    elif u < 5:
                        nc.scalar.activation(self.raw_qk[:, 2 * u - 2:2 * u, 2:2 + S], bank[:, b:b + 2, :],
                                             ACT.Copy).then_inc(self.s_evac, 1)
                    elif u < 9:
                        h = 2 * (u - 5)
                        for t in range(TB):
                            ins = nc.scalar.activation(
                                self.v[:, t, h:h + 2, 0:P],
                                two_banks(m)[:, t, :].rearrange("p (h n) -> p h n", h=2), ACT.Copy)
                            if t < TB - 1:
                                st.add(ins)
                        ins.then_inc(self.s_evac, 1)
                    else:
                        c = 256 * (u - 9)
                        nc.scalar.activation(self.o[:, :, c:c + 256], two_banks(m), ACT.Sigmoid).then_inc(self.s_evac, 1)
                    split_next_hi(act, m)
                    if u == 2:
                        act.wait_ge(self.s_abs, 1)
                        st.link(nc.scalar.activation(self.ex[0:R, :], self.ab[0:R, :], ACT.Exp, scale=-1.0))
                        nc.scalar.activation(self.ln[0:R, :], self.ex[0:R, :], ACT.Ln, bias=1.0).then_inc(self.s_ln, 1)
                    if u == 3:
                        act.wait_ge(self.s_em_in, 1)
                        nc.scalar.activation(self.em[0:R, :], self.fb[0:R, :], ACT.Exp, scale=-1.0).then_inc(self.s_em, 1)
                    if u == 7:
                        for c in range(8):
                            act.wait_ge(self.s_conv, c + 1)
                            nc.scalar.activation(self.qk[:, c, :], self.acc_of(c), ACT.Silu,
                                                 bias=col("conv_b", c)).then_inc(self.s_silu, 1)
                act.wait_ge(self.s_cols, 1)
                for q in range(2 * self.H):
                    h, d = q // 2, q % 2
                    r = h + 32 * d
                    act.wait_ge(self.s_masked, q + 1)
                    if q >= 2:
                        act.wait_ge(self.s_se, q - 1)
                    for a in range(TB):
                        lo, hi = self.span(d, a)
                        seg = self.e[:, q % 2, self.SEG[d][a]:self.SEG[d][a] + hi - lo]
                        bias = self.gcol[:, a * R + r:a * R + r + 1]
                        at_ = a * P - lo
                        ins = nc.scalar.activation(seg[:, at_:at_ + P], self.md[:, q % 2, a * P:a * P + P], ACT.Exp,
                                                   bias=bias, scale=-1.0)
                        if hi - lo > P:
                            st.add(ins)
                            rest = (P, hi - lo) if d == 0 else (0, hi - lo - P)
                            ins = nc.scalar.activation(seg[:, rest[0]:rest[1]],
                                                       bank[:, 4 + q % 2, lo + rest[0]:lo + rest[1]], ACT.Exp,
                                                       bias=bias, scale=-1.0)
                        if a < TB - 1:
                            st.add(ins)
                        else:
                            ins.then_inc(self.s_weights, 1)
                    if d and h:
                        self.tail.group_squares(act, st, h - 1)
                act.preload_act_table_set("sqrt_and_others")
                self.tail.group_squares(act, st, self.H - 1)
                self.tail.scalar(act, st)

            def acc_of(self, c):
                return self.qk[:, c, :]

            def vector(self, dve, st):
                R = self.R
                rows = (slice(0, 8), slice(32, 40))
                for u in range(13):
                    m = self.m0 + u
                    if u == 0:
                        dve.wait_ge(unit_used, m + 1)
                        st.add(nc.vector.memset(self.raw_qk[:, :, 0:2], 0.0))
                        st.link(nc.vector.memset(self.raw_qk[:, :, 2 + S:], 0.0))
                        st.add(nc.vector.memset(self.v[:, :, :, P:P + 1], 1.0))
                        for v in (self.f, self.m):
                            st.add(nc.vector.memset(v[0:R, :], 0.0))
                    split_next_lo(dve, m)
                    if u == 1:
                        dve.wait_ge(self.s_sel, 1)
                        st.link(nc.vector.tensor_scalar(self.fb[0:R, :], bank[0:R, 5, :],
                                                        par[0:R, PCOL["gate_b_f"]:PCOL["gate_b_f"] + 1], None, ALU.add))
                        nc.vector.scalar_tensor_tensor(self.ab[0:R, :], self.fb[0:R, :], -1.0, self.fb[0:R, :], ALU.mult,
                                                       ALU.max).then_inc(self.s_abs, 1)
                    if u == 2:
                        dve.wait_ge(self.s_ln, 1)
                        st.link(nc.vector.scalar_tensor_tensor(self.lf[0:R, :], self.fb[0:R, :], 0.0, self.ln[0:R, :],
                                                               ALU.min, ALU.subtract))
                        for d, r in enumerate(rows):
                            way = slice(None, None, -1) if d else slice(None)
                            st.add(nc.vector.tensor_tensor_scan(
                                self.f[r, way], ones[r, 0:1].to_broadcast([8, S]), self.lf[r, way], 0.0, ALU.mult,
                                ALU.add))
                        st.settle()
                        st.link(nc.vector.scalar_tensor_tensor(self.g[0:R, :], bank[0:R, 4, :],
                                                               par[0:R, PCOL["gate_b_i"]:PCOL["gate_b_i"] + 1],
                                                               self.f[0:R, :], ALU.add, ALU.subtract))
                        for d, r in enumerate(rows):
                            way = slice(None, None, -1) if d else slice(None)
                            st.add(nc.vector.tensor_tensor_scan(self.m[r, way], self.g[r, way], self.g[r, way], 0.0,
                                                                ALU.max, ALU.max))
                        st.settle()
                        nc.vector.tensor_tensor(self.fb[0:R, :], self.f[0:R, :], self.m[0:R, :],
                                                ALU.add).then_inc(self.s_em_in, 1)
                    if 1 <= u < 5:
                        dve.wait_ge(self.s_evac, u + 1)
                        for c in (2 * u - 2, 2 * u - 1):
                            acc = self.acc_of(c)
                            for j in range(5):
                                w = col("conv_w", 8 * j + c)
                                src = self.raw_qk[:, c, j:j + S]
                                if j == 0:
                                    ins = nc.vector.tensor_scalar(acc, src, w, None, ALU.mult)
                                else:
                                    ins = nc.vector.scalar_tensor_tensor(acc, src, w, acc, ALU.mult, ALU.add)
                                if j < 4:
                                    st.link(ins)
                                else:
                                    ins.then_inc(self.s_conv, 1)
                    if u == 5:
                        dve.wait_ge(self.s_cols_mm, 1)
                        nc.vector.tensor_copy(small[:, 160:480], bank[:, 6, 0:320]).then_inc(self.s_cols, 1)
                dve.wait_ge(self.s_cols, 1)
                for q in range(2 * self.H + 1):
                    if q < 2 * self.H:
                        self.weigh(dve, st, q)
                    if q >= 1:
                        self.divide(dve, st, q - 1)
                    if q >= 4 and q % 2 == 0:
                        self.tail.gate_rows(dve, q // 2 - 2)
                self.tail.gate_rows(dve, self.H - 1)
                self.tail.vector(dve, st)

            def weigh(self, dve, st, q):
                d = q % 2
                dve.wait_ge(self.s_spread, q + 1)
                if q >= 2:
                    dve.wait_ge(self.s_weights, q - 1)
                hide = table("hide_bwd" if d else "hide_fwd").unsqueeze(1).to_broadcast([P, TB, P])
                nc.vector.tensor_tensor(self.md[:, q % 2, :].rearrange("p (a t) -> p a t", a=TB),
                                        bank[:, 4 + q % 2, :].rearrange("p (a t) -> p a t", a=TB), hide,
                                        ALU.add).then_inc(self.s_masked, 1)
                dve.wait_ge(self.s_weights, q + 1)
                dve.wait_ge(self.s_scored, q // 2 + 1)
                if q >= 2:
                    dve.wait_ge(self.s_summed, q - 1)
                for a in range(TB):
                    lo, hi = self.span(d, a)
                    seg = slice(self.SEG[d][a], self.SEG[d][a] + hi - lo)
                    ins = nc.vector.scalar_tensor_tensor(self.se[:, q % 2, seg], bank[:, a, lo:hi], 64 ** -0.5,
                                                         self.e[:, q % 2, seg], ALU.mult, ALU.mult)
                    if a < TB - 1:
                        st.add(ins)
                    else:
                        ins.then_inc(self.s_se, 1)

            def divide(self, dve, st, q):
                h, d = q // 2, q % 2
                r = h + 32 * d
                num = bank[:, 6:8, 0:2 * (P + 1)].rearrange("p a (b n) -> p a b n", b=2)
                dn, ab, fl, rc = (small[:, 12 * 4 + 4 * a:12 * 4 + 4 * a + 4] for a in range(4))
                dve.wait_ge(self.s_summed, q + 1)
                st.link(nc.vector.tensor_copy(dn.rearrange("p (a b) -> p a b", a=2).unsqueeze(3), num[:, :, :, P:P + 1]))
                st.link(nc.vector.scalar_tensor_tensor(ab, dn, -1.0, dn, ALU.mult, ALU.max))
                em = self.emcol.rearrange("p (a r) -> p a r", a=TB)[:, :, r]
                st.link(nc.vector.tensor_tensor(fl, ab, em, ALU.max))
                st.link(nc.vector.reciprocal(rc, fl))
                for t in range(TB):
                    out = self.out[:, t, h * P:h * P + P]
                    src = num[:, t // 2, t % 2, 0:P]
                    if d == 0:
                        ins = nc.vector.tensor_scalar(out, src, rc[:, t:t + 1], None, ALU.mult)
                    else:
                        if t == 0:
                            dve.wait_ge(self.s_out, q)
                        ins = nc.vector.scalar_tensor_tensor(out, src, rc[:, t:t + 1], out, ALU.mult, ALU.add)
                    if t < TB - 1:
                        st.add(ins)
                    else:
                        ins.then_inc(self.s_out, 1)

            def tensor(self, pe):
                R = self.R
                for u in range(13):
                    m, b = self.m0 + u, 2 * slot(self.m0 + u)
                    pe.wait_ge(lo_split, m + 1)
                    if u >= 2:
                        pe.wait_ge(self.s_evac, u - 1)
                    if u == 0:
                        last = features(pe, m, 0, bank[:, b, :], self.norm.wait_chunk)
                    elif u < 5:
                        features(pe, m, 0, bank[:, b, :])
                        last = features(pe, m, 1, bank[:, b + 1, :])
                    else:
                        last = tokens(pe, m, two_banks(m))
                    last.then_inc(unit_used, 1)
                    if u == 1:
                        pe.wait_ge(self.s_evac, 1)
                        nc.tensor.matmul(bank[0:R, 4, :], table("gate_i"), self.gates, start=True, stop=True)
                        nc.tensor.matmul(bank[0:R, 5, :], table("gate_f"), self.gates, start=True,
                                         stop=True).then_inc(self.s_sel, 1)
                    if u == 4:
                        pe.wait_ge(self.s_em, 1)
                        for a, src in ((0, self.em), (1, self.g)):
                            for t in range(TB):
                                c = a * TB * R + t * R
                                last = nc.tensor.transpose(bank[:, 6, c:c + R], src[0:R, t * P:t * P + P],
                                                           ident[0:R, 0:R])
                        last.then_inc(self.s_cols_mm, 1)
                pe.wait_ge(self.s_cols, 1)
                pe.wait_ge(self.s_evac, 13)
                pe.wait_ge(self.s_silu, 8)
                for q in range(2 * self.H + 1):
                    if q < 2 * self.H:
                        h, d = q // 2, q % 2
                        r = h + 32 * d
                        if q >= 2:
                            pe.wait_ge(self.s_weights, q - 1)
                        nc.tensor.matmul(bank[:, 4 + q % 2, :], ident[0:R, r:r + 1].to_broadcast([R, P]),
                                         self.m[0:R, :], start=True, stop=True).then_inc(self.s_spread, 1)
                        if d == 0:
                            half = slice(64 * (h % 2), 64 * (h % 2) + 64)
                            if h:
                                pe.wait_ge(self.s_se, 2 * h)
                            for a in range(TB):
                                last = nc.tensor.matmul(bank[:, a, :], self.qk[half, 4 + h // 2, a * P:a * P + P],
                                                        self.qk[half, h // 2, :], start=True, stop=True)
                            last.then_inc(self.s_scored, 1)
                    if q >= 1:
                        self.sum_values(pe, q - 1)
                self.tail.tensor(pe)

            def sum_values(self, pe, q):
                h, d = q // 2, q % 2
                pe.wait_ge(self.s_se, q + 1)
                if q:
                    pe.wait_ge(self.s_out, q)
                for t in range(TB):
                    blocks = range(0, t + 1) if d == 0 else range(t, TB)
                    out = bank[:, 6 + t // 2, (t % 2) * (P + 1):(t % 2 + 1) * (P + 1)]
                    for a in blocks:
                        c = self.SEG[d][a] + t * P - self.span(d, a)[0]
                        last = nc.tensor.matmul(out, self.se[:, q % 2, c:c + P], self.v[:, a, h, :],
                                                start=(a == blocks[0]), stop=(a == blocks[-1]))
                last.then_inc(self.s_summed, 1)

        class Hgrn:
            H = 4
            STEPS = LEVELS + 2
            q, k, b = area(0, H, S), area(2048, H, S), area(4096, H, S)
            f = area(6144, H, S)
            out = area(6144, TB, H * P)
            v, gate = area(8192, TB, H * P), area(10240, TB, H * P)
            sq, sk, sv = area(12288, 4, S), area(14336, 4, S), area(16384, TB, 512)
            diff, e, kq = area(18432, 2, S), area(19456, 2, S), area(20480, 2, S)
            near, far = area(21504, 2, S), area(22528, 2, 768)
            masks, run = area(24064, LEVELS + 1, P), area(25088, S)
            junk = small[:, 232:232 + P]

            AHEAD, UNITS, QUARTERS = 6, 14, 4

            def __init__(self, norm):
                self.norm, self.m0 = norm, FIRST_UNIT["mix_in"]
                (self.s_evac, self.s_f, self.s_lf, self.s_b, self.s_diff, self.s_e, self.s_kq, self.s_mm, self.s_cp,
                 self.s_summed, self.s_out, self.s_lb) = (
                    sem("hgrn_" + n) for n in ("evac", "f", "lf", "b", "diff", "e", "kq", "mm", "cp", "summed", "out",
                                               "lb"))
                self.tail = ToFeatures("hgrn_rows", self.out, 0, 4, group=P, junk=self.junk, gate=self.gate,
                                       gain=lambda b: col("hg_gnorm", b), cols=32,
                                       ready=lambda act, g: act.wait_ge(self.s_out, g + 1))
                self.lb, self.one_lb = small[:, 192:196], small[:, 196:200]
                self.lbt = small[:, 200:224]
                self.tot01 = small[:, 224:228]

            def scalar(self, act, st):
                act.wait_ge(self.s_lb, 1)
                nc.scalar.activation(self.lbt[:, 8:16], self.lbt[:, 0:8], ACT.Exp).then_inc(self.s_lb, 1)
                for u in range(self.UNITS):
                    m, b = self.m0 + u, 2 * slot(self.m0 + u)
                    if u >= self.AHEAD:
                        g = self.QUARTERS * (u - self.AHEAD)
                        self.exponents(act, st, g + 2 if g else 0, g + self.QUARTERS + 2)
                    act.wait_ge(unit_used, m + 1)
                    both = bank[:, b:b + 2, :]
                    c = 256 * (u % 2)
                    r = slice(2 * (u % 2), 2 * (u % 2) + 2)
                    dst, src, fn, scale = [
                        (self.f[:, r, :], both, ACT.Sigmoid, 1.0), (self.q[:, r, :], both, ACT.Copy, 1.0),
                        (self.v[:, :, c:c + 256], two_banks(m), ACT.Copy, 1.0),
                        (self.gate[:, :, c:c + 256], two_banks(m), ACT.Silu, 1.0),
                        (self.sq[:, r, :], both, ACT.Copy, 0.125), (self.sk[:, r, :], both, ACT.Copy, 1.0),
                        (self.sv[:, :, c:c + 256], two_banks(m), ACT.Copy, 1.0)][u // 2]
                    nc.scalar.activation(dst, src, fn, scale=scale).then_inc(self.s_evac, 1)
                    split_next_hi(act, m)
                    if u == 3:
                        act.wait_ge(self.s_f, 1)
                        nc.scalar.activation(self.f.rearrange("p a n -> p (a n)"), self.f.rearrange("p a n -> p (a n)"),
                                             ACT.Ln).then_inc(self.s_lf, 1)
                self.exponents(act, st, self.QUARTERS * (self.UNITS - self.AHEAD) + 2, self.H * self.STEPS)
                self.copy_out(act, self.H - 1)
                self.tail.group_squares(act, st, self.H - 1)
                self.tail.take_roots(act)

            def exponents(self, act, st, first, end):
                for g in range(first, end):
                    self.exponent(act, st, g)

            def exponent(self, act, st, g):
                h, l = g // self.STEPS, g % self.STEPS
                bh = self.b[:, h, :]
                e = self.e[:, g % 2, :]
                if g == 0:
                    act.wait_ge(self.s_b, 1)
                if g >= 2:
                    act.wait_ge(self.s_kq, g - 1)
                if l < LEVELS:
                    n = 1 << l
                    act.wait_ge(self.s_diff, h * LEVELS + l + 1)
                    d4 = self.diff[:, (h * LEVELS + l) % 2, :].rearrange("p (b z m) -> p b z m", z=2, m=n)
                    e4 = e.rearrange("p (b z m) -> p b z m", z=2, m=n)
                    st.add(nc.scalar.activation(e4[:, :, 0, :], d4[:, :, 0, :], ACT.Exp, scale=-1.0))
                    nc.scalar.activation(e4[:, :, 1, :], d4[:, :, 1, :], ACT.Exp).then_inc(self.s_e, 1)
                    return

                def total(t):
                    return bh[:, t * P + P - 1:t * P + P]

                if l == LEVELS:
                    parts = [(-1.0, total(0)), (1.0, 0.0), (-1.0, total(2)), (1.0, 0.0)]
                else:
                    parts = [(-1.0, self.tot01[:, h:h + 1]), (-1.0, total(1)), (1.0, 0.0), (1.0, total(2))]
                for t, (sign, bias) in enumerate(parts):
                    ins = nc.scalar.activation(e[:, t * P:t * P + P], bh[:, t * P:t * P + P], ACT.Exp,
                                               bias=bias, scale=sign)
                    if t < TB - 1:
                        st.add(ins)
                    else:
                        ins.then_inc(self.s_e, 1)
                if l == self.STEPS - 1 and h:
                    self.copy_out(act, h - 1)
                    self.tail.group_squares(act, st, h - 1)

            def copy_out(self, act, h):
                act.wait_ge(self.s_summed, h + 1)
                nc.scalar.activation(self.out[:, :, h * P:h * P + P],
                                     bank[:, 7, :].rearrange("p (t n) -> p t n", t=TB),
                                     ACT.Copy).then_inc(self.s_out, 1)

            def vector(self, dve, st):
                raws = par[:, PCOL["lb_raw0"]:PCOL["lb_raw0"] + 8].rearrange("p (a b) -> p a b", a=2)
                t = self.lbt
                st.link(nc.vector.tensor_tensor(t[:, 16:20], raws[:, 0, :], raws[:, 1, :], ALU.max))
                st.add(nc.vector.tensor_tensor(t[:, 0:4], raws[:, 0, :], t[:, 16:20], ALU.subtract))
                nc.vector.tensor_tensor(t[:, 4:8], raws[:, 1, :], t[:, 16:20], ALU.subtract).then_inc(self.s_lb, 1)
                st.settle()
                dve.wait_ge(self.s_lb, 2)
                st.link(nc.vector.tensor_tensor(t[:, 16:20], t[:, 8:12], t[:, 12:16], ALU.add))
                st.link(nc.vector.reciprocal(t[:, 20:24], t[:, 16:20]))
                st.link(nc.vector.tensor_tensor(self.lb, t[:, 8:12], t[:, 20:24], ALU.mult))
                st.link(nc.vector.tensor_scalar(self.one_lb, self.lb, -1.0, 1.0, ALU.mult, ALU.add))
                dve.wait_ge(mix_loaded, 16)
                for u in range(self.UNITS):
                    if u >= self.AHEAD:
                        g = self.QUARTERS * (u - self.AHEAD)
                        self.steps(dve, st, g + 1 if g else 0, g + self.QUARTERS + 1)
                    split_next_lo(dve, self.m0 + u)
                    if u == 2:
                        dve.wait_ge(self.s_evac, 2)
                        for h in range(self.H):
                            st.link(nc.vector.tensor_scalar(self.f[:, h, :], self.f[:, h, :], self.one_lb[:, h:h + 1],
                                                            self.lb[:, h:h + 1], ALU.mult, ALU.add))
                        nc.vector.tensor_scalar(self.k.rearrange("p a n -> p (a n)"),
                                                self.f.rearrange("p a n -> p (a n)"), -1.0, 1.0, ALU.mult,
                                                ALU.add).then_inc(self.s_f, 1)
                    if u == 4:
                        dve.wait_ge(self.s_lf, 1)
                        for h in range(self.H):
                            st.add(nc.vector.tensor_tensor_scan(self.b[:, h, :], self.run, self.f[:, h, :], 0.0,
                                                                ALU.mult, ALU.add))
                        st.settle()
                        nc.vector.tensor_tensor(self.tot01, self.b[:, :, P - 1], self.b[:, :, 2 * P - 1],
                                                ALU.add).then_inc(self.s_b, 1)
                n = self.H * self.STEPS
                self.steps(dve, st, self.QUARTERS * (self.UNITS - self.AHEAD) + 1, n)
                self.keep(dve, n - 1)

            def steps(self, dve, st, first, end):
                for g in range(first, end):
                    if g == 0:
                        dve.wait_ge(self.s_b, 1)
                        self.differ(dve, 0)
                    if g + 1 < self.H * self.STEPS:
                        self.differ(dve, g + 1)
                    self.weigh(dve, st, g)
                    if g:
                        self.keep(dve, g - 1)

            def differ(self, dve, g):
                h, l = g // self.STEPS, g % self.STEPS
                if l >= LEVELS:
                    return
                n, i = 1 << l, h * LEVELS + l
                if i >= 2:
                    back = i - 2
                    dve.wait_ge(self.s_e, (back // LEVELS) * self.STEPS + back % LEVELS + 1)
                b3 = self.b[:, h, :].rearrange("p (b m) -> p b m", m=2 * n)
                nc.vector.tensor_tensor(self.diff[:, i % 2, :].rearrange("p (b m) -> p b m", m=2 * n), b3,
                                        b3[:, :, n - 1:n].to_broadcast([P, S // (2 * n), 2 * n]),
                                        ALU.subtract).then_inc(self.s_diff, 1)

            def weigh(self, dve, st, g):
                h, l = g // self.STEPS, g % self.STEPS
                n = 1 << l
                dve.wait_ge(self.s_e, g + 1)
                if g >= 2:
                    dve.wait_ge(self.s_mm, g - 1)
                e, kq, k, q = (v.rearrange("p (b z m) -> p b z m", z=2, m=n) for v in
                               (self.e[:, g % 2, :], self.kq[:, g % 2, :], self.k[:, h, :], self.q[:, h, :]))
                st.add(nc.vector.tensor_tensor(kq[:, :, 0, :], k[:, :, 0, :], e[:, :, 0, :], ALU.mult))
                nc.vector.tensor_tensor(kq[:, :, 1, :], q[:, :, 1, :], e[:, :, 1, :], ALU.mult).then_inc(self.s_kq, 1)

            def keep(self, dve, g):
                h, l = g // self.STEPS, g % self.STEPS
                near = self.near[:, h % 2, :].rearrange("p (a t) -> p a t", a=TB)
                far = self.far[:, h % 2, :]
                src = bank[:, 4 + g % 2, :]
                dve.wait_ge(self.s_mm, g + 1)
                if l == 0:
                    if h >= 2:
                        dve.wait_ge(self.s_summed, h - 1)
                    diag = self.masks[:, LEVELS:LEVELS + 1, :].to_broadcast([P, TB, P])
                    nc.vector.tensor_tensor(near, bank[:, 6, :].rearrange("p (a t) -> p a t", a=TB), diag,
                                            ALU.mult).then_inc(self.s_cp, 1)
                if l < LEVELS:
                    dve.wait_ge(self.s_cp, h * (self.STEPS + 1) + l + 1)
                    nc.vector.copy_predicated(near, self.masks[:, l:l + 1, :].bitcast(I32).to_broadcast([P, TB, P]),
                                              src.rearrange("p (a t) -> p a t", a=TB)).then_inc(self.s_cp, 1)
                elif l == LEVELS:
                    nc.vector.tensor_copy(far[:, 0:256], src[:, 0:256]).then_inc(self.s_cp, 1)
                else:
                    nc.vector.tensor_copy(far[:, 256:768], src).then_inc(self.s_cp, 1)

            def tensor(self, pe):
                for u in range(self.UNITS):
                    m, b = self.m0 + u, 2 * slot(self.m0 + u)
                    pe.wait_ge(lo_split, m + 1)
                    if u >= 2:
                        pe.wait_ge(self.s_evac, u - 1)
                    if u == 0:
                        last = both_features(pe, m, bank[:, b:b + 2, :], self.norm.wait_chunk)
                    elif u < 4:
                        features(pe, m, 0, bank[:, b, :])
                        last = features(pe, m, 1, bank[:, b + 1, :])
                    elif u < self.AHEAD:
                        last = tokens(pe, m, two_banks(m))
                    else:
                        for j in range(self.QUARTERS):
                            last = self.quarter(m, j, u in (8, 9, 10, 11))
                            if j == self.QUARTERS - 1:
                                last.then_inc(unit_used, 1)
                            self.step(pe, self.QUARTERS * (u - self.AHEAD) + j)
                        continue
                    last.then_inc(unit_used, 1)
                for g in range(self.QUARTERS * (self.UNITS - self.AHEAD), self.H * self.STEPS):
                    self.step(pe, g)
                self.sum_values(pe, self.H - 1)

            def quarter(self, m, j, as_features):
                wh, wl = unit_cols(m)
                for k in range(4 * (j % 2), 4 * (j % 2) + 4) if as_features else range(KC):
                    if as_features:
                        r = slice((j // 2) * P, (j // 2) * P + P)
                        last = three_passes(bank[:, 2 * slot(m) + j // 2, :], (wh[:, k, r], wl[:, k, r]),
                                            (h_hi[:, k, :], h_lo[:, k, :]), k == 0, k == KC - 1)
                    else:
                        r = slice(j * P, j * P + P)
                        last = three_passes(two_banks(m)[:, j, :], (h_hi[:, k, r], h_lo[:, k, r]),
                                            (wh[:, k, :], wl[:, k, :]), k == 0, k == KC - 1)
                return last

            def step(self, pe, g):
                h, l = g // self.STEPS, g % self.STEPS
                if l == 0:
                    if h:
                        pe.wait_ge(self.s_cp, (h - 1) * (self.STEPS + 1) + 1)
                    for t in range(TB):
                        r = slice(t * P, t * P + P)
                        nc.tensor.matmul(bank[:, 6, r], self.k[:, h, r], self.q[:, h, r], start=True, stop=True)
                pe.wait_ge(self.s_kq, g + 1)
                if g >= 2:
                    hh, ll = (g - 2) // self.STEPS, (g - 2) % self.STEPS
                    pe.wait_ge(self.s_cp, hh * (self.STEPS + 1) + ll + 2)
                kq, out = self.kq[:, g % 2, :], bank[:, 4 + g % 2, :]
                if l < LEVELS:
                    for t in range(TB):
                        r = slice(t * P, t * P + P)
                        last = nc.tensor.matmul(out[:, r], kq[:, r], kq[:, r], start=True, stop=True)
                elif l == LEVELS:
                    nc.tensor.matmul(out[:, 0:P], kq[:, 0:P], kq[:, P:2 * P], start=True, stop=True)
                    last = nc.tensor.matmul(out[:, P:2 * P], kq[:, 2 * P:3 * P], kq[:, 3 * P:4 * P], start=True,
                                            stop=True)
                else:
                    nc.tensor.matmul(out[:, 0:2 * P], kq[:, 0:P], kq[:, 2 * P:4 * P], start=True, stop=True)
                    last = nc.tensor.matmul(out[:, 2 * P:4 * P], kq[:, P:2 * P], kq[:, 2 * P:4 * P], start=True,
                                            stop=True)
                last.then_inc(self.s_mm, 1)
                if l == 1 and h:
                    self.sum_values(pe, h - 1)

            def sum_values(self, pe, h):
                pe.wait_ge(self.s_cp, (h + 1) * (self.STEPS + 1))
                pe.wait_ge(self.s_evac, 6)
                if h:
                    pe.wait_ge(self.s_out, h)
                near, far = self.near[:, h % 2, :], self.far[:, h % 2, :]
                where = {(a, a): near[:, a * P:a * P + P] for a in range(TB)}
                for n, pair in enumerate([(0, 1), (2, 3), (0, 2), (0, 3), (1, 2), (1, 3)]):
                    where[pair] = far[:, n * P:n * P + P]
                for t in range(TB):
                    for a in range(t + 1):
                        last = nc.tensor.matmul(bank[:, 7, t * P:t * P + P], where[(a, t)],
                                                self.v[:, a, h * P:h * P + P], start=(a == 0), stop=(a == t))
                last.then_inc(self.s_summed, 1)

        class Stick:
            H = 8
            OFF = [0, 512, 896, 1152]
            N = 1280
            z = [area(2048, 1280), area(18432, 1280)]
            e = [area(3328, 1280), area(19712, 1280)]
            l = [area(4608, 1280), area(20992, 1280)]
            out = area(0, TB, 512)

            def __init__(self, hgrn):
                self.hg = hgrn
                (self.s_z, self.s_abs, self.s_ln, self.s_l, self.s_suf, self.s_x, self.s_nx, self.s_a, self.s_o,
                 self.s_out) = (sem("stick_" + n) for n in ("z", "abs", "ln", "l", "suf", "x", "nx", "a", "o", "out"))
                self.tail = ToFeatures("stick_rows", self.out, 4, 4, group=64, junk=self.hg.junk,
                                       gain=lambda b: col("sb_gnorm", b),
                                       ready=lambda act, g: act.wait_ge(self.s_out, g + 1))

            def seg(self, a):
                return slice(self.OFF[a], self.OFF[a] + S - a * P)

            def diag(self, a):
                return slice(self.OFF[a], self.OFF[a] + P)

            def wait_chunk(self, pe, k):
                self.hg.tail.wait_chunk(pe, k)
                if k in (2, 3):
                    self.tail.turn(pe, k - 2)
                self.tail.wait_chunk(pe, k)

            def tensor(self, pe):
                pe.wait_ge(self.hg.s_evac, self.hg.UNITS)
                pe.wait_ge(self.hg.s_cp, self.hg.H * (self.hg.STEPS + 1))
                pe.wait_ge(self.hg.s_out, self.hg.H)
                for i in range(self.H + 2):
                    h = i
                    if h < self.H:
                        half = slice(64 * (h % 2), 64 * (h % 2) + 64)
                        if h:
                            pe.wait_ge(self.s_abs, h)
                        for a in range(TB):
                            last = nc.tensor.matmul(bank[:, a, a * P:S], self.hg.sk[half, h // 2, a * P:a * P + P],
                                                    self.hg.sq[half, h // 2, a * P:S], start=True, stop=True)
                        last.then_inc(self.s_z, 1)
                    h = i - 2
                    if h >= 0:
                        pe.wait_ge(self.s_a, h + 1)
                        if h >= 2:
                            pe.wait_ge(self.s_out, h - 1)
                        w = self.z[h % 2]
                        for t in range(TB):
                            for a in range(t + 1):
                                c = self.OFF[a] + (t - a) * P
                                last = nc.tensor.matmul(bank[:, 6 + h % 2, t * 64:t * 64 + 64], w[:, c:c + P],
                                                        self.hg.sv[:, a, h * 64:h * 64 + 64], start=(a == 0),
                                                        stop=(a == t))
                        last.then_inc(self.s_o, 1)
                    h = i - 1
                    if 0 <= h < self.H:
                        pe.wait_ge(self.s_l, h + 1)
                        for a in range(TB):
                            n = TB * h + a
                            if n >= 2:
                                pe.wait_ge(self.s_x, n - 1)
                            for j in range(a, TB):
                                last = nc.tensor.matmul(bank[:, 4 + n % 2, j * P:S],
                                                        table("tri") if j == a else ones,
                                                        self.l[h % 2][:, self.seg(j)], start=(j == a),
                                                        stop=(j == TB - 1))
                            last.then_inc(self.s_suf, 1)

            def vector(self, dve, st):
                for i in range(self.H + 1):
                    h = i
                    if h < self.H:
                        z, e = self.z[h % 2], self.e[h % 2]
                        dve.wait_ge(self.s_z, h + 1)
                        if h >= 2:
                            dve.wait_ge(self.s_o, h - 1)
                        for a in range(TB):
                            st.add(nc.vector.tensor_copy(z[:, self.seg(a)], bank[:, a, a * P:S]))
                        st.settle()
                        nc.vector.scalar_tensor_tensor(e, z, -1.0, z, ALU.mult, ALU.max).then_inc(self.s_abs, 1)
                    h = i - 1
                    if h >= 0:
                        z = self.z[h % 2]
                        for a in range(TB):
                            n = TB * h + a
                            dve.wait_ge(self.s_suf, n + 1)
                            nc.vector.scalar_tensor_tensor(z[:, self.seg(a)], bank[:, 4 + n % 2, a * P:S], -1.0,
                                                           z[:, self.seg(a)], ALU.mult, ALU.add).then_inc(self.s_x, 1)
                        dve.wait_ge(self.s_x, TB * h + TB)
                        for a in range(TB):
                            ins = nc.vector.tensor_tensor(z[:, self.diag(a)], z[:, self.diag(a)], table("neg_strict"),
                                                          ALU.add)
                            if a < TB - 1:
                                st.add(ins)
                            else:
                                ins.then_inc(self.s_nx, 1)
                    h = i
                    if h < self.H:
                        z, e, l = self.z[h % 2], self.e[h % 2], self.l[h % 2]
                        dve.wait_ge(self.s_ln, h + 1)
                        st.link(nc.vector.scalar_tensor_tensor(l, z, 0.0, e, ALU.max, ALU.add))
                        for a in range(TB):
                            ins = nc.vector.tensor_tensor(l[:, self.diag(a)], l[:, self.diag(a)], table("strict"),
                                                          ALU.mult)
                            if a < TB - 1:
                                st.add(ins)
                            else:
                                ins.then_inc(self.s_l, 1)
                    if i == 0:
                        self.hg.tail.take_inverses(dve, st)
                    if i < 4:
                        self.hg.tail.gate_rows(dve, i)
                        self.hg.tail.scale_rows(dve, i)
                self.tail.take_inverses(dve, st)
                for b in range(4):
                    self.tail.scale_rows(dve, b)
                    self.hg.tail.low(dve, b)
                for b in range(4):
                    self.tail.low(dve, b)

            def scalar(self, act, st):
                act.preload_act_table_set("natural_log_exp_and_others")
                for i in range(self.H + 2):
                    h = i
                    if h < self.H:
                        e = self.e[h % 2]
                        act.wait_ge(self.s_abs, h + 1)
                        st.link(nc.scalar.activation(e, e, ACT.Exp, scale=-1.0))
                        nc.scalar.activation(e, e, ACT.Ln, bias=1.0).then_inc(self.s_ln, 1)
                    h = i - 1
                    if 0 <= h < self.H:
                        act.wait_ge(self.s_nx, h + 1)
                        nc.scalar.activation(self.z[h % 2], self.z[h % 2], ACT.Exp).then_inc(self.s_a, 1)
                    h = i - 2
                    if h >= 0:
                        act.wait_ge(self.s_o, h + 1)
                        nc.scalar.activation(self.out[:, :, h * 64:h * 64 + 64],
                                             bank[:, 6 + h % 2, 0:256].rearrange("p (t n) -> p t n", t=TB),
                                             ACT.Copy).then_inc(self.s_out, 1)
                        if h == self.H - 1:
                            act.preload_act_table_set("sqrt_and_others")
                        self.tail.group_squares(act, st, h)
                self.tail.take_roots(act)
                for tail in (self.hg.tail, self.tail):
                    for b in range(4):
                        tail.high(act, b)

        class Mix:
            def __init__(self, norm):
                self.norm = norm
                self.hg = Hgrn(norm)
                self.sb = Stick(self.hg)
                self.wait_chunk = self.sb.wait_chunk

            def scalar(self, act, st):
                self.hg.scalar(act, st)
                self.sb.scalar(act, st)

            def vector(self, dve, st):
                self.hg.vector(dve, st)
                self.sb.vector(dve, st)

            def tensor(self, pe):
                self.hg.tensor(pe)
                self.sb.tensor(pe)
                self.hg.tail.tensor(pe)

        class Memory:
            HEADS = 4
            mt, sq, t = area(8192, KC, N_MEM), area(10240, KC, N_MEM), area(12288, KC, N_MEM)
            kt, v = area(8192, KC, N_MEM), area(10240, MB, D)
            q = area(0, KC, S)
            p, pt = area(14336, 2, N_MEM), area(14848, 2, N_MEM)
            out = area(15360, TB, D)
            root, rstd = area(23552, N_MEM), area(23808, N_MEM)

            def __init__(self):
                self.m0 = FIRST_UNIT["mem_kv"]
                (self.s_sq, self.s_ms, self.s_root, self.s_scaled, self.s_hi, self.s_lo, self.s_evac) = (
                    sem("mem_" + n) for n in ("sq", "ms", "root", "scaled", "hi", "lo", "evac"))

                def scores(s):
                    h, t = s // TB, s % TB
                    return [(self.q[:, 2 * h + c, t * P:t * P + P], self.kt[:, 2 * h + c, :]) for c in range(2)]

                def values(s, k):
                    h = s // TB
                    return self.v[:, k, 256 * h:256 * h + 256]

                def out(s):
                    h, t = s // TB, s % TB
                    return self.out[:, t, 256 * h:256 * h + 256]

                self.softmax = Softmax("mem", self.HEADS * TB, N_MEM, 256 ** -0.5, scores, values, out, 256, self.p,
                                       self.pt, lambda pe: pe.wait_ge(self.s_evac, 12))
                self.tail = ToFeatures("mem_rows", self.out, 0, KC,
                                       ready=lambda pe: pe.wait_ge(self.softmax.out_done, self.HEADS * TB))
                self.wait_chunk = self.tail.wait_chunk

            def prepare_scalar(self, act, u):
                if u == 0:
                    act.wait_ge(mem_loaded, 16)
                    nc.scalar.activation(self.sq.rearrange("p a n -> p (a n)"), self.mt.rearrange("p a n -> p (a n)"),
                                         ACT.Square).then_inc(self.s_sq, 1)
                if u == 1:
                    act.wait_ge(self.s_ms, 1)
                    nc.scalar.activation(self.root, bank[:, 5, 0:N_MEM], ACT.Sqrt, bias=eps, scale=1.0 / D).then_inc(
                        self.s_root, 1)
                    for k in range(KC):
                        act.wait_ge(self.s_scaled, k + 1)
                        nc.scalar.activation(mem_hi[:, k, :], self.t[:, k, :], ACT.Copy).then_inc(self.s_hi, 1)

            def prepare_vector(self, dve, st, u):
                if u == 1:
                    dve.wait_ge(mem_loaded, 16)
                    dve.wait_ge(self.s_root, 1)
                    st.link(nc.vector.reciprocal(self.rstd, self.root))
                    for k in range(KC):
                        nc.vector.scalar_tensor_tensor(self.t[:, k, :], self.mt[:, k, :], col("mem_kv_norm", k),
                                                       self.rstd, ALU.mult, ALU.mult).then_inc(self.s_scaled, 1)
                    for k in range(KC):
                        dve.wait_ge(self.s_hi, k + 1)
                        nc.vector.tensor_tensor(mem_lo[:, k, :], self.t[:, k, :], mem_hi[:, k, :],
                                                ALU.subtract).then_inc(self.s_lo, 1)

            def prepare_tensor(self, pe, u):
                if u == 0:
                    pe.wait_ge(self.s_sq, 1)
                    for k in range(KC):
                        last = nc.tensor.matmul(bank[:, 5, 0:N_MEM], ones, self.sq[:, k, :], start=(k == 0),
                                                stop=(k == KC - 1))
                    last.then_inc(self.s_ms, 1)

            def scalar(self, act, st):
                self.norm.take_root(act)
                for u in range(12):
                    m, b = self.m0 + u, 2 * slot(self.m0 + u)
                    act.wait_ge(unit_used, m + 1)
                    if u < 4:
                        dst, src = self.kt[:, 2 * u:2 * u + 2, :], bank[:, b:b + 2, 0:N_MEM]
                    elif u < 8:
                        c = 256 * (u - 4)
                        dst, src = self.v[:, :, c:c + 256], two_banks(m, MB)
                    else:
                        dst, src = self.q[:, 2 * (u - 8):2 * (u - 8) + 2, :], bank[:, b:b + 2, :]
                    nc.scalar.activation(dst, src, ACT.Copy).then_inc(self.s_evac, 1)
                    split_next_hi(act, m)
                    if 1 <= u < 5:
                        for k in (2 * u - 2, 2 * u - 1):
                            self.norm.high(act, k)
                self.softmax.scalar(act, st)
                self.tail.scalar(act, st)

            def vector(self, dve, st):
                self.norm.take_inverse(dve)
                for u in range(12):
                    split_next_lo(dve, self.m0 + u)
                    if 1 <= u < 5:
                        for k in (2 * u - 2, 2 * u - 1):
                            self.norm.scale_chunk(dve, k)
                        for k in (2 * u - 2, 2 * u - 1):
                            self.norm.low(dve, k)
                self.softmax.vector(dve, st)
                self.tail.vector(dve, st)

            def tensor(self, pe):
                pe.wait_ge(self.s_lo, KC)
                for u in range(12):
                    m, b = self.m0 + u, 2 * slot(self.m0 + u)
                    pe.wait_ge(lo_split, m + 1)
                    if u >= 2:
                        pe.wait_ge(self.s_evac, u - 1)
                    if u < 4:
                        features(pe, m, 0, bank[:, b, 0:N_MEM], src=(mem_hi, mem_lo))
                        last = features(pe, m, 1, bank[:, b + 1, 0:N_MEM], src=(mem_hi, mem_lo))
                    elif u < 8:
                        last = tokens(pe, m, two_banks(m, MB), blocks=MB, src=(mem_hi, mem_lo))
                    elif u == 8:
                        last = both_features(pe, m, bank[:, b:b + 2, :], self.norm.wait_chunk)
                    else:
                        features(pe, m, 0, bank[:, b, :])
                        last = features(pe, m, 1, bank[:, b + 1, :])
                    last.then_inc(unit_used, 1)
                    if u == 0:
                        self.norm.sum_features(pe)
                    if u == 1:
                        self.norm.spread_row(pe)
                self.softmax.tensor(pe)
                self.tail.tensor(pe)

        def shift_of(layer, part):
            return lambda k: mod[:, 48 * layer + 8 * part + k:48 * layer + 8 * part + k + 1]

        def scale_of(layer, part):
            return lambda k: mod1[:, 48 * layer + 8 * part + k:48 * layer + 8 * part + k + 1]

        def gain_of(name):
            return lambda k: col(name, k)

        def constant(name):
            return lambda k: col(name)

        DOWN, OUT = 0, 4
        conditioning = Conditioning()
        stages = [conditioning]

        def add(stage):
            stages.append(stage)
            return stage

        norm = add(Norm(scale_of(0, 1), shift_of(0, 0), OUT))
        conditioning.norm = norm
        even = add(Even(norm))
        last = add(Project("even_out", shift_of(0, 2), even.wait_chunk))
        norm = add(Norm(scale_of(0, 4), shift_of(0, 3), OUT, last))
        last = add(FeedForward("ffn0", shift_of(0, 5), norm))
        norm = add(Norm(scale_of(1, 1), shift_of(1, 0), DOWN, last))
        odd = add(Mlstm(norm))
        last = add(Project("odd_out", shift_of(1, 2), odd.wait_chunk))
        norm = add(Norm(scale_of(1, 4), shift_of(1, 3), OUT, last))
        last = add(FeedForward("ffn1", shift_of(1, 5), norm))
        norm = add(Norm(gain_of("ffn1_norm"), constant("zero"), DOWN, last))
        last = add(FeedForward("ffn2", constant("half"), norm))
        mix_tables_free = KC * updates[0]
        norm = add(Norm(gain_of("mix_norm"), constant("zero"), DOWN, last))
        mix = add(Mix(norm))
        memory = Memory()
        last = add(Project("mix_out", constant("one"), mix.wait_chunk, during=memory))
        memory.norm = Norm(gain_of("mem_q_norm"), constant("zero"), OUT, last, late=False)
        add(memory)
        last = add(Project("mem_out", constant("one"), memory.wait_chunk))
        norm = add(Norm(gain_of("ffn2_norm"), constant("zero"), OUT, last))
        last = add(FeedForward("ffn3", constant("half"), norm))
        final = add(Norm(gain_of("final_norm"), constant("zero"), DOWN, last, final=True))
        n_units = N_UNITS

        block = ctx.enter_context(nc.Block())

        @block.sync
        def _(sp):
            for dst, src in ((par, params), (tab, tables)):
                sp.dma_start(dst[:, :], src[:, :]).then_inc(setup_loaded, 16)

            def load(place, i=None):
                at = slice(place, place + 1) if i is None else bass.ds(2 * i + place, 1)
                r = place % 2
                sp.dma_start(raw[:, r, :], stream[at, :, :].rearrange("o p n -> p (o n)")).then_inc(landed[r], 16)

            e = FIRST_UNIT["even_out"]
            for n in range(2):
                load(place_of_ada(n))
            sp.dma_start(x[:, :, :], xT[:, :, :]).then_inc(x_loaded, 16)
            for n in range(2, ADA_FIRST):
                sp.wait_ge(ada_used, n - 1)
                load(place_of_ada(n))
            for m in range(e):
                if m < 2:
                    sp.wait_ge(ada_used, ADA_FIRST - 1 + m)
                else:
                    sp.wait_ge(lo_split, m - 1)
                load(place_of(m))
            for n in range(ADA_FIRST, ADA_FIRST + 2):
                sp.wait_ge(lo_split, e - 1 + n - ADA_FIRST)
                load(place_of_ada(n))
            with sp.Fori(0, ADA_REST // 2 - 1) as i:
                for n in range(ADA_FIRST + 2, ADA_FIRST + 4):
                    sp.wait_ge(ada_used, 2 * i + n - 1)
                    load(place_of_ada(n), i)
            for m in range(e, e + 2):
                sp.wait_ge(ada_used, ADA_UNITS - 1 + m - e)
                load(place_of(m))
            with sp.Fori(0, (n_units - e - 2) // 2) as i:
                for m in range(e + 2, e + 4):
                    sp.wait_ge(lo_split, 2 * i + m - 1)
                    load(place_of(m), i)
            if (n_units - e) % 2:
                sp.wait_ge(lo_split, n_units - 2)
                load(place_of(n_units - 1))
            for k in range(KC):
                sp.wait_ge(scaled, KC * final.n + k + 1)
                sp.dma_start(outT[:, k, :], final.t[:, k, :]).then_inc(stored, 16)
            sp.wait_ge(stored, 16 * KC)

        @block.gpsimd
        def _(pool):
            pool.dma_start(area(16384, 4 * S), even_tables[:, 0:4 * S]).then_inc(even_loaded, 16)
            pool.dma_start(area(18432, 2 * S), even_tables[:, 4 * S:6 * S]).then_inc(even_loaded, 16)
            pool.dma_start(area(19456, 4 * P), w_pool[:, :]).then_inc(even_loaded, 16)
            pool.wait_ge(x_ready, mix_tables_free)
            pool.dma_start(area(24064, MIX_TABLES), mix_tables[:, :]).then_inc(mix_loaded, 16)
            pool.wait_ge(mix.hg.s_summed, mix.hg.H)
            pool.dma_start(area(8192, KC * N_MEM), memT[:, :]).then_inc(mem_loaded, 16)

        @block.scalar
        def _(act):
            st = Steps(act, sem("act_steps"))
            for stage in stages:
                stage.scalar(act, st)

        @block.vector
        def _(dve):
            st = Steps(dve, sem("dve_steps"))
            for stage in stages:
                stage.vector(dve, st)

        @block.tensor
        def _(pe):
            for stage in stages:
                stage.tensor(pe)


def columns(v):
    return np.asarray(v).reshape(-1, P).T


def in_units(w, cols=256):
    k, n = w.shape
    return w.reshape(k // P, P, n // cols, cols).transpose(2, 1, 0, 3).reshape(n // cols, P, -1)


def by_rows(w):
    return w.reshape(-1, 2, P, D).transpose(0, 2, 1, 3).reshape(-1, P, UNIT)


def ffn_units(w1, w3, w2):
    a, b = in_units(w1, P).reshape(FB, P, KC, P), in_units(w3, P).reshape(FB, P, KC, P)
    return [np.concatenate([a, b], axis=3).reshape(FB, P, UNIT), by_rows(w2)]


def build_stream(i):
    ada = i["ada_w"].reshape(2, KC, P, 3, UNIT).transpose(0, 3, 1, 2, 4).reshape(ADA_UNITS, P, UNIT)
    w = i["ev_w_in"][0]
    heads = w[:, 512:1024].reshape(D, 2, 4, 64).transpose(0, 2, 1, 3).reshape(D, 512)
    even = np.concatenate([w[:, 0:512], heads, w[:, 1024:]], axis=1)
    wo = i["ev_w_out"][0]
    even_out = np.concatenate([wo[0:512], wo[512:].reshape(2, 4, 64, D).transpose(1, 0, 2, 3).reshape(512, D)], axis=0)
    w = i["od_w_in"][0]
    gates = np.concatenate([w[:, 3072:], np.zeros((D, 224), w.dtype)], axis=1)
    odd = np.concatenate([gates, w[:, 0:3072]], axis=1)
    w = i["w_in_2"][0]
    q, f, rest = w[:, 0:512], w[:, 512:1024], w[:, 1024:]
    mix = np.concatenate([f, q, rest], axis=1)
    parts = [ada[:ADA_FIRST], in_units(even), ada[ADA_FIRST:], in_units(even_out)]
    parts += ffn_units(i["ffn_w1"][0], i["ffn_w3"][0], i["ffn_w2"][0])
    parts += [in_units(odd), in_units(i["od_w_out"][0])]
    parts += ffn_units(i["ffn_w1"][1], i["ffn_w3"][1], i["ffn_w2"][1])
    gu = i["ffn1_w_gu_2"][0]
    parts += ffn_units(gu[:, :FF], gu[:, FF:], i["ffn1_w_down_2"][0])
    parts += [in_units(mix), in_units(i["w_out_2"][0]), in_units(i["mem_w_kv_2"][0]), in_units(i["mem_w_q_2"][0]),
              in_units(i["mem_w_o_2"][0])]
    gu = i["ffn2_w_gu_2"][0]
    parts += ffn_units(gu[:, :FF], gu[:, FF:], i["ffn2_w_down_2"][0])
    return np.ascontiguousarray(np.concatenate(parts, axis=0))


def build_params(i):
    f = np.float32
    gb = np.zeros((P, 2), f)
    g = i["od_gate_b"][0].reshape(2, 2, 8)
    for d in range(2):
        for kind in range(2):
            gb[32 * d:32 * d + 8, kind] = g[d, kind]
    twice = lambda v: np.concatenate([v, v]).reshape(P, 1)
    cols = [columns(i["c"]), columns(i["ada_b"]), columns(i["ev_b_pool"]), columns(i["ev_pool_scale"]),
            twice(i["ev_q_gain"][0]), twice(i["ev_k_gain"][0]), columns(i["od_conv_w"]), columns(i["od_conv_b"]),
            columns(i["od_head_gain"]), columns(i["ffn1_norm_2"]), columns(i["mix_norm_2"]),
            columns(i["mem_q_norm_2"]), columns(i["mem_kv_norm_2"]), columns(i["ffn2_norm_2"]),
            columns(i["final_norm_2"]), columns(i["hg_lb_raw_2"]), columns(i["hg_gnorm_2"]), columns(i["sb_gnorm_2"]),
            gb, np.full((P, 1), EPS, f), np.zeros((P, 1), f), np.ones((P, 1), f), np.full((P, 1), 0.5, f)]
    out = np.ascontiguousarray(np.concatenate(cols, axis=1))
    assert out.shape == (P, N_PARAMS)
    return out


def build_tables():
    f = np.float32
    a = np.arange(P)
    part, free = a[:, None], a[None, :]
    pair = np.zeros((P, 32), f)
    pair[:64, 15], pair[64:, 16] = 1, 1
    gi, gf = np.zeros((P, 40), f), np.zeros((P, 40), f)
    for d in range(2):
        for h in range(8):
            gi[16 * d + h, 32 * d + h] = 1
            gf[16 * d + 8 + h, 32 * d + h] = 1
    spread = np.concatenate([part == 2 * b + free // 64 for b in range(5)], axis=1)
    t = [np.eye(P), free == (part ^ 1), part >= free, part < free, np.where(part < free, 0, -BIG),
         np.where(free < part, BIG, 0), np.where(free > part, BIG, 0), np.ones((P, P)), pair, gi, gf, spread]
    tables = np.ascontiguousarray(np.concatenate([np.asarray(v, f) for v in t], axis=1))
    t = np.arange(S)
    counts = [1.0 / (np.clip(t + w - w // 2, 0, S) - np.clip(t - w // 2, 0, S)) for w in (2, 4, 8, 16)]
    inv_freq = (np.float32(10000.0) ** (-np.arange(16, dtype=f) / f(16))).astype(f)
    ang = np.concatenate([(t // 64).astype(f)[:, None] * inv_freq, (t % 64).astype(f)[:, None] * inv_freq], axis=1)
    ang = ang[:, (a % 64) // 2].T.astype(np.float64)
    sign = np.where(a % 2 == 0, -1.0, 1.0)[:, None]
    even = np.concatenate([np.tile(np.concatenate(counts)[None, :], (P, 1)), np.cos(ang), sign * np.sin(ang)], axis=1)
    masks = []
    for l in range(LEVELS):
        n = 1 << l
        masks.append((part // (2 * n) == free // (2 * n)) & (part % (2 * n) < n) & (free % (2 * n) >= n))
    masks.append(part == free)
    run = np.tile((np.arange(S) % P != 0)[None, :], (P, 1))
    mix = np.concatenate([np.asarray(m, f) for m in masks] + [run.astype(f)], axis=1)
    return tables, np.ascontiguousarray(even.astype(f)), np.ascontiguousarray(mix)


def kernel(**inputs):
    import concourse.bacc as _bacc
    from concourse.bass_utils import run_bass_kernel_spmd as _run

    i = {n: np.asarray(v) for n, v in inputs.items()}
    tables, even_tables, mix_tables = build_tables()
    arrays = {
        "xT": np.ascontiguousarray(i["x"][0].T.reshape(KC, P, S).transpose(1, 0, 2)),
        "memT": np.ascontiguousarray(i["mem_2"][0].T.reshape(KC, P, N_MEM).transpose(1, 0, 2).reshape(P, -1)),
        "stream": build_stream(i),
        "params": build_params(i),
        "tables": tables,
        "even_tables": even_tables,
        "mix_tables": mix_tables,
        "w_pool": np.ascontiguousarray(i["ev_w_pool"][0].transpose(1, 0, 2).reshape(P, -1)),
    }
    nc = _bacc.Bacc("TRN2", target_bir_lowering=False, num_devices=1)
    args = [nc.dram_tensor(n, a.shape, F32, kind="ExternalInput").ap() for n, a in arrays.items()]
    args.append(nc.dram_tensor("outT", (P, KC, S), F32, kind="ExternalOutput").ap())
    program(nc, *args)
    r = _run(nc, [arrays], core_ids=[0])
    out = r.results[0]["outT"]
    return np.ascontiguousarray(out.transpose(1, 0, 2).reshape(D, S).T)[None]
```
